# Optimizing a Trainium2 kernel written in Bass

```python
import jax, jax.numpy as jnp
from jax import lax
import numpy as np

D_MODEL = 1024
BATCH = 1
SEQ = 512
DEPTH = 1

HEAD_DIM = 64
N_ATTN_HEADS = 8
N_KV_GROUPS = 2
HEADS_PER_GROUP = N_ATTN_HEADS // N_KV_GROUPS
ATTN_WIDTH = N_ATTN_HEADS * HEAD_DIM
CONV_WIDTH = D_MODEL - ATTN_WIDTH
KV_WIDTH = N_KV_GROUPS * HEAD_DIM
N_BRANCH = 3
CMP_BLOCK = 32
CMP_STRIDE = 16
CMP_HIDDEN = 4 * HEAD_DIM
SEL_BLOCK = 64
SEL_TOPK = 16
WINDOW = 512
Q_BLOCK = 128
CONV_K = 3
D_FF = 4 * D_MODEL
IN_WIDTH = ATTN_WIDTH + 6 * KV_WIDTH + N_BRANCH * N_ATTN_HEADS + 3 * CONV_WIDTH
EPS = 1e-6
NEG = -1e30
FORCE_BONUS = 1e4


def rms_norm(x, g):
    xf = x.astype(jnp.float32)
    y = xf * lax.rsqrt(jnp.mean(xf * xf, axis=-1, keepdims=True) + EPS)
    return (y * g.astype(jnp.float32)).astype(x.dtype)

def alibi_slopes():
    h = np.arange(1, N_ATTN_HEADS + 1, dtype=np.float32)
    s = np.power(np.float32(2.0), -8.0 * h / N_ATTN_HEADS).astype(np.float32)
    return jnp.asarray(s, dtype=jnp.float32).reshape(N_KV_GROUPS, HEADS_PER_GROUP)

def masked_softmax(s, mask):
    s = jnp.where(mask, s, NEG)
    m = jnp.max(s, axis=-1, keepdims=True)
    p = jnp.where(mask, jnp.exp(s - m), 0.0)
    return p / jnp.maximum(jnp.sum(p, axis=-1, keepdims=True), 1e-30)

def cmp_to_sel_matrix(n_cmp, n_sel):
    s0 = jnp.arange(n_cmp)[:, None] * CMP_STRIDE
    s1 = jnp.arange(n_sel)[None, :] * SEL_BLOCK
    shared = jnp.clip(jnp.minimum(s0 + CMP_BLOCK, s1 + SEL_BLOCK) - jnp.maximum(s0, s1), 0, None)
    return shared.astype(jnp.float32) / CMP_BLOCK

def compress(k_raw, pe, w1, b1, w2, b2):
    B, T = k_raw.shape[0], k_raw.shape[1]
    ch = k_raw.reshape(B, T // CMP_STRIDE, CMP_STRIDE, N_KV_GROUPS, HEAD_DIM)
    blk = jnp.concatenate([ch[:, :-1], ch[:, 1:]], axis=2)
    blk = blk + pe[None, None, :, None, :]
    blk = blk.transpose(0, 3, 1, 2, 4).reshape(B, N_KV_GROUPS, -1, CMP_BLOCK * HEAD_DIM)
    hdn = jax.nn.gelu(blk @ w1 + b1)
    return hdn @ w2 + b2

def nsa_attention(q, k_cmp, v_cmp, k_slc, v_slc, k_win, v_win, gates):
    B, T = q.shape[0], q.shape[1]
    G, R, hd = N_KV_GROUPS, HEADS_PER_GROUP, HEAD_DIM
    f32 = jnp.float32
    n_cmp = k_cmp.shape[2]
    n_sel = T // SEL_BLOCK
    n_top = min(SEL_TOPK, n_sel)
    n_qb = T // Q_BLOCK
    slopes = alibi_slopes()[None, :, :, None, None]
    sel_map = cmp_to_sel_matrix(n_cmp, n_sel)
    cmp_end = jnp.arange(n_cmp, dtype=jnp.int32) * CMP_STRIDE + (CMP_BLOCK - 1)
    sel_id = jnp.arange(n_sel, dtype=jnp.int32)
    sel_off = jnp.arange(SEL_BLOCK, dtype=jnp.int32)
    win_off = jnp.arange(Q_BLOCK + WINDOW, dtype=jnp.int32) - WINDOW
    ks_blk = k_slc.reshape(B, n_sel, SEL_BLOCK, G, hd).transpose(0, 3, 1, 2, 4)
    vs_blk = v_slc.reshape(B, n_sel, SEL_BLOCK, G, hd).transpose(0, 3, 1, 2, 4)
    kw_pad = jnp.pad(k_win, ((0, 0), (WINDOW, 0), (0, 0), (0, 0)))
    vw_pad = jnp.pad(v_win, ((0, 0), (WINDOW, 0), (0, 0), (0, 0)))
    q_blocks = (q * (hd ** -0.5)).reshape(B, n_qb, Q_BLOCK, G, R, hd).transpose(1, 0, 3, 4, 2, 5)
    g_blocks = gates.reshape(B, n_qb, Q_BLOCK, G, R, N_BRANCH).transpose(1, 0, 3, 4, 2, 5)
    b_ix = jnp.arange(B)[:, None, None, None]
    g_ix = jnp.arange(G)[None, :, None, None]

    def one_block(args):
        c, qb, gb = args
        q0 = c * Q_BLOCK
        t = q0 + jnp.arange(Q_BLOCK, dtype=jnp.int32)
        s = jnp.einsum('bgrqd,bgid->bgrqi', qb, k_cmp).astype(f32)
        dist = (t[:, None] - cmp_end[None, :]).astype(f32)
        p_cmp = masked_softmax(s - slopes * dist, dist >= 0)
        o_cmp = jnp.einsum('bgrqi,bgid->bgrqd', p_cmp.astype(v_cmp.dtype), v_cmp)
        imp = jnp.einsum('bgrqi,ij->bgqj', p_cmp, sel_map)
        jt = (t // SEL_BLOCK)[:, None]
        forced = (sel_id == 0) | (sel_id == jt) | (sel_id == jt - 1)
        valid = sel_id * SEL_BLOCK <= t[:, None]
        imp = jnp.where(valid, jnp.where(forced, imp + FORCE_BONUS, imp), NEG)
        _, idx = lax.top_k(imp, n_top)
        kg = ks_blk[b_ix, g_ix, idx].reshape(B, G, Q_BLOCK, n_top * SEL_BLOCK, hd)
        vg = vs_blk[b_ix, g_ix, idx].reshape(B, G, Q_BLOCK, n_top * SEL_BLOCK, hd)
        pos = (idx[..., None] * SEL_BLOCK + sel_off).reshape(B, G, Q_BLOCK, n_top * SEL_BLOCK)
        dist = (t[None, None, :, None] - pos).astype(f32)[:, :, None]
        s = jnp.einsum('bgrqd,bgqmd->bgrqm', qb, kg).astype(f32)
        p_slc = masked_softmax(s - slopes * dist, dist >= 0)
        o_slc = jnp.einsum('bgrqm,bgqmd->bgrqd', p_slc.astype(vg.dtype), vg)
        kw = lax.dynamic_slice_in_dim(kw_pad, q0, Q_BLOCK + WINDOW, axis=1)
        vw = lax.dynamic_slice_in_dim(vw_pad, q0, Q_BLOCK + WINDOW, axis=1)
        spos = q0 + win_off
        dist_i = t[:, None] - spos[None, :]
        mask = (spos[None, :] >= 0) & (dist_i >= 0) & (dist_i < WINDOW)
        s = jnp.einsum('bgrqd,bsgd->bgrqs', qb, kw).astype(f32)
        p_win = masked_softmax(s - slopes * dist_i.astype(f32), mask)
        o_win = jnp.einsum('bgrqs,bsgd->bgrqd', p_win.astype(vw.dtype), vw)
        o = gb[..., 0:1] * o_cmp + gb[..., 1:2] * o_slc + gb[..., 2:3] * o_win
        return o.astype(q.dtype)

    out = lax.map(one_block, (jnp.arange(n_qb, dtype=jnp.int32), q_blocks, g_blocks))
    return out.transpose(1, 0, 4, 2, 3, 5).reshape(B, T, N_ATTN_HEADS * hd)

def short_conv_mixer(h, c_gate, b_gate, conv_w):
    u = c_gate * h
    v = lax.conv_general_dilated(u, conv_w[:, None, :], window_strides=(1,),
                                 padding=((CONV_K - 1, 0),),
                                 dimension_numbers=('NWC', 'WIO', 'NWC'),
                                 feature_group_count=CONV_WIDTH)
    return b_gate * v

def first_inputs(seed: int = 0) -> dict:
    key = jax.random.key(seed)
    ks = jax.random.split(key, 16)
    f32 = jnp.float32

    def nrm(k, shape, scale):
        return jax.random.normal(k, shape, f32) * scale

    return {
        'x': nrm(ks[0], (BATCH, SEQ, D_MODEL), 1.0),
        'g_mix_norm': 1.0 + nrm(ks[1], (DEPTH, D_MODEL), 0.02),
        'w_in': nrm(ks[2], (DEPTH, D_MODEL, IN_WIDTH), D_MODEL ** -0.5),
        'g_q': 1.0 + nrm(ks[3], (DEPTH, HEAD_DIM), 0.02),
        'g_k': 1.0 + nrm(ks[4], (DEPTH, N_BRANCH, HEAD_DIM), 0.02),
        'pe_cmp': nrm(ks[5], (DEPTH, 2, CMP_BLOCK, HEAD_DIM), 0.1),
        'w_cmp1': nrm(ks[6], (DEPTH, 2, CMP_BLOCK * HEAD_DIM, CMP_HIDDEN), (CMP_BLOCK * HEAD_DIM) ** -0.5),
        'b_cmp1': nrm(ks[7], (DEPTH, 2, CMP_HIDDEN), 0.01),
        'w_cmp2': nrm(ks[8], (DEPTH, 2, CMP_HIDDEN, HEAD_DIM), CMP_HIDDEN ** -0.5),
        'b_cmp2': nrm(ks[9], (DEPTH, 2, HEAD_DIM), 0.01),
        'conv_w': nrm(ks[10], (DEPTH, CONV_K, CONV_WIDTH), CONV_K ** -0.5),
        'g_out': 1.0 + nrm(ks[11], (DEPTH, D_MODEL), 0.02),
        'w_o': nrm(ks[12], (DEPTH, D_MODEL, D_MODEL), (2 * DEPTH * D_MODEL) ** -0.5),
        'g_ffn_norm': 1.0 + nrm(ks[13], (DEPTH, D_MODEL), 0.02),
        'w_up': nrm(ks[14], (DEPTH, D_MODEL, D_FF), D_MODEL ** -0.5),
        'w_down': nrm(ks[15], (DEPTH, D_FF, D_MODEL), (2 * DEPTH * D_FF) ** -0.5),
    }

def first_block(x, g_mix_norm, w_in, g_q, g_k, pe_cmp, w_cmp1, b_cmp1, w_cmp2, b_cmp2,
              conv_w, g_out, w_o, g_ffn_norm, w_up, w_down):
    B, T = x.shape[0], x.shape[1]
    sizes = [ATTN_WIDTH] + [KV_WIDTH] * 6 + [N_BRANCH * N_ATTN_HEADS] + [CONV_WIDTH] * 3
    offs = [int(o) for o in np.cumsum(sizes)[:-1]]
    kv_shape = (B, T, N_KV_GROUPS, HEAD_DIM)
    for l in range(DEPTH):
        h = rms_norm(x, g_mix_norm[l])
        z = h @ w_in[l]
        q, kc, vc, ks_, vs_, kw_, vw_, gl, hc, cg, bg = jnp.split(z, offs, axis=-1)
        q = rms_norm(q.reshape(B, T, N_ATTN_HEADS, HEAD_DIM), g_q[l])
        k_cmp = rms_norm(compress(kc.reshape(kv_shape), pe_cmp[l, 0], w_cmp1[l, 0], b_cmp1[l, 0],
                                  w_cmp2[l, 0], b_cmp2[l, 0]), g_k[l, 0])
        v_cmp = compress(vc.reshape(kv_shape), pe_cmp[l, 1], w_cmp1[l, 1], b_cmp1[l, 1],
                         w_cmp2[l, 1], b_cmp2[l, 1])
        k_slc = rms_norm(ks_.reshape(kv_shape), g_k[l, 1])
        k_win = rms_norm(kw_.reshape(kv_shape), g_k[l, 2])
        gates = jax.nn.sigmoid(gl).reshape(B, T, N_ATTN_HEADS, N_BRANCH)
        attn_out = nsa_attention(q, k_cmp, v_cmp, k_slc, vs_.reshape(kv_shape),
                                 k_win, vw_.reshape(kv_shape), gates)
        conv_out = short_conv_mixer(hc, cg, bg, conv_w[l])
        mixed = jnp.concatenate([rms_norm(attn_out, g_out[l, :ATTN_WIDTH]),
                                 rms_norm(conv_out, g_out[l, ATTN_WIDTH:])], axis=-1)
        x = x + mixed @ w_o[l]
        h = rms_norm(x, g_ffn_norm[l])
        x = x + jnp.square(jax.nn.relu(h @ w_up[l])) @ w_down[l]
    return x


CHUNK = 64
N_MOD = 6

M_HEADS = 4
M_QK_DIM = 128
M_V_DIM = 256
M_QK_WIDTH = M_HEADS * M_QK_DIM
M_V_WIDTH = M_HEADS * M_V_DIM
CONV_WIDTH_2 = 4

A_HEADS = 8
Q_LORA = 384
KV_LORA = 256
QK_NOPE = 128
QK_ROPE = 64
V_HEAD = 128
A_V_WIDTH = A_HEADS * V_HEAD
ROPE_THETA = 10000.0

N_BRANCHES = 2
IN_SIZES = (M_QK_WIDTH, M_QK_WIDTH, M_V_WIDTH, M_V_WIDTH, M_HEADS, M_HEADS,
            Q_LORA, KV_LORA, QK_ROPE, N_BRANCHES * D_MODEL)
D_IN = sum(IN_SIZES)
IN_SPLIT_POINTS = tuple(sum(IN_SIZES[:i + 1]) for i in range(len(IN_SIZES) - 1))

N_GROUPS = 4
EXPERTS_PER_GROUP = 8
N_EXPERTS = N_GROUPS * EXPERTS_PER_GROUP
TOP_K = 2
D_EXPERT = 256
MOE_BLOCK = 128


def rms_norm_2(x, g):
    xf = x.astype(jnp.float32)
    y = xf * lax.rsqrt(jnp.mean(xf * xf, axis=-1, keepdims=True) + EPS)
    return (y * g.astype(jnp.float32)).astype(x.dtype)

def modulate(h, shift, scale):
    return h * (1.0 + scale[:, None, :]) + shift[:, None, :]

def apply_rope(x, cos, sin):
    x1, x2 = jnp.split(x, 2, axis=-1)
    return jnp.concatenate([x1 * cos - x2 * sin, x1 * sin + x2 * cos], axis=-1)

def causal_depthwise_conv(x, w, b):
    C = x.shape[-1]
    y = lax.conv_general_dilated(x, w[:, None, :], window_strides=(1,),
                                 padding=((CONV_WIDTH_2 - 1, 0),),
                                 dimension_numbers=('NWC', 'WIO', 'NWC'),
                                 feature_group_count=C)
    return y + b

def mlstm_chunkwise(q, k, v, log_i, log_f):
    B, S, NH, DQK = q.shape
    DV = v.shape[-1]
    nc = S // CHUNK

    def to_chunks(t):
        t = t.reshape(B, nc, CHUNK, NH, *t.shape[3:])
        return jnp.moveaxis(t, (1, 3), (0, 2))

    causal = jnp.tril(jnp.ones((CHUNK, CHUNK), dtype=bool))

    def step(carry, xs):
        C, n, m = carry
        qc, kc, vc, lic, lfc = xs
        b = jnp.cumsum(lfc, axis=-1)
        dmat = b[..., :, None] - b[..., None, :] + lic[..., None, :]
        dmat = jnp.where(causal, dmat, -jnp.inf)
        m_inter = b + m[..., None]
        m_t = jnp.maximum(jnp.max(dmat, axis=-1), m_inter)
        s = jnp.einsum('bhtd,bhsd->bhts', qc, kc) * jnp.exp(dmat - m_t[..., None])
        w_inter = jnp.exp(m_inter - m_t)
        num = (jnp.einsum('bhts,bhsv->bhtv', s, vc)
               + w_inter[..., None] * jnp.einsum('bhtd,bhvd->bhtv', qc, C))
        den = jnp.sum(s, axis=-1) + w_inter * jnp.einsum('bhtd,bhd->bht', qc, n)
        h = num / jnp.maximum(jnp.abs(den), jnp.exp(-m_t))[..., None]
        b_last = b[..., -1]
        a = b_last[..., None] - b + lic
        m_new = jnp.maximum(b_last + m, jnp.max(a, axis=-1))
        decay = jnp.exp(b_last + m - m_new)
        wk = jnp.exp(a - m_new[..., None])
        C_new = decay[..., None, None] * C + jnp.einsum('bhs,bhsv,bhsd->bhvd', wk, vc, kc)
        n_new = decay[..., None] * n + jnp.einsum('bhs,bhsd->bhd', wk, kc)
        return (C_new, n_new, m_new), h

    init = (jnp.zeros((B, NH, DV, DQK), jnp.float32),
            jnp.zeros((B, NH, DQK), jnp.float32),
            jnp.zeros((B, NH), jnp.float32))
    _, h = lax.scan(step, init, (to_chunks(q), to_chunks(k), to_chunks(v),
                                 to_chunks(log_i), to_chunks(log_f)))
    return jnp.moveaxis(h, (0, 2), (1, 3)).reshape(B, S, NH, DV)

def chunk_causal_mla_attention(q_nope, q_rope, k_nope, k_rope, v):
    B, S, H, _ = q_nope.shape
    nqb = S // Q_BLOCK
    key_chunk = jnp.arange(S) // CHUNK
    scale = (QK_NOPE + QK_ROPE) ** -0.5

    def to_blocks(t):
        return t.reshape(B, nqb, Q_BLOCK, *t.shape[2:]).swapaxes(0, 1)

    def one_block(args):
        qn, qr, blk = args
        s = (jnp.einsum('bqhd,bkhd->bhqk', qn, k_nope)
             + jnp.einsum('bqhr,bkr->bhqk', qr, k_rope)).astype(jnp.float32) * scale
        q_chunk = (blk * Q_BLOCK + jnp.arange(Q_BLOCK)) // CHUNK
        mask = key_chunk[None, :] <= q_chunk[:, None]
        s = jnp.where(mask, s, -jnp.inf)
        p = jax.nn.softmax(s, axis=-1).astype(v.dtype)
        return jnp.einsum('bhqk,bkhd->bqhd', p, v)

    out = lax.map(one_block, (to_blocks(q_nope), to_blocks(q_rope), jnp.arange(nqb)))
    return out.swapaxes(0, 1).reshape(B, S, H * V_HEAD)

def mixer_sublayer(h, cos, sin, w_in, conv_w, conv_b, igate_b, fgate_b, q_norm_g,
                   kv_norm_g, w_uq, w_ukv, w_branch_m, w_branch_a, w_out):
    B, S, _ = h.shape
    proj = h @ w_in
    (q_m, k_m, v_m, o_m, i_m, f_m, c_q, c_kv, k_r, gate_pre) = jnp.split(
        proj, IN_SPLIT_POINTS, axis=-1)

    qk = jax.nn.silu(causal_depthwise_conv(jnp.concatenate([q_m, k_m], axis=-1), conv_w, conv_b))
    q_m, k_m = jnp.split(qk.astype(jnp.float32), 2, axis=-1)
    q_m = q_m.reshape(B, S, M_HEADS, M_QK_DIM) * (M_QK_DIM ** -0.5)
    k_m = k_m.reshape(B, S, M_HEADS, M_QK_DIM)
    v_m = v_m.astype(jnp.float32).reshape(B, S, M_HEADS, M_V_DIM)
    log_i = (i_m + igate_b).astype(jnp.float32)
    log_f = jax.nn.log_sigmoid((f_m + fgate_b).astype(jnp.float32))
    y_m = mlstm_chunkwise(q_m, k_m, v_m, log_i, log_f).reshape(B, S, M_V_WIDTH).astype(h.dtype)
    y_m = jax.nn.sigmoid(o_m) * y_m

    q_a = (rms_norm_2(c_q, q_norm_g) @ w_uq).reshape(B, S, A_HEADS, QK_NOPE + QK_ROPE)
    q_nope = q_a[..., :QK_NOPE]
    q_rope = apply_rope(q_a[..., QK_NOPE:], cos[:, None, :], sin[:, None, :])
    kv = (rms_norm_2(c_kv, kv_norm_g) @ w_ukv).reshape(B, S, A_HEADS, QK_NOPE + V_HEAD)
    k_nope, v_a = kv[..., :QK_NOPE], kv[..., QK_NOPE:]
    k_rope = apply_rope(k_r, cos, sin)
    y_a = chunk_causal_mla_attention(q_nope, q_rope, k_nope, k_rope, v_a)

    g_m, g_a = jnp.split(jax.nn.sigmoid(gate_pre), 2, axis=-1)
    merged = g_m * (y_m @ w_branch_m) + g_a * (y_a @ w_branch_a)
    return merged @ w_out

def hierarchical_moe(h, w_group, b_group, w_router, b_router, w_gate, w_up, w_down):
    B, S, D = h.shape
    T = B * S
    ht = h.reshape(T, D)
    hf = ht.astype(jnp.float32)
    grp_probs = jax.nn.softmax(hf @ w_group.astype(jnp.float32) + b_group.astype(jnp.float32), axis=-1)
    grp = jnp.argmax(grp_probs, axis=-1)
    p_grp = jnp.take_along_axis(grp_probs, grp[:, None], axis=-1)[:, 0]
    e_logits = (hf @ w_router.astype(jnp.float32) + b_router.astype(jnp.float32)).reshape(
        T, N_GROUPS, EXPERTS_PER_GROUP)
    in_grp = jnp.take_along_axis(e_logits, grp[:, None, None], axis=1)[:, 0]
    top_p, top_e = lax.top_k(jax.nn.softmax(in_grp, axis=-1), TOP_K)
    weights = p_grp[:, None] * top_p / jnp.sum(top_p, axis=-1, keepdims=True)
    expert_id = grp[:, None] * EXPERTS_PER_GROUP + top_e

    n_assign = T * TOP_K
    flat_e = expert_id.reshape(-1).astype(jnp.int32)
    flat_t = jnp.repeat(jnp.arange(T, dtype=jnp.int32), TOP_K)
    flat_w = weights.reshape(-1)
    order = jnp.argsort(flat_e)
    se, st, sw = flat_e[order], flat_t[order], flat_w[order]
    counts = jnp.bincount(flat_e, length=N_EXPERTS)
    padded = (counts + MOE_BLOCK - 1) // MOE_BLOCK * MOE_BLOCK
    starts = jnp.cumsum(counts) - counts
    p_ends = jnp.cumsum(padded)
    p_starts = p_ends - padded
    dest = p_starts[se] + jnp.arange(n_assign, dtype=jnp.int32) - starts[se]
    cap = n_assign + N_EXPERTS * MOE_BLOCK
    n_blocks = cap // MOE_BLOCK
    slot_tok = jnp.zeros((cap,), jnp.int32).at[dest].set(st)
    slot_w = jnp.zeros((cap,), jnp.float32).at[dest].set(sw)
    blk_start = jnp.arange(n_blocks) * MOE_BLOCK
    blk_expert = jnp.minimum(jnp.sum(p_ends[None, :] <= blk_start[:, None], axis=1), N_EXPERTS - 1)
    xg = ht[slot_tok].reshape(n_blocks, MOE_BLOCK, D)

    def run_block(args):
        xb, e, wb = args
        a = jax.nn.silu(xb @ w_gate[e]) * (xb @ w_up[e])
        return (a @ w_down[e]) * wb[:, None].astype(xb.dtype)

    out = lax.map(run_block, (xg, blk_expert, slot_w.reshape(n_blocks, MOE_BLOCK)))
    y = jnp.zeros((T, D), h.dtype).at[slot_tok].add(out.reshape(cap, D))
    return y.reshape(B, S, D)

def second_inputs(seed: int = 0) -> dict:
    key = jax.random.key(seed)
    ks = jax.random.split(key, 26)
    f32 = jnp.float32

    def nrm(k, shape, scale):
        return jax.random.normal(k, shape, f32) * scale

    def gain(k, shape):
        return 1.0 + 0.02 * jax.random.normal(k, shape, f32)

    L, D = DEPTH, D_MODEL
    return {
        "x": nrm(ks[0], (BATCH, SEQ, D), 1.0),
        "c": nrm(ks[1], (BATCH, D), 1.0),
        "mod_w": nrm(ks[2], (L, D, N_MOD * D), 0.5 * D ** -0.5),
        "mod_b": nrm(ks[3], (L, N_MOD * D), 0.02),
        "norm1_g": gain(ks[4], (L, D)),
        "w_in": nrm(ks[5], (L, D, D_IN), D ** -0.5),
        "conv_w": nrm(ks[6], (L, CONV_WIDTH_2, 2 * M_QK_WIDTH), CONV_WIDTH_2 ** -0.5),
        "conv_b": nrm(ks[7], (L, 2 * M_QK_WIDTH), 0.02),
        "igate_b": nrm(ks[8], (L, M_HEADS), 0.1),
        "fgate_b": 3.0 + nrm(ks[9], (L, M_HEADS), 0.5),
        "q_norm_g": gain(ks[10], (L, Q_LORA)),
        "kv_norm_g": gain(ks[11], (L, KV_LORA)),
        "w_uq": nrm(ks[12], (L, Q_LORA, A_HEADS * (QK_NOPE + QK_ROPE)), Q_LORA ** -0.5),
        "w_ukv": nrm(ks[13], (L, KV_LORA, A_HEADS * (QK_NOPE + V_HEAD)), KV_LORA ** -0.5),
        "w_branch_m": nrm(ks[14], (L, M_V_WIDTH, D), M_V_WIDTH ** -0.5),
        "w_branch_a": nrm(ks[15], (L, A_V_WIDTH, D), A_V_WIDTH ** -0.5),
        "w_out": nrm(ks[16], (L, D, D), D ** -0.5),
        "norm2_g": gain(ks[17], (L, D)),
        "w_group": nrm(ks[18], (L, D, N_GROUPS), D ** -0.5),
        "b_group": nrm(ks[19], (L, N_GROUPS), 0.01),
        "w_router": nrm(ks[20], (L, D, N_EXPERTS), D ** -0.5),
        "b_router": nrm(ks[21], (L, N_EXPERTS), 0.01),
        "w_expert_gate": nrm(ks[22], (L, N_EXPERTS, D, D_EXPERT), D ** -0.5),
        "w_expert_up": nrm(ks[23], (L, N_EXPERTS, D, D_EXPERT), D ** -0.5),
        "w_expert_down": nrm(ks[24], (L, N_EXPERTS, D_EXPERT, D), D_EXPERT ** -0.5),
        "final_norm_g": gain(ks[25], (D,)),
    }

def second_block(x, c, mod_w, mod_b, norm1_g, w_in, conv_w, conv_b, igate_b, fgate_b,
              q_norm_g, kv_norm_g, w_uq, w_ukv, w_branch_m, w_branch_a, w_out, norm2_g,
              w_group, b_group, w_router, b_router, w_expert_gate, w_expert_up,
              w_expert_down, final_norm_g):
    B, S, D = x.shape
    pos = jnp.arange(S, dtype=jnp.float32)
    inv_freq = 1.0 / (ROPE_THETA ** (jnp.arange(0, QK_ROPE, 2, dtype=jnp.float32) / QK_ROPE))
    ang = pos[:, None] * inv_freq[None, :]
    cos = jnp.cos(ang).astype(x.dtype)
    sin = jnp.sin(ang).astype(x.dtype)
    cond = jax.nn.silu(c)
    for l in range(DEPTH):
        mod = cond @ mod_w[l] + mod_b[l]
        shift1, scale1, gate1, shift2, scale2, gate2 = jnp.split(mod, N_MOD, axis=-1)
        h = modulate(rms_norm_2(x, norm1_g[l]), shift1, scale1)
        x = x + gate1[:, None, :] * mixer_sublayer(
            h, cos, sin, w_in[l], conv_w[l], conv_b[l], igate_b[l], fgate_b[l],
            q_norm_g[l], kv_norm_g[l], w_uq[l], w_ukv[l], w_branch_m[l], w_branch_a[l], w_out[l])
        h = modulate(rms_norm_2(x, norm2_g[l]), shift2, scale2)
        x = x + gate2[:, None, :] * hierarchical_moe(
            h, w_group[l], b_group[l], w_router[l], b_router[l],
            w_expert_gate[l], w_expert_up[l], w_expert_down[l])
    return rms_norm_2(x, final_norm_g)


def setup_inputs(seed=0):
    out = dict(first_inputs(seed))
    for name, value in second_inputs(seed + 1).items():
        if name != "x":
            out[name + "_2"] = value
    return out


def reference(
    x, g_mix_norm, w_in, g_q, g_k, pe_cmp, w_cmp1, b_cmp1, w_cmp2, b_cmp2, conv_w, g_out, w_o,
    g_ffn_norm, w_up, w_down, c_2, mod_w_2, mod_b_2, norm1_g_2, w_in_2, conv_w_2, conv_b_2,
    igate_b_2, fgate_b_2, q_norm_g_2, kv_norm_g_2, w_uq_2, w_ukv_2, w_branch_m_2, w_branch_a_2,
    w_out_2, norm2_g_2, w_group_2, b_group_2, w_router_2, b_router_2, w_expert_gate_2,
    w_expert_up_2, w_expert_down_2, final_norm_g_2,
):
    x = first_block(
        x, g_mix_norm, w_in, g_q, g_k, pe_cmp, w_cmp1, b_cmp1, w_cmp2, b_cmp2, conv_w, g_out,
        w_o, g_ffn_norm, w_up, w_down,
    )
    return second_block(
        x, c_2, mod_w_2, mod_b_2, norm1_g_2, w_in_2, conv_w_2, conv_b_2, igate_b_2, fgate_b_2,
        q_norm_g_2, kv_norm_g_2, w_uq_2, w_ukv_2, w_branch_m_2, w_branch_a_2, w_out_2,
        norm2_g_2, w_group_2, b_group_2, w_router_2, b_router_2, w_expert_gate_2, w_expert_up_2,
        w_expert_down_2, final_norm_g_2,
    )


_drawn_inputs = setup_inputs


def setup_inputs(seed=0):
    import zlib

    import numpy as np

    out = dict(_drawn_inputs(seed))
    spreads = {}
    factors = {'g_q': 7.37,
     'g_k': 8.0,
     'b_cmp1': 8.0,
     'b_cmp2': 7.417,
     'g_out': 3.832,
     'g_ffn_norm': 3.667,
     'mod_b_2': 4.92,
     'norm1_g_2': 8.0,
     'conv_w_2': 2.841,
     'conv_b_2': 200.0,
     'igate_b_2': 200.0,
     'fgate_b_2': 7.639,
     'q_norm_g_2': 8.0,
     'kv_norm_g_2': 8.0,
     'w_uq_2': 4.741,
     'norm2_g_2': 7.352,
     'b_group_2': 7.872,
     'b_router_2': 26.764,
     'final_norm_g_2': 21.048}
    for name, (base, spread) in spreads.items():
        noise = np.random.default_rng([zlib.crc32(name.encode()), seed]).standard_normal(out[name].shape)
        drawn = base * np.exp(spread * noise) if base else spread * noise
        out[name] = __import__('jax').numpy.asarray(drawn.astype(out[name].dtype))
    for name, factor in factors.items():
        out[name] = (out[name] * factor).astype(out[name].dtype)
    return out
```

```python
from contextlib import ExitStack

import concourse.bass as bass
import numpy as np
from concourse import mybir

F32 = mybir.dt.float32
F32R = mybir.dt.float32r
I32 = mybir.dt.int32
ALU = mybir.AluOpType
ACT = mybir.ActivationFunctionType
AX = mybir.AxisListType

P = 128
T = 512
D = 1024
NT = T // P
KT = D // P
PC = 256
PIECE = KT * PC
EPS = 1e-6
NEG = -1e30

HD = 64
NH = 8
NG = 2
CMP_I = 31
CS = 16
FQ = 4



def first_pieces():
    return ([("kcvc",), ("ksvs",), ("kwvw",), ("q", 0), ("q", 1)]
            + [("cmp", c, f) for c in range(2) for f in range(2)]
            + [(n, i) for i in range(2) for n in ("hc", "cg", "bg")]
            + [("wo", n) for n in range(4)])


def ffn_pieces():
    return [(n, r, j) for r in range(FQ) for n in ("up", "down") for j in range(4)]


MOD_PIECES = 24

MH = 4
MV = 256
AH = 8
NE = 32
NEG_ = 4
EG = NE // NEG_
DE = 256
BS = 64
NBLK = 48
MIN_BLK = 2 * T // BS
WE = 3 * PIECE
WS = 4
CQ, CKV = 384, 256


def mixer_pieces():
    return ([("qk", j) for j in range(4)] + [("om", j) for j in range(4)] + [("vm", j) for j in range(4)]
            + [("c3", j) for j in range(3)]
            + [(n, j) for j in range(4) for n in ("gm", "bm")]
            + [("qn", 0), ("qn", 1), ("qr",), ("kn",), ("va",)]
            + [(n, j) for j in range(4) for n in ("ga", "ba")]
            + [("wout", j) for j in range(4)])


def split_pieces():
    return first_pieces() + ffn_pieces() + mixer_pieces()


def all_pieces():
    out = list(first_pieces())
    for i, p in enumerate(ffn_pieces()):
        out.append(p)
        if i < MOD_PIECES:
            out.append(("mod", i))
    return out + mixer_pieces()


def columns(fields):
    at, out = 0, {}
    for name, n in fields:
        out[name] = (at, at + n)
        at += n
    out["_"] = (0, at)
    return out


PAR = columns([("g_mix", 8), ("g_ffn", 8), ("g_out", 8), ("g_q", 1), ("g_k", 3), ("b_cmp1", 4), ("pe", 32),
               ("conv_w", 12), ("w_cmp2", 256), ("b_cmp2", 128), ("c", 8), ("mod_b", 48)])
PAR2 = columns([("g_1", 8), ("g_2", 8), ("conv_w2", 32), ("conv_b2", 8), ("g_cq", 3), ("g_ckv", 2), ("b_if", 8), ("b_gr", 36)])
TAB3 = columns([("dec", 32), ("iota", NBLK), ("thr", 8), ("tok", NT), ("final_g", D)])
SMW = columns([("gl", KT * 24)])
SMW2 = columns([("if", KT * 8), ("gr", KT * 36)])
TAB2 = columns([("cos", NT * 32), ("sin", NT * 32), ("causal", T), ("chunk", T)])
CON = columns([("ident", P), ("tri", P), ("one", 1), ("mhalf", 1)])
BIAS = columns([("alibi", NH * T), ("cmpb", NT * NH * 32), ("cmpm", NT * 32)])



def plan_groups():
    g = [("h0", f, "v") for f in range(KT)]
    g += [("gl", 0, "a")]
    for n in ("kcvc", "ksvs", "kwvw"):
        g += [(n, t, "a") for t in range(2)]
    g += [("cT", c, "v") for c in range(4)]
    g += [(("q", j), t, "a") for j in range(2) for t in range(2)]
    g += [("kT", c, "v") for c in range(4)]
    g += [("cmp1", c, "v") for c in range(4)]
    g += [("cmpk", 0, "v"), ("cmpv", 0, "v"), ("cmpkT", 0, "v")]
    g += [("qT", c, "v") for c in range(4)]
    for q in range(NT):
        g += [("cS", 2 * q, "v"), ("cS", 2 * q + 1, "v"), ("cP", q, "v"), ("cO", q, "v")]
    for i in range(2):
        g += [("hc", 2 * i + f, "a") for f in range(2)]
        g += [("cg", 2 * i + f, "v") for f in range(2)]
        g += [("bg", 2 * i + f, "v") for f in range(2)]
    g += [("csq", 0, "v")]
    g += [("aT", f, "v") for f in range(4)]
    g += [("wo", i, "v") for i in range(16)]
    g += [("h1", f, "v") for f in range(KT)]
    m = 0
    for r in range(FQ):
        for j in range(4):
            g += [("up", (r * 4 + j) * 2 + f, "a") for f in range(2)]
            if m < MOD_PIECES:
                g += [("mod", m, "v")]
                m += 1
        for j in range(4):
            g += [("down", (r * 4 + j) * 2 + t, "v") for t in range(2)]
            if m < MOD_PIECES:
                g += [("mod", m, "v")]
                m += 1
    g += [("h2", f, "v") for f in range(KT)]
    g += [("if", 0, "v")]
    g += [("qk", f, "a") for f in range(8)]
    g += [("om", t, "a") for t in range(8)]
    g += [("cum", 0, "v")]
    g += [("crow", h, "v") for h in range(MH)]
    g += [("vm", t, "a") for t in range(8)]
    g += [("c3", t, "a") for t in range(6)]
    g += [("yT", f, "v") for f in range(KT)]
    for j in range(4):
        g += [("gm", 2 * j + f, "a") for f in range(2)]
        g += [("bm", 2 * j + f, "v") for f in range(2)]
    g += [("cT2", f, "v") for f in range(5)]
    g += [("krT", 0, "v")]
    g += [("qn", h, "a") for h in range(AH)]
    for t in range(NT):
        g += [("qr", t, "v")]
    g += [("qrT", t, "v") for t in range(NT)]
    g += [("kn", h, "a") for h in range(AH)]
    g += [("va", i, "a") for i in range(8)]
    g += [("yaT", i, "v") for i in range(8)]
    for j in range(4):
        g += [("ga", 2 * j + f, "a") for f in range(2)]
        g += [("ba", 2 * j + f, "v") for f in range(2)]
    g += [("g1r", i, "a") for i in range(2)]
    g += [("wout", i, "v") for i in range(8)]
    g += [("g2r", i, "a") for i in range(2)]
    g += [("h3", f, "v") for f in range(KT)]
    g += [("gr", 0, "v"), ("cnt", 0, "v"), ("rank", 0, "v"), ("pstart", 0, "v"), ("bexp", 0, "v"), ("slotT", 0, "v")]
    return g


GROUPS = plan_groups()
GIDX = {(w, i): n for n, (w, i, _) in enumerate(GROUPS)}
GRING = 3


def last_groups():
    out = {}
    for p in first_pieces() + ffn_pieces() + [("mod", m) for m in range(MOD_PIECES)] + mixer_pieces():
        k = p[0]
        if k in ("kcvc", "ksvs", "kwvw"):
            out[p] = GIDX[k, 1]
        elif k == "q":
            out[p] = GIDX[p, 1]
        elif k == "cmp":
            out[p] = GIDX["cmp1", 2 * p[1] + p[2]]
        elif k in ("hc", "cg", "bg"):
            out[p] = GIDX[k, 2 * p[1] + 1]
        elif k == "wo":
            out[p] = GIDX[k, 4 * p[1] + 3]
        elif k == "mod":
            out[p] = GIDX[p]
        elif k in ("om", "vm", "c3", "gm", "bm", "ga", "ba", "wout"):
            out[p] = GIDX[k, 2 * p[1] + 1]
        elif k == "qk":
            out[p] = GIDX[k, 2 * p[1] + 1]
        elif k == "qn":
            out[p] = GIDX[k, 4 * p[1] + 3]
        elif k in ("qr", "kn", "va"):
            out[p] = GIDX[k, 3 if k == "qr" else 7]
        else:
            out[p] = GIDX[k, 2 * (4 * p[1] + p[2]) + 1]
    return out


LAST = last_groups()


def freed_count(n):
    e = GROUPS[n][2]
    return e, sum(1 for x in GROUPS[:n + 1] if x[2] == e)


def build(nc, x, wp, par_d, con_d, smw_d, bias_d, par2_d, smw2_d, tab2_d, tab3_d, wexp, out):
    with ExitStack() as ctx:
        def sb(name, n, dt=F32):
            return ctx.enter_context(nc.sbuf_tensor(name, [P, n], dt))

        sems = {}

        def S(name):
            if name not in sems:
                sems[name] = ctx.enter_context(nc.semaphore(name))
            return sems[name]

        X = sb("X", NT * D)
        raw = sb("raw", 2 * PIECE)
        par = sb("par", PAR["_"][1])
        con = sb("con", CON["_"][1])
        smh, sml = sb("smh", SMW2["_"][1], F32R), sb("sml", SMW2["_"][1], F32R)
        st = sb("st", 384)
        arena = sb("arena", 18560)
        with ExitStack() as dense:
            def part(name, n, dt=F32R):
                return dense.enter_context(nc.sbuf_tensor(name, [P, n], dt))

            wh, wl = part("wh", 2 * PIECE), part("wl", 2 * PIECE)
            Hh, Hl = part("Hh", KT * T), part("Hl", KT * T)
            Yh, Yl = part("Yh", KT * T), part("Yl", KT * T)
        wgu2, wgu3, wdn2, wdn3 = sb("wgu2", 2 * PIECE), sb("wgu3", 2 * PIECE), sb("wdn2", PIECE), sb("wdn3", PIECE)
        wdh_, wdl_ = sb("wdh", 2 * PIECE, F32R), sb("wdl", 2 * PIECE, F32R)
        ahh_, ahl_ = sb("ahh", 256, F32R), sb("ahl", 256, F32R)
        yb_ = sb("yb", 2 * D)

        smw = arena[:, 0:SMW["_"][1]]
        smw2 = arena[:, 0:SMW2["_"][1]]
        x_spill = nc.dram_tensor("x_spill", (P, NT * D), F32).ap()
        Xv = X[:, :].rearrange("p (t n) -> p t n", t=NT)

        def AR(a, n):
            return arena[:, a:a + n]

        def cols(t, table, name):
            a, b = table[name]
            return t[:, a:b]

        ident = cols(con, CON, "ident")
        one = cols(con, CON, "one")
        mhalf = cols(con, CON, "mhalf")

        alibi = AR(0, 4096).rearrange("p (h n) -> p h n", h=NH)
        cmpb = AR(4096, 1024).rearrange("p (q h i) -> p q h i", q=NT, h=NH)
        cmpm = AR(5120, 128).rearrange("p (q i) -> p q i", q=NT)
        Zq = AR(5248, 2048).rearrange("p (t n) -> p t n", t=NT)
        Oat = Zq
        Zk = AR(7296, 2048).rearrange("p (t n) -> p t n", t=NT)
        Zv = AR(9344, 1024).rearrange("p (t s n) -> p t s n", t=NT, s=2)
        conv = AR(7296, 2048).rearrange("p (f n) -> p f n", f=4)
        kdup = AR(10368, 2048).rearrange("p (t c u d) -> p t c u d", t=NT, c=4, u=2)
        cw = AR(10368, 2048)
        ctmp_h = AR(10368, 1024).rearrange("p (f n) -> p f n", f=2)
        ctmp_u = AR(11392, 512)
        otmp = AR(11904, 512)
        fsq = AR(10368, 1024).rearrange("p (r n) -> p r n", r=2)
        kT = AR(12416, 2048).rearrange("p (c n) -> p c n", c=4)
        qT = AR(14464, 2048).rearrange("p (c n) -> p c n", c=4)
        blkt = AR(14464, 1984).rearrange("p (c b a i) -> p c b a i", c=4, b=2, a=8)
        cdup = AR(16512, 2048).rearrange("p (t c u d) -> p t c u d", t=NT, c=4, u=2)
        SP = AR(16512, 1024).rearrange("p (r n) -> p r n", r=2)
        PTs = AR(17536, 1024).rearrange("p (r n) -> p r n", r=2)
        frelu = SP
        hraw = AR(12416, 4096).rearrange("p (t n) -> p t n", t=NT)
        blkh = Yh[:, 0:1984].rearrange("p (c k n) -> p c k n", c=2, k=16)
        blkl = Yl[:, 0:1984].rearrange("p (c k n) -> p c k n", c=2, k=16)
        Hhv, Hlv = (t[:, :].rearrange("p (k n) -> p k n", k=KT) for t in (Hh, Hl))
        Yhv, Ylv = (t[:, :].rearrange("p (k n) -> p k n", k=KT) for t in (Yh, Yl))

        modc = st[:, 0:48]
        condc = st[:, 48:56]
        macc = AR(17536, 512).rearrange("p (r n) -> p r n", r=2)
        nst = [48 + 16]

        def small(n):
            nst[0] += n
            assert nst[0] <= 384
            return st[:, nst[0] - n:nst[0]]

        ss = small(NT)
        ms = small(NT)
        rstd = small(NT)
        ssqk = small(48)
        msqk = small(48)
        rqk = small(48)
        gates = small(96).rearrange("p (t n) -> p t n", t=NT)
        csum = small(8)
        cmaxn = small(8)
        ccoef = small(8)
        ssk = small(2)
        msk = small(2)
        rsk = small(2)
        ncoef = small(8)
        rsum = small(16)
        nmax = small(2)
        cond_t = small(8)

        modv = modc.rearrange("p (m k) -> p m k", m=6)
        nst[0] = 64
        ss2, ms2, rstd2 = small(NT), small(NT), small(NT)
        aff1, aff2 = small(KT), small(KT)
        ifr = small(32).rearrange("p (t n) -> p t n", t=NT)
        fabs = small(16).rearrange("p (t n) -> p t n", t=NT)
        flog = small(16).rearrange("p (t n) -> p t n", t=NT)
        lf = small(16).rearrange("p (t n) -> p t n", t=NT)
        Bc = small(16).rearrange("p (t n) -> p t n", t=NT)
        cc_ = small(16).rearrange("p (t n) -> p t n", t=NT)
        nm, emn, den, rr = small(16), small(16), small(16), small(16)
        ssc, msc, rsc = small(8), small(8), small(8)
        small_pad = small(1)
        ssc_done = small(1)
        rsum2, nmax2, rinv = small(16), small(2), small(16)
        TAB = {n: (a, b) for n, (a, b) in TAB2.items()}
        hraw2 = AR(8192, 4096).rearrange("p (t n) -> p t n", t=NT)
        qkT = AR(0, 4096).rearrange("p (f n) -> p f n", f=8)
        To = AR(4096, 4096).rearrange("p (t n) -> p t n", t=NT)
        c3 = AR(8192, 3072).rearrange("p (t n) -> p t n", t=NT)
        crow = AR(11264, 2048).rearrange("p (h n) -> p h n", h=MH)
        Eb = AR(13312, 1024).rearrange("p (r n) -> p r n", r=2)
        SP2 = AR(14336, 1024).rearrange("p (r n) -> p r n", r=2)
        PT2 = AR(15360, 1024).rearrange("p (r n) -> p r n", r=2)
        cacc, cth = Eb, SP2
        xpad = AR(16384, 1032).rearrange("p (r n) -> p r n", r=2)
        causal = AR(17924, 512)
        vm = Xv
        merged = AR(0, 4096).rearrange("p (f n) -> p f n", f=8)
        tg = Eb
        qn = AR(4096, 4096).rearrange("p (h n) -> p h n", h=AH)
        qrT = AR(8192, 2048).rearrange("p (c n) -> p c n", c=4)
        krT = AR(10240, 512)
        chunk = AR(10752, 512)
        cosT = AR(12288, 128).rearrange("p (t n) -> p t n", t=NT)
        sinT = AR(12416, 128).rearrange("p (t n) -> p t n", t=NT)
        kr2 = AR(12544, 512).rearrange("p (t u n) -> p t u n", t=NT, u=2)
        ropet = AR(13056, 256)
        kn = AR(11264, 4096).rearrange("p (h n) -> p h n", h=AH)
        SP3 = AR(15360, 1024).rearrange("p (r n) -> p r n", r=2)
        PT3 = AR(16384, 1024).rearrange("p (r n) -> p r n", r=2)
        qrr = AR(15360, 2048).rearrange("p (t n) -> p t n", t=NT)
        ya = AR(17408, 1024)
        va = Xv
        Ch, Cl = Yhv, Ylv
        tga = AR(16384, 1024).rearrange("p (r n) -> p r n", r=2)
        tba = AR(15360, 1024).rearrange("p (r n) -> p r n", r=2)
        g1row = AR(4096, 1024)
        wtmp = AR(5120, 1024).rearrange("p (r n) -> p r n", r=2)

        xn_rows = nc.dram_tensor("xn_rows", (T, D), F32).ap()
        slot_tok = nc.dram_tensor("slot_tok", (NBLK * BS, 1), F32).ap()
        y_rows = nc.dram_tensor("y_rows", (NBLK * BS, D), F32).ap()
        hraw3 = AR(0, 4096).rearrange("p (t n) -> p t n", t=NT)
        wgu = [AR(0, 2 * PIECE), AR(2 * PIECE, 2 * PIECE), wgu2[:, :], wgu3[:, :]]
        wdn = [AR(4 * PIECE, PIECE), AR(5 * PIECE, PIECE), wdn2[:, :], wdn3[:, :]]
        xgT = AR(12288, 1024).rearrange("p (u k n) -> p u k n", u=2, k=KT)
        g2row = AR(13312, 1024)
        tab3 = AR(14336, TAB3["_"][1])
        at = [14336 + TAB3["_"][1]]

        def AT(n):
            at[0] += n
            assert at[0] <= 18560
            return AR(at[0] - n, n)

        def v3(n):
            return AT(NT * n).rearrange("p (t n) -> p t n", t=NT)

        Lg, gsh, gex, okey = v3(36), v3(4), v3(4), v3(4)
        oh_g, insh, key8, oh1, oh2, d2 = v3(4), v3(8), v3(8), v3(8), v3(8), v3(8)
        gmx, gsum, pg, km, m1, m2, e2, w1c, w2c, dst1, dst2 = (AT(NT) for _ in range(11))
        ing4 = AT(NT * 32)
        A1, A2, Aa, Sl, Tmp = v3(32), v3(32), v3(32), v3(32), v3(32)
        cntc, nbc, pend = AT(1), AT(1), AT(1)
        nb8 = AT(8)
        triex = AT(32)
        ps64 = AT(32)
        cmpe = AT(NBLK)
        bexpf = AT(NBLK)
        zer = AT(NBLK)
        slotr = AT(BS)
        bexp_i = AT(NBLK).bitcast(I32)
        slot_i = AT(NBLK + 2).bitcast(I32)
        dst_i = AT(8).bitcast(I32)
        idxc = AT(WS).bitcast(I32)
        nblkf = AT(1)
        nblk_i = AT(1).bitcast(I32)
        tanhg = AT(2 * 128).rearrange("p (u n) -> p u n", u=2)
        acth = AT(2 * 128).rearrange("p (u n) -> p u n", u=2)
        ahh, ahl, wdh, wdl, yb = (t[:, :].rearrange("p (u n) -> p u n", u=2) for t in (ahh_, ahl_, wdh_, wdl_, yb_))
        xg = raw[:, :].rearrange("p (u n) -> p u n", u=WS)
        r12 = AR(0, 8192).rearrange("p (t k n) -> p t k n", t=NT, k=2)
        ssf, msf, rsf = AT(NT), AT(NT), AT(NT)

        G = [ctx.enter_context(nc.psum_tensor(f"G{i}", [P, 512], F32)) for i in range(GRING)]
        SA = [ctx.enter_context(nc.psum_tensor(f"SA{i}", [P, 512], F32)) for i in range(2)]
        PB = [ctx.enter_context(nc.psum_tensor(f"PB{i}", [P, 512], F32)) for i in range(2)]
        OB = ctx.enter_context(nc.psum_tensor("OB", [P, 512], F32))

        SPL = {p: n for n, p in enumerate(split_pieces())}
        MODN = MOD_PIECES
        ORDER = all_pieces()

        def wait_group(eng, what, i):
            eng.wait_ge(S("group_filled"), GIDX[what, i] + 1)
            return G[GIDX[what, i] % GRING]

        def free_group(ins, what, i):
            ins.then_inc(S("bank_freed_" + GROUPS[GIDX[what, i]][2]), 1)

        def wait_freed(eng, what, i):
            e, n = freed_count(GIDX[what, i])
            eng.wait_ge(S("bank_freed_" + e), n)

        def wait_used(eng, p):
            eng.wait_ge(S("group_filled"), LAST[p] + 1)

        def split_slot(s):
            a = (s % 2) * PIECE
            return slice(a, a + PIECE)

        raw_of = {}
        for n, p in enumerate(ORDER):
            raw_of[p] = n

        def wait_raw(eng, p):
            n = raw_of[p]
            eng.wait_ge(S(f"raw_loaded{n % 2}"), 16 * (n // 2 + 1))
            return raw[:, (n % 2) * PIECE:(n % 2 + 1) * PIECE]

        units = [(ty, q, h) for ty in range(2) for q in range(NT) for h in range(NH)]
        munits = [(h, q) for h in range(MH) for q in range(NT)]
        aunits = [(q, h) for q in range(NT) for h in range(AH)]
        M0, A0 = len(units), len(units) + len(munits)
        MSCALE = 0.25 * 128 ** -0.5
        ASCALE = 192 ** -0.5

        def bc4(a):
            return a.unsqueeze(3).to_broadcast([P, NT, NEG_, EG])

        XT = [G[0], G[1]]
        GB, UB = [G[2], SA[0]], [SA[1], PB[0]]
        YB = [PB[1], OB]

        def SPsq(f):
            return PTs[:, f % 2, :] if f < 2 else SP[:, f % 2, :]

        block = ctx.enter_context(nc.Block())

        @block.sync
        def _(sp):
            sp.dma_start(Xv[:, 0:1, :], x.rearrange("(t p) n -> p t n", p=P)[:, 0:1, :]).then_inc(S("x_loaded"), 16)
            sp.dma_start(con[:, :], con_d).then_inc(S("con_loaded"), 16)
            sp.dma_start(par[:, :], par_d).then_inc(S("par_loaded"), 16)
            sp.dma_start(smw, smw_d).then_inc(S("smw_loaded"), 16)
            for t in range(1, NT):
                sp.dma_start(Xv[:, t:t + 1, :], x.rearrange("(t p) n -> p t n", p=P)[:, t:t + 1, :]).then_inc(S("x_loaded"), 16)
            for n, p in enumerate(ORDER):
                if p == ("bg", 0):
                    sp.wait_ge(S("bias_loaded"), 16)
                    for k in range(MIN_BLK * BS, NBLK * BS, T):
                        sp.dma_start(y_rows[k:k + T, :].rearrange("(t p) n -> p t n", p=P), AR(0, 4096).rearrange("p (t n) -> p t n", t=NT)).then_inc(S("rows_filled"), 16)
                if n >= 2:
                    o = ORDER[n - 2]
                    if o[0] == "mod":
                        sp.wait_ge(S("mod_summed"), o[1] + 1)
                    else:
                        sp.wait_ge(S("low_split"), SPL[o] + 1)
                sp.dma_start(raw[:, (n % 2) * PIECE:(n % 2 + 1) * PIECE], wp[n]).then_inc(S(f"raw_loaded{n % 2}"), 16)
                if p == ("qk", 0):
                    wait_freed(sp, "mod", MOD_PIECES - 1)
                    wait_group(sp, "down", 0)
                    sp.wait_ge(S("rows_filled"), 16 * (NBLK - MIN_BLK) * BS // T)
                    sp.dma_start(par[:, 0:PAR2["_"][1]], par2_d).then_inc(S("par2_loaded"), 16)
                    sp.dma_start(smw2, smw2_d).then_inc(S("smw2_loaded"), 16)
                if p == ("om", 0):
                    sp.wait_ge(S("rows_normed"), 3 * NT)
                    sp.dma_start(x_spill, X[:, :]).then_inc(S("x_spilled"), 16)
                if p == ("vm", 0):
                    wait_freed(sp, "h2", KT - 1)
                    sp.wait_ge(S("qk_done"), 8)
                    sp.dma_start(causal, tab2_d[:, 256:768]).then_inc(S("causal_loaded"), 16)
                if p == ("qr",):
                    wait_freed(sp, "bm", 7)
                    sp.wait_ge(S("kr_normed"), 1)
                    sp.dma_start(AR(12288, 256), tab2_d[:, 0:256]).then_inc(S("cos_loaded"), 16)
                if p == ("va",):
                    wait_group(sp, "krT", 0)
                    wait_group(sp, "cT2", 4)
                    sp.dma_start(chunk, tab2_d[:, 768:1280]).then_inc(S("chunk_loaded"), 16)
                if p == ("wout", 0):
                    sp.wait_ge(S("values_summed"), A0 + len(aunits))
                    sp.dma_start(X[:, :], x_spill).then_inc(S("x_back"), 16)
                if n == 1:
                    sp.wait_ge(S("sml_done"), 1)
                    sp.dma_start(AR(0, BIAS["_"][1]), bias_d).then_inc(S("bias_loaded"), 16)
            wait_freed(sp, "ba", 7)
            sp.dma_start(tab3, tab3_d).then_inc(S("tab3_loaded"), 16)
            sp.wait_ge(S("rows_normed"), 4 * NT)
            sp.dma_start(xn_rows.rearrange("(t p) n -> p t n", p=P), hraw3).then_inc(S("xn_stored"), 16)
            sp.wait_ge(S("zeros_ready"), 1)
            sp.dma_start(slot_tok.rearrange("(p b) o -> p (b o)", b=NBLK), zer[0:BS, :]).then_inc(S("slots_zeroed"), 16)
            sp.wait_ge(S("scattered"), 128)
            sp.dma_start(slotr[0:NBLK, :], slot_tok.rearrange("(b p) o -> b (p o)", p=BS)).then_inc(S("slots_loaded"), 16)
            sp.wait_ge(S("xn_stored"), 16)
            sp.wait_ge(S("bexp_ready"), 1)
            blocks = sp.value_load(nblk_i[0:1, :], min_val=0, max_val=NBLK)
            with sp.Fori(0, NBLK // WS) as i:
                for v in range(WS):
                    with sp.If(WS * i + v < blocks):
                        e = sp.value_load(bexp_i[0:1, bass.ds(WS * i + v, 1)], min_val=0, max_val=NE - 1)
                        sp.wait_ge(S("up_ready"), WS * i + v + 1)
                        sp.dma_start(wgu[v].rearrange("p (o n) -> p o n", o=1),
                                     wexp[bass.ds(e, 1), :, 0:2 * PIECE].rearrange("o p n -> p o n")).then_inc(S(f"gu_loaded{v}"), 16)
                        sp.wait_ge(S("down_low_p"), WS * i + v + 1)
                        sp.wait_ge(S("down_low_v"), WS * i + v + 1)
                        sp.dma_start(wdn[v].rearrange("p (o n) -> p o n", o=1),
                                     wexp[bass.ds(e, 1), :, 2 * PIECE:WE].rearrange("o p n -> p o n")).then_inc(S(f"down_loaded{v}"), 16)
            for t in range(NT):
                sp.wait_ge(S("out_ready"), t + 1)
                sp.dma_start(out[t * P:(t + 1) * P, :], Xv[:, t, :]).then_inc(S("stored"), 16)
            sp.wait_ge(S("stored"), 16 * NT)

        @block.gpsimd
        def _(pool):
            c = [0]

            def own(ins):
                c[0] += 1
                ins.then_inc(S("pool_step"), 1)
                pool.wait_ge(S("pool_step"), c[0])

            def low(p):
                s = SPL[p]
                pool.wait_ge(S("high_split"), s + 1)
                pool.tensor_tensor(wl[:, split_slot(s)], wait_raw(pool, p), wh[:, split_slot(s)].bitcast(F32),
                                   ALU.subtract).then_inc(S("low_split"), 1)

            def rstd_of(dst, tmp, src, n, width):
                own(pool.tensor_scalar(tmp, src, 1.0 / width, EPS, ALU.mult, ALU.add))
                return pool.tensor_tensor(dst, tmp, mhalf.to_broadcast([P, n]), ALU.pow)

            order = iter(split_pieces())
            sp_list = split_pieces()
            pool.wait_ge(S("con_loaded"), 16)
            pool.wait_ge(S("ss_x"), 1)
            rstd_of(rstd, ms, ss, NT, D).then_inc(S("rstd_x"), 1)
            pool.wait_ge(S("smh_done"), 1)
            pool.tensor_tensor(sml[:, 0:SMW["_"][1]], smw, smh[:, 0:SMW["_"][1]].bitcast(F32), ALU.subtract).then_inc(S("sml_done"), 1)
            for p in sp_list[:5]:
                low(p)
            pool.wait_ge(S("ss_k"), 1)
            rstd_of(rqk[:, 0:16], msqk[:, 0:16], ssqk[:, 0:16], 16, HD).then_inc(S("rstd_k"), 1)
            low(sp_list[5])
            pool.wait_ge(S("ss_q"), 1)
            rstd_of(rqk[:, 16:48], msqk[:, 16:48], ssqk[:, 16:48], 32, HD).then_inc(S("rstd_q"), 1)
            for p in sp_list[6:9]:
                low(p)
            pool.wait_ge(S("ss_kc"), 1)
            own(pool.tensor_scalar(msk[0:32, :], ssk[0:32, :], 1.0 / HD, EPS, ALU.mult, ALU.add))
            pool.tensor_tensor(rsk[0:32, :], msk[0:32, :], mhalf[0:32, :].to_broadcast([32, 2]), ALU.pow).then_inc(S("rstd_kc"), 1)
            for p in sp_list[9:16]:
                low(p)
            wait_freed(pool, "csq", 0)
            rstd_of(rqk[:, 4:8], msqk[:, 4:8], ssqk[:, 4:8], NT, 512).then_inc(S("rstd_conv"), 1)
            pool.wait_ge(S("ss_attn"), 1)
            rstd_of(rqk[:, 0:4], msqk[:, 0:4], ssqk[:, 0:4], NT, 512).then_inc(S("rstd_attn"), 1)
            for p in sp_list[16:20]:
                low(p)
            pool.wait_ge(S("ss_x"), 2)
            rstd_of(rstd, ms, ss, NT, D).then_inc(S("rstd_x"), 1)
            NB1 = len(first_pieces()) + len(ffn_pieces())
            for p in sp_list[20:NB1]:
                low(p)
            pool.wait_ge(S("ss_x"), 3)
            rstd_of(rstd2, ms2, ss2, NT, D).then_inc(S("rstd_x"), 1)
            pool.wait_ge(S("smh_done"), 2)
            pool.tensor_tensor(sml[:, :], smw2, smh[:, :].bitcast(F32), ALU.subtract).then_inc(S("sml_done"), 1)
            NC3 = NB1 + 15
            for p in sp_list[NB1:NC3]:
                low(p)
            low(sp_list[NC3])
            pool.wait_ge(S("ss_c"), 1)
            own(pool.tensor_scalar(msc[:, 0:4], ssc[:, 0:4], 1.0 / CQ, EPS, ALU.mult, ALU.add))
            own(pool.tensor_scalar(msc[:, 4:8], ssc[:, 4:8], 1.0 / CKV, EPS, ALU.mult, ALU.add))
            pool.tensor_tensor(rsc, msc, mhalf.to_broadcast([P, 8]), ALU.pow).then_inc(S("rstd_c"), 1)
            for p in sp_list[NC3 + 1:]:
                low(p)
            pool.wait_ge(S("ss_x"), 4)
            rstd_of(rstd2, ms2, ss2, NT, D).then_inc(S("rstd_x"), 1)
            pool.wait_ge(S("dst_ready"), 1)
            pool.wait_ge(S("slots_zeroed"), 16)
            for k in range(2):
                for t in range(NT):
                    pool.indirect_dma_start(slot_tok, bass.IndirectOffsetOnAxis(ap=dst_i[:, 4 * k + t:4 * k + t + 1], axis=0),
                                            cols(tab3, TAB3, "tok")[:, t:t + 1], None).then_inc(S("scattered"), 16)
            pool.wait_ge(S("slot_idx_ready"), 1)
            pool.wait_ge(S("bexp_ready"), 1)
            pool.wait_ge(S("xn_stored"), 16)
            blocks = pool.value_load(nblk_i[0:1, :], min_val=0, max_val=NBLK)

            def gather(b, u, turn):
                if turn is not None:
                    pool.wait_ge(S("xt_ready"), turn)
                pool.tensor_copy(idxc[0:BS, u:u + 1], slot_i[0:BS, bass.ds(b, 1)]).then_inc(S("idx_ready"), 1)
                pool.wait_ge(S("idx_ready"), b + 1)
                pool.sem_inc(S("gather_turn"), 1)
                pool.indirect_dma_start(xg[0:BS, u, :], None, xn_rows, bass.IndirectOffsetOnAxis(ap=idxc[0:BS, u:u + 1], axis=0))                    .then_inc(S(f"xg_loaded{u}"), 16)

            gather(0, 0, None)
            gather(1, 1, None)
            with pool.Fori(0, NBLK // WS) as i:
                for v in range(WS):
                    with pool.If(WS * i + v < blocks):
                        b, u = WS * i + v, v % 2
                        gather(b + 2, (v + 2) % WS, b + 3)
                        pool.wait_ge(S("down_high"), b + 1)
                        pool.tensor_tensor(wdl[:, u, 0:1024], wdn[v][:, 0:1024], wdh[:, u, 0:1024].bitcast(F32), ALU.subtract).then_inc(S("down_low_p"), 1)
            for u in range(2):
                pool.wait_ge(S(f"y_stored{u}"), 16 * (NBLK // 2) + 16)
            for t in range(NT):
                for k in range(2):
                    pool.indirect_dma_start(r12[:, t, k, :], None, y_rows, bass.IndirectOffsetOnAxis(ap=dst_i[:, 4 * k + t:4 * k + t + 1], axis=0))\
                        .then_inc(S(f"picked{t}"), 16)
            for t in range(NT):
                pool.wait_ge(S("ss_f"), t + 1)
                own(pool.tensor_scalar(msf[:, t:t + 1], ssf[:, t:t + 1], 1.0 / D, EPS, ALU.mult, ALU.add))
                pool.tensor_tensor(rsf[:, t:t + 1], msf[:, t:t + 1], mhalf, ALU.pow).then_inc(S("rstd_f"), 1)

        @block.scalar
        def _(act):
            c = [0]

            def own(ins):
                c[0] += 1
                ins.then_inc(S("act_step"), 1)
                act.wait_ge(S("act_step"), c[0])

            sp_list = split_pieces()

            def high(s):
                if s >= len(sp_list):
                    return
                if s >= 2:
                    wait_used(act, sp_list[s - 2])
                act.activation(wh[:, split_slot(s)], wait_raw(act, sp_list[s]), ACT.Copy).then_inc(S("high_split"), 1)

            def squares(n, junk):
                for t in range(NT):
                    if n == 0:
                        act.wait_ge(S("x_loaded"), 64)
                    ins = act.activation(junk[:, t, :], Xv[:, t, :], ACT.Square, accum_out=ss[:, t:t + 1])
                ins.then_inc(S("ss_x"), 1)

            def transposed_high(what, n, dst, scale):
                for f in range(n):
                    b = wait_group(act, what, f)
                    act.activation(dst[:, f, :], b[:, :], ACT.Copy, scale=scale[:, f:f + 1]).then_inc(S(what + "_high"), 1)

            squares(0, hraw)
            act.wait_ge(S("par_loaded"), 16)
            act.activation(cond_t, cols(par, PAR, "c"), ACT.Tanh, scale=0.5).then_inc(S("cond_tanh"), 1)
            act.wait_ge(S("smw_loaded"), 16)
            act.activation(smh[:, 0:SMW["_"][1]], smw, ACT.Copy).then_inc(S("smh_done"), 1)
            high(0)
            act.wait_ge(S("par_loaded"), 16)
            transposed_high("h0", KT, Hhv, cols(par, PAR, "g_mix"))
            high(1)
            b = wait_group(act, "gl", 0)
            own(act.activation(gates, b[:, 0:96].rearrange("p (t n) -> p t n", t=NT), ACT.Tanh, scale=0.5))
            free_group(act.activation(gates, gates, ACT.Copy, scale=0.5, bias=0.5), "gl", 0)
            for s, what in enumerate(("kcvc", "ksvs", "kwvw")):
                if s:
                    high(s + 1)
                for t in range(2):
                    b = wait_group(act, what, t)
                    bv = b[:, :].rearrange("p (t n) -> p t n", t=2)
                    if s == 0:
                        ins = act.activation(Zk[:, 2 * t:2 * t + 2, 0:256], bv, ACT.Copy)
                    else:
                        act.activation(Zk[:, 2 * t:2 * t + 2, 128 + s * 128:256 + s * 128], bv[:, :, 0:128], ACT.Copy)
                        ins = act.activation(Zv[:, 2 * t:2 * t + 2, s - 1, :], bv[:, :, 128:256], ACT.Copy)
                    free_group(ins, what, t)
            for j in range(2):
                high(4 + j)
                for t in range(2):
                    b = wait_group(act, ("q", j), t)
                    free_group(act.activation(Zq[:, 2 * t:2 * t + 2, j * 256:(j + 1) * 256], b[:, :].rearrange("p (t n) -> p t n", t=2), ACT.Copy), ("q", j), t)
            wait_freed(act, "cT", 3)
            act.activation(Yh[:, 0:1984].rearrange("p (c k g i) -> p c k g i", c=2, k=16, g=2)[:, 0],
                           AR(14464, 1984).rearrange("p (c g k i) -> p c k g i", c=2, g=2, k=16)[:, 0], ACT.Copy)
            act.activation(Yh[:, 0:1984].rearrange("p (c k g i) -> p c k g i", c=2, k=16, g=2)[:, 1],
                           AR(14464, 1984).rearrange("p (c g k i) -> p c k g i", c=2, g=2, k=16)[:, 1], ACT.Copy).then_inc(S("blk_high"), 1)
            for s in range(6, 9):
                high(s)
                act.wait_ge(S("gelu_in"), s - 5)
                act.activation(cw[:, 512 + (s - 6) * 62:512 + (s - 5) * 62], cw[:, 256 + (s - 6) * 62:256 + (s - 5) * 62], ACT.Tanh, scale=0.7978845608028654).then_inc(S("gelu_tanh"), 1)
            high(9)
            act.wait_ge(S("gelu_in"), 4)
            act.activation(cw[:, 512 + 3 * 62:512 + 4 * 62], cw[:, 256 + 3 * 62:256 + 4 * 62], ACT.Tanh, scale=0.7978845608028654).then_inc(S("gelu_tanh"), 1)
            for q in range(NT):
                act.wait_ge(S("cmp_shifted"), q + 1)
                act.activation(cw[:, 1024:1280], cw[:, 768:1024], ACT.Exp).then_inc(S("cmp_exp"), 1)

            def unit(u):
                act.wait_ge(S("score_biased"), u + 1)
                ty, q, h = units[u]
                nk = (q + 1) * P
                act.activation(SP[:, u % 2, 0:nk], SP[:, u % 2, 0:nk], ACT.Exp, scale=-1.0, bias=nmax[:, u % 2:u % 2 + 1],
                               accum_out=rsum[:, ((u // 8) % 2) * 8 + h:((u // 8) % 2) * 8 + h + 1]).then_inc(S("probs_ready"), 1)

            for t in range(len(units) + 3):
                if t % 8 == 0 and t < 48:
                    high(10 + t // 8)
                if t < len(units):
                    unit(t)
                if t % 4 == 3 and t < 48 and (t // 4) % 6 < 2:
                    g = t // 4
                    f = 2 * (g // 6) + g % 6
                    b = wait_group(act, "hc", f)
                    if f >= 2:
                        wait_freed(act, "cg", f - 2)
                    free_group(act.activation(ctmp_h[:, f % 2, :], b[:, :], ACT.Copy), "hc", f)
            act.wait_ge(S("values_summed"), len(units))
            for f in range(4):
                wait_freed(act, "bg", f)
                act.activation(SPsq(f), conv[:, f, :], ACT.Square).then_inc(S("conv_sq"), 1)
                act.activation(Yhv[:, 4 + f, :], conv[:, f, :], ACT.Copy, scale=cols(par, PAR, "g_out")[:, 4 + f:5 + f]).then_inc(S("conv_high"), 1)
            act.wait_ge(S("attn_sum"), NT * 2)
            for t in range(NT):
                ins = act.activation(kT[:, t, :], Oat[:, t, :], ACT.Square, accum_out=ssqk[:, t:t + 1])
            ins.then_inc(S("ss_attn"), 1)
            high(16)
            transposed_high("aT", 4, Yhv, cols(par, PAR, "g_out"))
            high(17)
            high(18)
            high(19)
            wait_freed(act, "wo", 15)
            squares(1, hraw)
            transposed_high("h1", KT, Hhv, cols(par, PAR, "g_ffn"))
            s = 20
            for r in range(FQ):
                for j in range(4):
                    high(s)
                    s += 1
                    for f in range(2):
                        i = (r * 4 + j) * 2 + f
                        b = wait_group(act, "up", i)
                        if i >= 2:
                            act.wait_ge(S("ffn_sq"), i - 1)
                        ins = act.activation(frelu[:, i % 2, :], b[:, :], ACT.Relu)
                        free_group(ins, "up", i)
                        e, n = freed_count(GIDX["up", i])
                        act.wait_ge(S("bank_freed_a"), n)
                        act.activation(Yhv[:, 2 * j + f, :], frelu[:, i % 2, :], ACT.Square).then_inc(S("ffn_high"), 1)
                for j in range(4):
                    high(s)
                    s += 1

            NB1 = len(first_pieces()) + len(ffn_pieces())
            assert s == NB1 + 1
            wait_freed(act, "down", 31)
            for t in range(NT):
                ins = act.activation(hraw2[:, t, :], Xv[:, t, :], ACT.Square, accum_out=ss2[:, t:t + 1])
            ins.then_inc(S("ss_x"), 1)
            act.wait_ge(S("smw2_loaded"), 16)
            act.activation(smh[:, :], smw2, ACT.Copy).then_inc(S("smh_done"), 1)
            act.wait_ge(S("aff_ready"), 1)
            for f in range(KT):
                b = wait_group(act, "h2", f)
                act.activation(Hhv[:, f, :], b[:, :], ACT.Identity, scale=aff1[:, f:f + 1], bias=modv[:, 0, f:f + 1]).then_inc(S("h2_high"), 1)
            act.wait_ge(S("fabs_ready"), 1)
            own(act.activation(flog, fabs, ACT.Exp, scale=-1.0))
            act.activation(flog, flog, ACT.Ln, bias=1.0).then_inc(S("flog_ready"), 1)
            for i in range(8):
                if i % 2 == 0:
                    high(s)
                    s += 1
                b = wait_group(act, "qk", i)
                if i == 0:
                    act.wait_ge(S("xpad_zeroed"), 1)
                if i >= 2:
                    act.wait_ge(S("conv2_done"), i - 1)
                free_group(act.activation(xpad[:, i % 2, 3:515], b[:, :], ACT.Copy), "qk", i)
                if i >= 1:
                    act.wait_ge(S("conv2_done"), i)
                    act.activation(cth[:, (i - 1) % 2, :], cacc[:, (i - 1) % 2, :], ACT.Tanh, scale=0.5).then_inc(S("conv2_tanh"), 1)
            high(s)
            s += 1
            act.wait_ge(S("conv2_done"), 8)
            act.activation(cth[:, 1, :], cacc[:, 1, :], ACT.Tanh, scale=0.5).then_inc(S("conv2_tanh"), 1)
            for j in range(4):
                if j:
                    high(s)
                    s += 1
                for tp in range(2):
                    b = wait_group(act, "om", 2 * j + tp)
                    free_group(act.activation(To[:, 2 * tp:2 * tp + 2, j * PC:(j + 1) * PC], b[:, :].rearrange("p (t n) -> p t n", t=2), ACT.Tanh, scale=0.5), "om", 2 * j + tp)
            act.wait_ge(S("x_spilled"), 16)
            for j in range(4):
                high(s)
                s += 1
                for tp in range(2):
                    b = wait_group(act, "vm", 2 * j + tp)
                    free_group(act.activation(vm[:, 2 * tp:2 * tp + 2, j * PC:(j + 1) * PC], b[:, :].rearrange("p (t n) -> p t n", t=2), ACT.Copy), "vm", 2 * j + tp)

            def munit(u):
                h, q = munits[u]
                nk = (q + 1) * P
                act.wait_ge(S("decay_biased"), u + 1)
                act.activation(Eb[:, u % 2, 0:nk], Eb[:, u % 2, 0:nk], ACT.Exp, scale=-1.0, bias=nm[:, u:u + 1]).then_inc(S("decay_ready"), 1)
                act.activation(emn[:, u:u + 1], Bc[:, q, h:h + 1], ACT.Exp, scale=-1.0, bias=nm[:, u:u + 1]).then_inc(S("floor_ready"), 1)

            for t in range(len(munits) + 3):
                if t % 6 == 0 and t < 18:
                    high(s)
                    s += 1
                if t < len(munits):
                    munit(t)
                if t % 3 == 2 and t < 18:
                    i = t // 3
                    j, tp = divmod(i, 2)
                    b = wait_group(act, "c3", i)
                    free_group(act.activation(c3[:, 2 * tp:2 * tp + 2, j * PC:(j + 1) * PC], b[:, :].rearrange("p (t n) -> p t n", t=2), ACT.Copy), "c3", i)
            wait_freed(act, "c3", 5)
            for t in range(NT):
                own(act.activation(Eb[:, 0, 0:CQ], c3[:, t, 0:CQ], ACT.Square, accum_out=ssc[:, t:t + 1]))
                own(act.activation(Eb[:, 0, 0:CKV], c3[:, t, CQ:CQ + CKV], ACT.Square, accum_out=ssc[:, 4 + t:5 + t]))
            act.activation(ssc_done, mhalf, ACT.Copy).then_inc(S("ss_c"), 1)
            for f in range(KT):
                b = wait_group(act, "yT", f)
                act.activation(Yhv[:, f, :], b[:, :], ACT.Copy, scale=0.5).then_inc(S("yT_high"), 1)
            for j in range(4):
                high(s)
                s += 1
                for f in range(2):
                    i = 2 * j + f
                    b = wait_group(act, "gm", i)
                    if i >= 2:
                        wait_freed(act, "bm", i - 2)
                    free_group(act.activation(tg[:, f, :], b[:, :], ACT.Tanh, scale=0.5), "gm", i)
                high(s)
                s += 1
            for f in range(5):
                b = wait_group(act, "cT2", f)
                act.activation(Ch[:, f, :], b[:, :], ACT.Copy, scale=cols(par, PAR2, "g_cq")[:, f:f + 1] if f < 3 else cols(par, PAR2, "g_ckv")[:, f - 3:f - 2]).then_inc(S("cT2_high"), 1)
            for j in range(2):
                high(s)
                s += 1
                for h in range(4 * j, 4 * j + 4):
                    b = wait_group(act, "qn", h)
                    free_group(act.activation(qn[:, h, :], b[:, :], ACT.Copy), "qn", h)
            high(s)
            s += 1
            high(s)
            s += 1
            for h in range(AH):
                b = wait_group(act, "kn", h)
                free_group(act.activation(kn[:, h, :], b[:, :], ACT.Copy), "kn", h)
            high(s)
            s += 1
            for i in range(8):
                b = wait_group(act, "va", i)
                free_group(act.activation(va[:, i // 2, (i % 2) * 512:(i % 2 + 1) * 512], b[:, :], ACT.Copy), "va", i)

            def aunit(u):
                q, h = aunits[u]
                nk = (q + 1) * P
                act.wait_ge(S("score_biased"), A0 + u + 1)
                act.activation(SP3[:, u % 2, 0:nk], SP3[:, u % 2, 0:nk], ACT.Exp, scale=-1.0, bias=nmax2[:, u % 2:u % 2 + 1],
                               accum_out=rsum2[:, (q % 2) * 8 + h:(q % 2) * 8 + h + 1]).then_inc(S("probs_ready"), 1)

            for t in range(len(aunits) + 4):
                if t < len(aunits):
                    aunit(t)
                if t >= 11 and (t - 11) % 8 == 0:
                    q = (t - 11) // 8
                    for i in range(2):
                        b = wait_group(act, "yaT", 2 * q + i)
                        act.activation(Yhv[:, 4 * i:4 * i + 4, q * P:(q + 1) * P], b[:, :].rearrange("p (f n) -> p f n", f=4), ACT.Copy).then_inc(S("yaT_high"), 1)
            for j in range(4):
                high(s)
                s += 1
                for f in range(2):
                    i = 2 * j + f
                    b = wait_group(act, "ga", i)
                    if i >= 2:
                        wait_freed(act, "ba", i - 2)
                    free_group(act.activation(tga[:, f, :], b[:, :], ACT.Tanh, scale=0.5), "ga", i)
                high(s)
                s += 1
            for f in range(KT):
                act.wait_ge(S("merged_done"), f + 1)
                act.activation(Hhv[:, f, :], merged[:, f, :], ACT.Copy).then_inc(S("merged_high"), 1)
            for i in range(2):
                b = wait_group(act, "g1r", i)
                free_group(act.activation(g1row[:, i * 512:(i + 1) * 512], b[:, :], ACT.Copy, scale=0.5), "g1r", i)
            while s < len(sp_list):
                high(s)
                s += 1
            wait_freed(act, "wout", 7)
            for t in range(NT):
                ins = act.activation(hraw3[:, t, :], Xv[:, t, :], ACT.Square, accum_out=ss2[:, t:t + 1])
            ins.then_inc(S("ss_x"), 1)
            for i in range(2):
                b = wait_group(act, "g2r", i)
                free_group(act.activation(g2row[:, i * 512:(i + 1) * 512], b[:, :], ACT.Copy, scale=0.5), "g2r", i)
            for f in range(KT):
                b = wait_group(act, "h3", f)
                act.activation(Hhv[:, f, :], b[:, :], ACT.Identity, scale=aff2[:, f:f + 1], bias=modv[:, 3, f:f + 1]).then_inc(S("h3_high"), 1)
            act.wait_ge(S("group_shifted"), 1)
            act.activation(gex, gsh, ACT.Exp).then_inc(S("group_exp"), 1)
            act.wait_ge(S("second_ready"), 1)
            act.activation(e2, m2, ACT.Exp).then_inc(S("second_exp"), 1)
            act.wait_ge(S("bexp_ready"), 1)
            blocks = act.value_load(nblk_i[0:1, :], min_val=0, max_val=NBLK)
            with act.Fori(0, NBLK // WS) as i:
                for v in range(WS):
                    b, u = WS * i + v, v % 2
                    with act.If(b < blocks):
                        act.wait_ge(S(f"down_loaded{v}"), 16 * i + 16)
                        act.wait_ge(S("y_ready"), b + 3)
                        act.activation(wdh[:, u, :], wdn[v], ACT.Copy).then_inc(S("down_high"), 1)
                        act.wait_ge(S("gate_ready"), b + 1)
                        act.wait_ge(S("tanh_free"), b + 3)
                        act.activation(tanhg[:, u, :], GB[u][:, 0:128], ACT.Tanh, scale=0.5).then_inc(S("tanh_ready"), 1)
                        act.wait_ge(S("y_ready"), b + 5)
                        act.wait_ge(S(f"y_stored{u}"), 32 * i + 16 * (v // 2) + 16)
                        act.activation(yb[0:BS, u, 0:512], YB[0][0:BS, :], ACT.Copy)
                        act.activation(yb[0:BS, u, 512:1024], YB[1][0:BS, :], ACT.Copy).then_inc(S("y_copied"), 1)
                        act.wait_ge(S("y_copied"), b + 5)
                        act.dma_start(y_rows[bass.ds(b * BS, BS), :], yb[0:BS, u, :]).then_inc(S(f"y_stored{u}"), 16)
                    with act.Else():
                        act.sem_inc(S(f"y_stored{u}"), 16)
            for t in range(NT):
                act.wait_ge(S("x_final"), t + 1)
                act.activation(r12[:, t, 0, :], Xv[:, t, :], ACT.Square, accum_out=ssf[:, t:t + 1]).then_inc(S("ss_f"), 1)

        @block.vector
        def _(dve):
            c = [0]

            def own(ins):
                c[0] += 1
                ins.then_inc(S("dve_step"), 1)
                dve.wait_ge(S("dve_step"), c[0])

            def norm_rows(n, dst):
                dve.wait_ge(S("rstd_x"), n + 1)
                for t in range(NT):
                    dve.tensor_scalar(dst[:, t, :], Xv[:, t, :], rstd[:, t:t + 1], None, ALU.mult).then_inc(S("rows_normed"), 1)

            def transposed_low(what, n, dst, high, scale):
                for f in range(n):
                    b = wait_group(dve, what, f)
                    dve.wait_ge(S(what + "_high"), f + 1)
                    free_group(dve.scalar_tensor_tensor(dst[:, f, :], b[:, :], scale[:, f:f + 1], high[:, f, :].bitcast(F32),
                                                        ALU.mult, ALU.subtract), what, f)

            dve.wait_ge(S("con_loaded"), 16)
            dve.wait_ge(S("par_loaded"), 16)
            norm_rows(0, hraw)
            transposed_low("h0", KT, Hlv, Hhv, cols(par, PAR, "g_mix"))
            wait_freed(dve, "kcvc", 1)
            for u in range(2):
                ins = dve.tensor_copy(cdup[:, :, :, u, :], Zk[:, :, 0:256].rearrange("p t (c d) -> p t c d", c=4))
            ins.then_inc(S("cdup_ready"), 1)
            wait_freed(dve, "kwvw", 1)
            kview = Zk[:, :, 256:512]
            ksq = AR(14464, 1024).rearrange("p (t n) -> p t n", t=NT)
            own(dve.tensor_tensor(ksq, kview, kview, ALU.mult))
            dve.tensor_reduce(ssqk[:, 0:16].rearrange("p (c o) -> p c o", o=1), AR(14464, 1024).rearrange("p (c d) -> p c d", d=HD), AX.X, ALU.add).then_inc(S("ss_k"), 1)
            dve.wait_ge(S("ss_k"), 1)
            pe = cols(par, PAR, "pe").rearrange("p (c b a) -> p c b a", c=2, b=2)
            for c4 in range(4):
                b = wait_group(dve, "cT", c4)
                for half in range(2):
                    r = slice(64 * half, 64 * half + 64)
                    for a in range(2):
                        src = b[r, 16 * a:16 * a + 496].rearrange("p (i s) -> p s i", s=16)[:, half:16:2, :]
                        ins = dve.tensor_tensor(blkt[r, c4, a, :, :], src,
                                                pe[r, c4 // 2, a, :].unsqueeze(2).to_broadcast([64, 8, CMP_I]), ALU.add)
                free_group(ins, "cT", c4)
            dve.wait_ge(S("rstd_k"), 1)
            for u in range(2):
                ins = dve.tensor_tensor(kdup[:, :, :, u, :], kview.rearrange("p t (c d) -> p t c d", d=HD),
                                        rqk[:, 0:16].rearrange("p (t c) -> p t c", t=NT).unsqueeze(3).to_broadcast([P, NT, 4, HD]), ALU.mult)
            ins.then_inc(S("kdup_ready"), 1)
            dve.wait_ge(S("blk_high"), 1)
            for cc in range(2):
                ins = dve.tensor_tensor(Yl[:, 0:1984].rearrange("p (c k g i) -> p c k g i", c=2, k=16, g=2)[:, cc],
                                        AR(14464, 1984).rearrange("p (c g k i) -> p c k g i", c=2, g=2, k=16)[:, cc],
                                        Yh[:, 0:1984].bitcast(F32).rearrange("p (c k g i) -> p c k g i", c=2, k=16, g=2)[:, cc], ALU.subtract)
            ins.then_inc(S("blk_low"), 1)
            wait_freed(dve, ("q", 1), 1)
            dve.wait_ge(S("blk_low"), 1)
            own(dve.tensor_tensor(AR(14464, 2048), AR(5248, 2048), AR(5248, 2048), ALU.mult))
            dve.tensor_reduce(ssqk[:, 16:48].rearrange("p (c o) -> p c o", o=1), AR(14464, 2048).rearrange("p (c d) -> p c d", d=HD), AX.X, ALU.add).then_inc(S("ss_q"), 1)
            gk = cols(par, PAR, "g_k")
            for c4 in range(4):
                b = wait_group(dve, "kT", c4)
                free_group(dve.tensor_scalar(kT[:, c4, :], b[:, :], gk[:, 1 + c4 // 2:2 + c4 // 2], None, ALU.mult), "kT", c4)
            dve.wait_ge(S("rstd_q"), 1)
            dve.tensor_tensor(AR(5248, 2048).rearrange("p (c d) -> p c d", d=HD), AR(5248, 2048).rearrange("p (c d) -> p c d", d=HD),
                              rqk[:, 16:48].unsqueeze(2).to_broadcast([P, 32, HD]), ALU.mult).then_inc(S("q_normed"), 1)
            for i in range(4):
                b = wait_group(dve, "cmp1", i)
                h = cw[:, i * 62:(i + 1) * 62]
                u = cw[:, 256 + i * 62:256 + (i + 1) * 62]
                ins = dve.tensor_scalar(h, b[:, 0:62], cols(par, PAR, "b_cmp1")[:, i:i + 1], None, ALU.add)
                free_group(ins, "cmp1", i)
                wait_freed(dve, "cmp1", i)
                own(dve.tensor_tensor(u, h, h, ALU.mult))
                own(dve.tensor_scalar(u, u, 0.044715, 1.0, ALU.mult, ALU.add))
                dve.tensor_tensor(u, u, h, ALU.mult).then_inc(S("gelu_in"), 1)
                dve.wait_ge(S("gelu_tanh"), i + 1)
                own(dve.scalar_tensor_tensor(h, cw[:, 512 + i * 62:512 + (i + 1) * 62], 1.0, h, ALU.add, ALU.mult))
                dve.tensor_scalar(h, h, 0.5, None, ALU.mult).then_inc(S("gelu_done"), 1)
            b2k = cols(par, PAR, "b_cmp2").rearrange("p (c d) -> p c d", c=2)
            kcr = cw[0:32, 1280:1408].rearrange("p (g d) -> p g d", g=2)
            ksqr = cw[0:32, 1408:1536]
            kcd = cw[0:32, 1536:1792].rearrange("p (g u d) -> p g u d", g=2, u=2)
            kcT = cw[:, 1792:1856].rearrange("p (g i) -> p g i", g=2)
            VBD = PTs[:, 0, :].rearrange("p (g n) -> p g n", g=2)
            own(dve.memset(PTs[:, 0, :], 0.0))
            own(dve.memset(cw[:, 1280:1856], 0.0))
            b = wait_group(dve, "cmpk", 0)
            ins = dve.tensor_tensor(kcr[0:31], b[0:31, 0:128].rearrange("p (g d) -> p g d", g=2),
                                    b2k[0:31, 0:1, :].to_broadcast([31, 2, HD]), ALU.add)
            free_group(ins, "cmpk", 0)
            wait_freed(dve, "cmpk", 0)
            own(dve.tensor_tensor(ksqr.rearrange("p (g d) -> p g d", g=2), kcr, kcr, ALU.mult))
            dve.tensor_reduce(ssk[0:32, :].unsqueeze(2), ksqr.rearrange("p (g d) -> p g d", g=2), AX.X, ALU.add).then_inc(S("ss_kc"), 1)
            b = wait_group(dve, "cmpv", 0)
            for r in range(4):
                ins = dve.tensor_tensor(VBD[32 * r:32 * r + 31, :, r * HD:(r + 1) * HD],
                                        b[32 * r:32 * r + 31, :].rearrange("p (g n) -> p g n", g=2)[:, :, r * HD:(r + 1) * HD],
                                        b2k[32 * r:32 * r + 31, 1:2, :].to_broadcast([31, 2, HD]), ALU.add)
            free_group(ins, "cmpv", 0)
            dve.wait_ge(S("rstd_kc"), 1)
            for u in range(2):
                ins = dve.tensor_tensor(kcd[:, :, u, :], kcr, rsk[0:32, :].unsqueeze(2).to_broadcast([32, 2, HD]), ALU.mult)
            ins.then_inc(S("kcd_ready"), 1)
            b = wait_group(dve, "cmpkT", 0)
            free_group(dve.tensor_scalar(kcT[:, :, :], b[:, 0:64].rearrange("p (g i) -> p g i", g=2), gk[:, 0:1], None, ALU.mult), "cmpkT", 0)
            for c4 in range(4):
                b = wait_group(dve, "qT", c4)
                free_group(dve.tensor_scalar(qT[:, c4, :], b[:, :], cols(par, PAR, "g_q"), 0.125, ALU.mult, ALU.mult), "qT", c4)
            dve.wait_ge(S("bias_loaded"), 16)
            for q in range(NT):
                sv = cw[:, 768:1024].rearrange("p (h i) -> p h i", h=8)
                pv = cw[:, 1024:1280].rearrange("p (h i) -> p h i", h=8)
                if q:
                    dve.wait_ge(S("cmp_exp"), q)
                for o in range(2):
                    b = wait_group(dve, "cS", 2 * q + o)
                    ins = dve.tensor_tensor(sv[:, o:8:2, :], b[:, 0:128].rearrange("p (h i) -> p h i", h=4), cmpb[:, q, o:8:2, :], ALU.add)
                    free_group(ins, "cS", 2 * q + o)
                wait_freed(dve, "cS", 2 * q + 1)
                own(dve.tensor_reduce(cmaxn.unsqueeze(2), sv, AX.X, ALU.max))
                dve.tensor_tensor(sv, sv, cmaxn.unsqueeze(2).to_broadcast([P, 8, 32]), ALU.subtract).then_inc(S("cmp_shifted"), 1)
                dve.wait_ge(S("cmp_exp"), q + 1)
                if q:
                    wait_freed(dve, "cP", q - 1)
                dve.tensor_tensor(pv, pv, cmpm[:, q:q + 1, :].to_broadcast([P, 8, 32]), ALU.mult).then_inc(S("cmp_p"), 1)
                dve.wait_ge(S("cmp_p"), q + 1)
                own(dve.tensor_reduce(csum.unsqueeze(2), pv, AX.X, ALU.add))
                own(dve.tensor_scalar(csum, csum, 1e-30, None, ALU.max))
                own(dve.reciprocal(csum, csum))
                own(dve.tensor_tensor(ccoef, csum, gates[:, q, 0:24:3], ALU.mult))
                b = wait_group(dve, "cP", q)
                free_group(dve.tensor_copy(SP[:, 0, 0:256], b[:, 0:256]), "cP", q)
                b = wait_group(dve, "cO", q)
                ins = dve.tensor_tensor(Oat[:, q, :].rearrange("p (h d) -> p h d", h=8), b[:, :].rearrange("p (h d) -> p h d", h=8),
                                        ccoef.unsqueeze(2).to_broadcast([P, 8, HD]), ALU.mult)
                free_group(ins, "cO", q)
            wait_freed(dve, "cO", NT - 1)

            def biased(u):
                ty, q, h = units[u]
                nk = (q + 1) * P
                dve.wait_ge(S("scores_ready"), u + 1)
                if u >= 2:
                    dve.wait_ge(S("probs_transposed"), u - 1)
                dve.tensor_tensor_reduce(SP[:, u % 2, 0:nk], SA[u % 2][:, 0:nk], alibi[:, h, T - nk:T], -1.0, 3e38,
                                         ALU.add, ALU.min, nmax[:, u % 2:u % 2 + 1]).then_inc(S("score_biased"), 1)

            def copied(u):
                ty, q, h = units[u]
                nk = (q + 1) * P
                dve.wait_ge(S("probs_transposed"), u + 1)
                if u >= 2:
                    dve.wait_ge(S("values_summed"), u - 1)
                dve.tensor_copy(PTs[:, u % 2, 0:nk], PB[u % 2][:, 0:nk]).then_inc(S("pt_copied"), 1)

            def weighted(v):
                ty, q = divmod(v, NT)
                dve.wait_ge(S("values_summed"), 8 * v + 8)
                own(dve.reciprocal(ncoef, rsum[:, (v % 2) * 8:(v % 2) * 8 + 8]))
                own(dve.tensor_tensor(ncoef, ncoef, gates[:, q, 1 + ty:24:3], ALU.mult))
                ins = dve.tensor_tensor(otmp.rearrange("p (h d) -> p h d", h=8), OB[:, :].rearrange("p (h d) -> p h d", h=8),
                                        ncoef.unsqueeze(2).to_broadcast([P, 8, HD]), ALU.mult)
                ins.then_inc(S("out_freed"), 1)
                dve.wait_ge(S("out_freed"), v + 1)
                dve.tensor_tensor(Oat[:, q, :], Oat[:, q, :], otmp, ALU.add).then_inc(S("attn_sum"), 1)

            def conv_group(g):
                i, k = divmod(g, 6)
                f = 2 * i + k % 2
                cwt = cols(par, PAR, "conv_w").rearrange("p (f k) -> p f k", k=3)
                if k < 2:
                    return
                if k < 4:
                    b = wait_group(dve, "cg", f)
                    wait_freed(dve, "hc", f)
                    free_group(dve.tensor_tensor(ctmp_u, b[:, :], ctmp_h[:, f % 2, :], ALU.mult), "cg", f)
                    wait_freed(dve, "cg", f)
                    own(dve.tensor_scalar(conv[:, f, :], ctmp_u, cwt[:, f, 2:3], None, ALU.mult))
                    own(dve.scalar_tensor_tensor(conv[:, f, 1:T], ctmp_u[:, 0:T - 1], cwt[:, f, 1:2], conv[:, f, 1:T], ALU.mult, ALU.add))
                    own(dve.scalar_tensor_tensor(conv[:, f, 2:T], ctmp_u[:, 0:T - 2], cwt[:, f, 0:1], conv[:, f, 2:T], ALU.mult, ALU.add))
                else:
                    b = wait_group(dve, "bg", f)
                    ins = dve.tensor_tensor(conv[:, f, :], conv[:, f, :], b[:, :], ALU.mult)
                    free_group(ins, "bg", f)

            for t in range(len(units) + 3):
                if t < len(units):
                    biased(t)
                if 0 <= t - 1 < len(units):
                    copied(t - 1)
                if t % 4 == 3 and t < 48:
                    conv_group(t // 4)
                if t >= 10 and (t - 2) % 8 == 0 and (t - 2) // 8 - 1 < 8:
                    weighted((t - 2) // 8 - 1)

            go = cols(par, PAR, "g_out")
            for f in range(4):
                dve.wait_ge(S("conv_high"), f + 1)
                dve.scalar_tensor_tensor(Ylv[:, 4 + f, :], conv[:, f, :], go[:, 4 + f:5 + f], Yhv[:, 4 + f, :].bitcast(F32),
                                         ALU.mult, ALU.subtract).then_inc(S("conv_low"), 1)
            b = wait_group(dve, "csq", 0)
            free_group(dve.tensor_copy(ssqk[:, 4:8], b[:, 0:4]), "csq", 0)
            dve.wait_ge(S("rstd_attn"), 1)
            for t in range(NT):
                dve.tensor_scalar(kT[:, t, :], Oat[:, t, :], rqk[:, t:t + 1], None, ALU.mult).then_inc(S("attn_normed"), 1)
            transposed_low("aT", 4, Ylv, Yhv, go)
            dve.wait_ge(S("rstd_conv"), 1)
            for n in range(4):
                for tp in range(2):
                    i = 4 * n + 2 * tp
                    xs = Xv[:, 2 * tp:2 * tp + 2, n * PC:(n + 1) * PC]
                    b = wait_group(dve, "wo", i)
                    ins = dve.tensor_tensor(xs, xs, b[:, :].rearrange("p (t n) -> p t n", t=2), ALU.add)
                    free_group(ins, "wo", i)
                    wait_freed(dve, "wo", i)
                    b = wait_group(dve, "wo", i + 1)
                    for j in range(2):
                        xt = Xv[:, 2 * tp + j, n * PC:(n + 1) * PC]
                        ins = dve.scalar_tensor_tensor(xt, b[:, j * PC:(j + 1) * PC], rqk[:, 4 + 2 * tp + j:5 + 2 * tp + j], xt, ALU.mult, ALU.add)
                    free_group(ins, "wo", i + 1)
            norm_rows(1, hraw)
            transposed_low("h1", KT, Hlv, Hhv, cols(par, PAR, "g_ffn"))
            m = 0

            def mod_cols(m):
                b = wait_group(dve, "mod", m)
                ins = dve.tensor_tensor(modc[:, 2 * m:2 * m + 2], b[:, 0:2],
                                        cols(par, PAR, "mod_b")[:, 2 * m:2 * m + 2], ALU.add)
                free_group(ins, "mod", m)

            dve.wait_ge(S("cond_tanh"), 1)
            own(dve.scalar_tensor_tensor(cond_t, cond_t, 1.0, cols(par, PAR, "c"), ALU.add, ALU.mult))
            own(dve.tensor_scalar(condc, cond_t, 0.5, None, ALU.mult))

            def mod_part(m):
                w = wait_raw(dve, ("mod", m)).rearrange("p (k n) -> p k n", n=PC)
                if m >= 2:
                    wait_freed(dve, "mod", m - 2)
                a = macc[:, m % 2, :]
                own(dve.tensor_scalar(a, w[:, 0, :], condc[:, 0:1], None, ALU.mult))
                for k in range(1, KT - 1):
                    own(dve.scalar_tensor_tensor(a, w[:, k, :], condc[:, k:k + 1], a, ALU.mult, ALU.add))
                dve.scalar_tensor_tensor(a, w[:, KT - 1, :], condc[:, KT - 1:KT], a, ALU.mult, ALU.add).then_inc(S("mod_summed"), 1)

            for r in range(FQ):
                for j in range(4):
                    if m < MODN:
                        mod_part(m)
                    for f in range(2):
                        i = (r * 4 + j) * 2 + f
                        wait_freed(dve, "up", i)
                        own(dve.tensor_tensor(fsq[:, i % 2, :], frelu[:, i % 2, :], frelu[:, i % 2, :], ALU.mult))
                        dve.wait_ge(S("ffn_high"), i + 1)
                        dve.tensor_tensor(Ylv[:, 2 * j + f, :], fsq[:, i % 2, :], Yhv[:, 2 * j + f, :].bitcast(F32), ALU.subtract).then_inc(S("ffn_sq"), 1)
                    if m < MODN:
                        mod_cols(m)
                        m += 1
                for j in range(4):
                    if m < MODN:
                        mod_part(m)
                    for tp in range(2):
                        i = (r * 4 + j) * 2 + tp
                        xs = Xv[:, 2 * tp:2 * tp + 2, j * PC:(j + 1) * PC]
                        b = wait_group(dve, "down", i)
                        ins = dve.tensor_tensor(xs, xs, b[:, :].rearrange("p (t n) -> p t n", t=2), ALU.add)
                        free_group(ins, "down", i)
                    if m < MODN:
                        mod_cols(m)
                        m += 1

            dve.wait_ge(S("par2_loaded"), 16)
            wait_freed(dve, "mod", MOD_PIECES - 1)
            own(dve.scalar_tensor_tensor(aff1, modv[:, 1, :], 1.0, cols(par, PAR2, "g_1"), ALU.add, ALU.mult))
            dve.scalar_tensor_tensor(aff2, modv[:, 4, :], 1.0, cols(par, PAR2, "g_2"), ALU.add, ALU.mult).then_inc(S("aff_ready"), 1)
            dve.wait_ge(S("aff_ready"), 1)
            dve.wait_ge(S("rstd_x"), 3)
            for t in range(NT):
                dve.tensor_scalar(hraw2[:, t, :], Xv[:, t, :], rstd2[:, t:t + 1], None, ALU.mult).then_inc(S("rows_normed"), 1)
            own(dve.memset(xpad, 0.0))
            ftmp = AR(17536, 1024).rearrange("p (r n) -> p r n", r=2)
            for f in range(KT):
                b = wait_group(dve, "h2", f)
                dve.wait_ge(S("h2_high"), f + 1)
                own(dve.tensor_scalar(ftmp[:, f % 2, :], b[:, :], aff1[:, f:f + 1], modv[:, 0, f:f + 1], ALU.mult, ALU.add))
                free_group(dve.tensor_tensor(Hlv[:, f, :], ftmp[:, f % 2, :], Hhv[:, f, :].bitcast(F32), ALU.subtract), "h2", f)
            b = wait_group(dve, "if", 0)
            free_group(dve.tensor_tensor(ifr, b[:, 0:32].rearrange("p (t n) -> p t n", t=NT),
                                         cols(par, PAR2, "b_if").unsqueeze(1).to_broadcast([P, NT, 8]), ALU.add), "if", 0)
            wait_freed(dve, "if", 0)
            dve.scalar_tensor_tensor(fabs, ifr[:, :, 4:8], -1.0, ifr[:, :, 4:8], ALU.mult, ALU.max).then_inc(S("fabs_ready"), 1)
            own(dve.tensor_scalar(lf, ifr[:, :, 4:8], 0.0, None, ALU.min))
            dve.wait_ge(S("flog_ready"), 1)
            dve.tensor_tensor(lf, lf, flog, ALU.subtract).then_inc(S("lf_ready"), 1)
            dve.memset(small_pad, 0.0).then_inc(S("xpad_zeroed"), 1)
            w4 = cols(par, PAR2, "conv_w2").rearrange("p (f k) -> p f k", k=4)
            b4 = cols(par, PAR2, "conv_b2")

            def silu_of(i):
                dve.wait_ge(S("conv2_tanh"), i + 1)
                dve.scalar_tensor_tensor(qkT[:, i, :], cth[:, i % 2, :], 1.0, cacc[:, i % 2, :], ALU.add, ALU.mult).then_inc(S("qk_done"), 1)

            for i in range(8):
                wait_freed(dve, "qk", i)
                xp, ac = xpad[:, i % 2, :], cacc[:, i % 2, :]
                if i >= 2:
                    dve.wait_ge(S("qk_done"), i - 1)
                own(dve.tensor_scalar(ac, xp[:, 3:515], w4[:, i, 3:4], b4[:, i:i + 1], ALU.mult, ALU.add))
                own(dve.scalar_tensor_tensor(ac, xp[:, 2:514], w4[:, i, 2:3], ac, ALU.mult, ALU.add))
                own(dve.scalar_tensor_tensor(ac, xp[:, 1:513], w4[:, i, 1:2], ac, ALU.mult, ALU.add))
                dve.scalar_tensor_tensor(ac, xp[:, 0:512], w4[:, i, 0:1], ac, ALU.mult, ALU.add).then_inc(S("conv2_done"), 1)
                if i:
                    silu_of(i - 1)
            silu_of(7)
            for j in range(4):
                wait_freed(dve, "om", 2 * j + 1)
                dve.tensor_scalar(To[:, :, j * PC:(j + 1) * PC], To[:, :, j * PC:(j + 1) * PC], 1.0, None, ALU.add).then_inc(S("ogate_done"), 1)
            b = wait_group(dve, "cum", 0)
            free_group(dve.tensor_copy(Bc, b[:, 0:16].rearrange("p (t n) -> p t n", t=NT)), "cum", 0)
            wait_freed(dve, "cum", 0)
            dve.tensor_tensor(cc_, ifr[:, :, 0:4], Bc, ALU.subtract).then_inc(S("c_ready"), 1)
            for h in range(MH):
                b = wait_group(dve, "crow", h)
                free_group(dve.tensor_copy(crow[:, h, :], b[:, :]), "crow", h)
            wait_freed(dve, "crow", MH - 1)
            dve.wait_ge(S("causal_loaded"), 16)
            dve.wait_ge(S("ogate_done"), 4)
            dve.wait_ge(S("qk_done"), 8)

            def mdecay(u):
                h, q = munits[u]
                nk = (q + 1) * P
                own(dve.tensor_tensor_reduce(Eb[:, u % 2, 0:nk], crow[:, h, 0:nk], causal[:, T - nk:T], -1.0, 3e38,
                                             ALU.add, ALU.min, nm[:, u:u + 1]))
                dve.tensor_scalar(nm[:, u:u + 1], nm[:, u:u + 1], 0.0, None, ALU.min).then_inc(S("decay_biased"), 1)

            def mscore(u):
                h, q = munits[u]
                nk = (q + 1) * P
                dve.wait_ge(S("scores_ready"), M0 + u + 1)
                dve.wait_ge(S("decay_ready"), u + 1)
                if u >= 2:
                    dve.wait_ge(S("probs_transposed"), M0 + u - 1)
                dve.tensor_tensor_reduce(SP2[:, u % 2, 0:nk], SA[u % 2][:, 0:nk], Eb[:, u % 2, 0:nk], MSCALE, 0.0,
                                         ALU.mult, ALU.add, den[:, u:u + 1]).then_inc(S("score_biased"), 1)
                dve.wait_ge(S("score_biased"), M0 + u + 1)
                own(dve.scalar_tensor_tensor(rr[:, u:u + 1], den[:, u:u + 1], -1.0, den[:, u:u + 1], ALU.mult, ALU.max))
                dve.wait_ge(S("floor_ready"), u + 1)
                own(dve.tensor_tensor(rr[:, u:u + 1], rr[:, u:u + 1], emn[:, u:u + 1], ALU.max))
                own(dve.reciprocal(rr[:, u:u + 1], rr[:, u:u + 1]))

            def mcopied(u):
                h, q = munits[u]
                nk = (q + 1) * P
                dve.wait_ge(S("probs_transposed"), M0 + u + 1)
                if u >= 2:
                    dve.wait_ge(S("values_summed"), M0 + u - 1)
                dve.tensor_copy(PT2[:, u % 2, 0:nk], PB[u % 2][:, 0:nk]).then_inc(S("pt_copied"), 1)

            def mout(u):
                h, q = munits[u]
                dve.wait_ge(S("values_summed"), M0 + u + 1)
                yt = To[:, q, h * MV:(h + 1) * MV]
                dve.scalar_tensor_tensor(yt, OB[:, 0:MV], rr[:, u:u + 1], yt, ALU.mult, ALU.mult).then_inc(S("m_out"), 1)

            mdecay(0)
            for t in range(len(munits) + 3):
                if 0 <= t - 3 < len(munits):
                    mout(t - 3)
                if t + 1 < len(munits):
                    mdecay(t + 1)
                if t < len(munits):
                    mscore(t)
                if 0 <= t - 1 < len(munits):
                    mcopied(t - 1)
            for f in range(KT):
                b = wait_group(dve, "yT", f)
                dve.wait_ge(S("yT_high"), f + 1)
                free_group(dve.scalar_tensor_tensor(Ylv[:, f, :], b[:, :], 0.5, Yhv[:, f, :].bitcast(F32), ALU.mult, ALU.subtract), "yT", f)
            dve.wait_ge(S("rstd_c"), 1)
            for t in range(NT):
                dve.tensor_scalar(c3[:, t, 0:CQ], c3[:, t, 0:CQ], rsc[:, t:t + 1], None, ALU.mult)
                ins = dve.tensor_scalar(c3[:, t, CQ:CQ + CKV], c3[:, t, CQ:CQ + CKV], rsc[:, 4 + t:5 + t], None, ALU.mult)
            ins.then_inc(S("kr_normed"), 1)
            for i in range(8):
                b = wait_group(dve, "bm", i)
                wait_freed(dve, "gm", i)
                free_group(dve.scalar_tensor_tensor(merged[:, i, :], tg[:, i % 2, :], 1.0, b[:, :], ALU.add, ALU.mult), "bm", i)
            for f in range(5):
                b = wait_group(dve, "cT2", f)
                dve.wait_ge(S("cT2_high"), f + 1)
                sc = cols(par, PAR2, "g_cq")[:, f:f + 1] if f < 3 else cols(par, PAR2, "g_ckv")[:, f - 3:f - 2]
                free_group(dve.scalar_tensor_tensor(Cl[:, f, :], b[:, :], sc, Ch[:, f, :].bitcast(F32), ALU.mult, ALU.subtract), "cT2", f)
            dve.wait_ge(S("cos_loaded"), 16)

            def rope(dst1, dst2, x1, x2, cs, sn, t1, t2):
                own(dve.tensor_tensor(t1, x1, cs, ALU.mult))
                own(dve.tensor_tensor(t2, x2, sn, ALU.mult))
                own(dve.tensor_tensor(dst1, t1, t2, ALU.subtract))
                own(dve.tensor_tensor(t1, x1, sn, ALU.mult))
                own(dve.tensor_tensor(t2, x2, cs, ALU.mult))
                return dve.tensor_tensor(dst2, t1, t2, ALU.add)

            tk = ropet.rearrange("p (r t n) -> p r t n", r=2, t=NT)
            kx = c3[:, :, CQ + CKV:CQ + CKV + 64]
            own(rope(kr2[:, :, 0, 0:32], kr2[:, :, 0, 32:64], kx[:, :, 0:32], kx[:, :, 32:64], cosT, sinT, tk[:, 0], tk[:, 1]))
            dve.tensor_copy(kr2[:, :, 1, :], kr2[:, :, 0, :]).then_inc(S("kr_turned"), 1)
            b = wait_group(dve, "krT", 0)
            free_group(dve.tensor_copy(krT, b[:, :]), "krT", 0)
            rt = ya.rearrange("p (r h n) -> p r h n", r=4, h=8)
            for t in range(NT):
                b = wait_group(dve, "qr", t)
                bx = b[:, :].rearrange("p (h n) -> p h n", h=8)
                dst = qrr[:, t, :].rearrange("p (h n) -> p h n", h=8)
                cs = cosT[:, t:t + 1, :].to_broadcast([P, 8, 32])
                sn = sinT[:, t:t + 1, :].to_broadcast([P, 8, 32])
                if t:
                    wait_freed(dve, "qr", t - 1)
                ins = rope(dst[:, :, 0:32], dst[:, :, 32:64], bx[:, :, 0:32], bx[:, :, 32:64], cs, sn, rt[:, 0], rt[:, 1])
                free_group(ins, "qr", t)
            for t in range(NT):
                b = wait_group(dve, "qrT", t)
                free_group(dve.tensor_copy(qrT[:, :, t * P:(t + 1) * P], b[:, :].rearrange("p (c n) -> p c n", c=4)), "qrT", t)
            dve.wait_ge(S("chunk_loaded"), 16)

            def abiased(u):
                q, h = aunits[u]
                nk = (q + 1) * P
                dve.wait_ge(S("scores_ready"), A0 + u + 1)
                if u >= 2:
                    dve.wait_ge(S("probs_transposed"), A0 + u - 1)
                dve.tensor_tensor_reduce(SP3[:, u % 2, 0:nk], SA[u % 2][:, 0:nk], chunk[:, T - nk:T], -ASCALE, 3e38,
                                         ALU.add, ALU.min, nmax2[:, u % 2:u % 2 + 1]).then_inc(S("score_biased"), 1)

            def acopied(u):
                q, h = aunits[u]
                nk = (q + 1) * P
                dve.wait_ge(S("probs_transposed"), A0 + u + 1)
                if u >= 2:
                    dve.wait_ge(S("values_summed"), A0 + u - 1)
                dve.tensor_copy(PT3[:, u % 2, 0:nk], PB[u % 2][:, 0:nk]).then_inc(S("pt_copied"), 1)

            def aout(u):
                q, h = aunits[u]
                j = (q % 2) * 8 + h
                dve.wait_ge(S("values_summed"), A0 + u + 1)
                own(dve.reciprocal(rinv[:, j:j + 1], rsum2[:, j:j + 1]))
                if h == 0 and q:
                    wait_group(dve, "yaT", 2 * q - 1)
                dve.tensor_scalar(ya[:, h * P:(h + 1) * P], OB[:, 0:P], rinv[:, j:j + 1], None, ALU.mult).then_inc(S("a_out"), 1)

            for t in range(len(aunits) + 4):
                if 0 <= t - 3 < len(aunits):
                    aout(t - 3)
                if t < len(aunits):
                    abiased(t)
                if 0 <= t - 1 < len(aunits):
                    acopied(t - 1)
                if t >= 11 and (t - 11) % 8 == 0:
                    q = (t - 11) // 8
                    for i in range(2):
                        b = wait_group(dve, "yaT", 2 * q + i)
                        dve.wait_ge(S("yaT_high"), 2 * q + i + 1)
                        free_group(dve.tensor_tensor(Ylv[:, 4 * i:4 * i + 4, q * P:(q + 1) * P], b[:, :].rearrange("p (f n) -> p f n", f=4),
                                                     Yhv[:, 4 * i:4 * i + 4, q * P:(q + 1) * P].bitcast(F32), ALU.subtract), "yaT", 2 * q + i)
            for i in range(8):
                b = wait_group(dve, "ba", i)
                wait_freed(dve, "ga", i)
                free_group(dve.scalar_tensor_tensor(tba[:, i % 2, :], tga[:, i % 2, :], 1.0, b[:, :], ALU.add, ALU.mult), "ba", i)
                wait_freed(dve, "ba", i)
                dve.tensor_tensor(merged[:, i, :], merged[:, i, :], tba[:, i % 2, :], ALU.add).then_inc(S("merged_done"), 1)
            for f in range(KT):
                dve.wait_ge(S("merged_high"), f + 1)
                dve.tensor_tensor(Hlv[:, f, :], merged[:, f, :], Hhv[:, f, :].bitcast(F32), ALU.subtract).then_inc(S("merged_low"), 1)
            wait_freed(dve, "g1r", 1)
            dve.wait_ge(S("x_back"), 16)
            for j in range(4):
                for tp in range(2):
                    i = 2 * j + tp
                    b = wait_group(dve, "wout", i)
                    w = wtmp[:, i % 2, :].rearrange("p (t n) -> p t n", t=2)
                    own(dve.tensor_tensor(w, b[:, :].rearrange("p (t n) -> p t n", t=2),
                                          g1row[:, j * PC:(j + 1) * PC].unsqueeze(1).to_broadcast([P, 2, PC]), ALU.mult))
                    xs = Xv[:, 2 * tp:2 * tp + 2, j * PC:(j + 1) * PC]
                    free_group(dve.tensor_tensor(xs, xs, w, ALU.add), "wout", i)

            dve.wait_ge(S("rstd_x"), 4)
            for t in range(NT):
                dve.tensor_scalar(hraw3[:, t, :], Xv[:, t, :], rstd2[:, t:t + 1], None, ALU.mult).then_inc(S("rows_normed"), 1)
            dve.wait_ge(S("tab3_loaded"), 16)
            dve.memset(zer, 0.0).then_inc(S("zeros_ready"), 1)
            ftmp3 = xgT.rearrange("p u k n -> p u (k n)")
            for f in range(KT):
                b = wait_group(dve, "h3", f)
                dve.wait_ge(S("h3_high"), f + 1)
                own(dve.tensor_scalar(ftmp3[:, f % 2, :], b[:, :], aff2[:, f:f + 1], modv[:, 3, f:f + 1], ALU.mult, ALU.add))
                free_group(dve.tensor_tensor(Hlv[:, f, :], ftmp3[:, f % 2, :], Hhv[:, f, :].bitcast(F32), ALU.subtract), "h3", f)

            def bc(a, n):
                return a.unsqueeze(2).to_broadcast([P, NT, n])

            dec = cols(tab3, TAB3, "dec")

            def first_of(dst, key, x, n):
                own(dve.tensor_scalar(key, x, 0.0, None, ALU.is_ge))
                own(dve.tensor_tensor(key, key, dec[:, 32 - n:32].unsqueeze(1).to_broadcast([P, NT, n]), ALU.mult))
                own(dve.tensor_reduce(km.unsqueeze(2), key, AX.X, ALU.max))
                own(dve.tensor_tensor(dst, key, bc(km, n), ALU.is_equal))

            b = wait_group(dve, "gr", 0)
            free_group(dve.tensor_tensor(Lg, b[:, 0:144].rearrange("p (t n) -> p t n", t=NT),
                                         cols(par, PAR2, "b_gr").unsqueeze(1).to_broadcast([P, NT, 36]), ALU.add), "gr", 0)
            wait_freed(dve, "gr", 0)
            own(dve.tensor_reduce(gmx.unsqueeze(2), Lg[:, :, 0:4], AX.X, ALU.max))
            dve.tensor_tensor(gsh, Lg[:, :, 0:4], bc(gmx, 4), ALU.subtract).then_inc(S("group_shifted"), 1)
            dve.wait_ge(S("group_shifted"), 1)
            first_of(oh_g, okey, gsh, 4)
            own(dve.tensor_tensor(ing4.rearrange("p (t e g) -> p t e g", t=NT, e=EG), Lg[:, :, 4:36].rearrange("p t (g e) -> p t e g", g=NEG_),
                                  oh_g.unsqueeze(2).to_broadcast([P, NT, EG, NEG_]), ALU.mult))
            own(dve.tensor_reduce(insh.rearrange("p t e -> p (t e)").unsqueeze(2), ing4.rearrange("p (a g) -> p a g", g=NEG_), AX.X, ALU.add))
            own(dve.tensor_reduce(m1.unsqueeze(2), insh, AX.X, ALU.max))
            own(dve.tensor_tensor(insh, insh, bc(m1, EG), ALU.subtract))
            first_of(oh1, key8, insh, EG)
            own(dve.scalar_tensor_tensor(d2, oh1, NEG, insh, ALU.mult, ALU.add))
            dve.tensor_reduce(m2.unsqueeze(2), d2, AX.X, ALU.max).then_inc(S("second_ready"), 1)
            dve.wait_ge(S("second_ready"), 1)
            own(dve.tensor_tensor(d2, d2, bc(m2, EG), ALU.subtract))
            first_of(oh2, key8, d2, EG)
            for A, oh in ((A1, oh1), (A2, oh2)):
                own(dve.tensor_tensor(A.rearrange("p t (g e) -> p t g e", g=NEG_), bc4(oh_g), oh.unsqueeze(2).to_broadcast([P, NT, NEG_, EG]), ALU.mult))
            own(dve.tensor_tensor(triex[0:32, :], cols(con, CON, "tri")[0:32, 0:32], ident[0:32, 0:32], ALU.subtract))
            dve.tensor_tensor(Aa, A1, A2, ALU.add).then_inc(S("assigned"), 1)
            dve.wait_ge(S("assigned"), 1)
            dve.wait_ge(S("group_exp"), 1)
            own(dve.tensor_reduce(gsum.unsqueeze(2), gex, AX.X, ALU.add))
            own(dve.reciprocal(pg, gsum))
            dve.wait_ge(S("second_exp"), 1)
            own(dve.tensor_scalar(gsum, e2, 1.0, None, ALU.add))
            own(dve.reciprocal(gsum, gsum))
            own(dve.tensor_tensor(w1c, pg, gsum, ALU.mult))
            own(dve.tensor_tensor(w2c, w1c, e2, ALU.mult))
            b = wait_group(dve, "cnt", 0)
            free_group(dve.tensor_copy(cntc[0:32, :], b[0:32, 0:1]), "cnt", 0)
            wait_freed(dve, "cnt", 0)
            own(dve.tensor_scalar(nb8[0:32, :], cols(tab3, TAB3, "thr")[0:32, :], cntc[0:32, :], None, ALU.is_le))
            dve.tensor_reduce(nbc[0:32, :], nb8[0:32, :], AX.X, ALU.add).then_inc(S("nb_ready"), 1)
            b = wait_group(dve, "rank", 0)
            free_group(dve.tensor_tensor(Sl, b[:, 0:128].rearrange("p (t n) -> p t n", t=NT), Aa, ALU.subtract), "rank", 0)
            b = wait_group(dve, "pstart", 0)
            own(dve.tensor_scalar(ps64, b[:, 0:32], float(BS), None, ALU.mult))
            own(dve.tensor_copy(nblkf, b[:, 33:34]))
            free_group(dve.tensor_copy(pend[0:32, :], b[0:32, 32:33]), "pstart", 0)
            wait_freed(dve, "pstart", 0)
            dve.tensor_scalar(cmpe[0:32, :], cols(tab3, TAB3, "iota")[0:32, :], pend[0:32, :], None, ALU.is_ge).then_inc(S("ended_ready"), 1)
            own(dve.tensor_tensor(Sl, Sl, ps64.unsqueeze(1).to_broadcast([P, NT, 32]), ALU.add))
            for A, dst, k in ((A1, dst1, 0), (A2, dst2, 1)):
                own(dve.tensor_tensor(Tmp, A, Sl, ALU.mult))
                own(dve.tensor_reduce(dst.unsqueeze(2), Tmp, AX.X, ALU.add))
                own(dve.tensor_copy(dst_i[:, 4 * k:4 * k + 4], dst))
            dve.memset(small_pad, 0.0).then_inc(S("dst_ready"), 1)
            b = wait_group(dve, "bexp", 0)
            free_group(dve.tensor_scalar(bexpf, b[:, 0:NBLK], float(NE - 1), None, ALU.min), "bexp", 0)
            wait_freed(dve, "bexp", 0)
            own(dve.tensor_copy(nblk_i, nblkf))
            dve.tensor_copy(bexp_i[:, :], bexpf).then_inc(S("bexp_ready"), 1)
            b = wait_group(dve, "slotT", 0)
            free_group(dve.tensor_copy(slot_i[0:BS, 0:NBLK], b[0:BS, 0:NBLK]), "slotT", 0)
            wait_freed(dve, "slotT", 0)
            dve.tensor_copy(slot_i[:, NBLK:NBLK + 2], zer[:, 0:2]).then_inc(S("slot_idx_ready"), 1)

            a2b = aff2.unsqueeze(2).to_broadcast([P, KT, BS])
            s2b = modv[:, 3, :].unsqueeze(2).to_broadcast([P, KT, BS])

            def scale_shift(b, u):
                dve.wait_ge(S("xt_ready"), b + 5)
                dve.tensor_tensor(xgT[:, u, :, :], XT[u][:, :].rearrange("p (k n) -> p k n", k=KT), a2b, ALU.mult).then_inc(S("xt_scaled"), 1)
                dve.wait_ge(S("xt_scaled"), b + 1)
                dve.tensor_tensor(xgT[:, u, :, :], xgT[:, u, :, :], s2b, ALU.add).then_inc(S("xgT_ready"), 1)

            blocks = dve.value_load(nblk_i[0:1, :], min_val=0, max_val=NBLK)
            scale_shift(0, 0)
            with dve.Fori(0, NBLK // WS) as i:
                for v in range(WS):
                    b, u = WS * i + v, v % 2
                    with dve.If(b < blocks):
                        dve.wait_ge(S("down_high"), b + 1)
                        dve.tensor_tensor(wdl[:, u, 1024:2048], wdn[v][:, 1024:2048], wdh[:, u, 1024:2048].bitcast(F32), ALU.subtract).then_inc(S("down_low_v"), 1)
                        dve.wait_ge(S("tanh_ready"), b + 1)
                        dve.wait_ge(S("y_ready"), b + 3)
                        dve.scalar_tensor_tensor(acth[:, u, :], tanhg[:, u, :], 1.0, GB[u][:, 0:128], ALU.add, ALU.mult).then_inc(S("tanh_free"), 1)
                        dve.wait_ge(S("tanh_free"), b + 5)
                        dve.wait_ge(S("up_ready"), b + 5)
                        dve.tensor_tensor(ahh[:, u, :], acth[:, u, :], UB[u][:, 0:128], ALU.mult).then_inc(S("act_high"), 1)
                        dve.tensor_tensor(acth[:, u, :], acth[:, u, :], UB[u][:, 0:128], ALU.mult).then_inc(S("act_whole"), 1)
                        dve.wait_ge(S("act_whole"), b + 1)
                        dve.wait_ge(S("act_high"), b + 1)
                        dve.tensor_tensor(ahl[:, u, :], acth[:, u, :], ahh[:, u, :].bitcast(F32), ALU.subtract).then_inc(S("act_low"), 1)
                        scale_shift(b + 1, 1 - u)
            for t in range(NT):
                dve.wait_ge(S(f"picked{t}"), 32)
                own(dve.tensor_scalar(r12[:, t, 0, :], r12[:, t, 0, :], w1c[:, t:t + 1], None, ALU.mult))
                own(dve.scalar_tensor_tensor(r12[:, t, 1, :], r12[:, t, 1, :], w2c[:, t:t + 1], r12[:, t, 0, :], ALU.mult, ALU.add))
                own(dve.tensor_tensor(r12[:, t, 1, :], r12[:, t, 1, :], g2row, ALU.mult))
                dve.tensor_tensor(Xv[:, t, :], Xv[:, t, :], r12[:, t, 1, :], ALU.add).then_inc(S("x_final"), 1)
            for t in range(NT):
                dve.wait_ge(S("rstd_f"), t + 1)
                dve.scalar_tensor_tensor(Xv[:, t, :], Xv[:, t, :], rsf[:, t:t + 1], cols(tab3, TAB3, "final_g"), ALU.mult, ALU.mult).then_inc(S("out_ready"), 1)

        @block.tensor
        def _(pe):
            done = [0]

            def group(what, i):
                n = GIDX[what, i]
                assert n == done[0], (what, i, n, done[0])
                done[0] += 1
                if n >= GRING:
                    e, k = freed_count(n - GRING)
                    pe.wait_ge(S("bank_freed_" + e), k)
                return G[n % GRING]

            def filled(ins):
                ins.then_inc(S("group_filled"), 1)

            def weights(p):
                s = SPL[p]
                pe.wait_ge(S("low_split"), s + 1)
                return wh[:, split_slot(s)], wl[:, split_slot(s)]

            def split3(out, lhs, rhs, first, last):
                (ah, al), (bh, bl) = lhs, rhs
                pe.matmul(out, ah, bh, start=first, stop=False)
                pe.matmul(out, ah, bl, start=False, stop=False)
                return pe.matmul(out, al, bh, start=False, stop=last)

            def rows(what, p, act=None, kts=range(KT), k0=0, names=None):
                h, l = act or (Hhv, Hlv)
                a, b = (w.rearrange("p (k n) -> p k n", n=PC) for w in weights(p))
                for tp in range(2):
                    bank = group(what, names[tp] if names else tp)
                    for j in range(2):
                        t = 2 * tp + j
                        for k in kts:
                            ins = split3(bank[:, j * PC:(j + 1) * PC], (h[:, k, t * P:(t + 1) * P], l[:, k, t * P:(t + 1) * P]),
                                         (a[:, k, :], b[:, k, :]), k == kts[0], k == kts[-1])
                    filled(ins)

            def transposes(what, i, srcs, width=P, parts=P):
                bank = group(what, i)
                for j, s in enumerate(srcs):
                    ins = pe.transpose(bank[:, j * width:(j + 1) * width] if parts == P else bank[:, j * parts:(j + 1) * parts], s, ident[0:parts, 0:parts])
                filled(ins)

            pe.wait_ge(S("con_loaded"), 16)
            pe.wait_ge(S("rows_normed"), NT)
            for f in range(KT):
                transposes("h0", f, [hraw[:, t, f * P:(f + 1) * P] for t in range(NT)])
            wait_freed(pe, "h0", KT - 1)
            pe.wait_ge(S("sml_done"), 1)
            bank = group("gl", 0)
            gh, gl = (cols(w, SMW, "gl").rearrange("p (k n) -> p k n", k=KT) for w in (smh, sml))
            for t in range(NT):
                for k in range(KT):
                    ins = split3(bank[:, t * 24:(t + 1) * 24], (Hhv[:, k, t * P:(t + 1) * P], Hlv[:, k, t * P:(t + 1) * P]),
                                 (gh[:, k, :], gl[:, k, :]), k == 0, k == KT - 1)
            filled(ins)
            for n in ("kcvc", "ksvs", "kwvw"):
                rows(n, (n,))
            pe.wait_ge(S("cdup_ready"), 1)
            for c4 in range(4):
                transposes("cT", c4, [cdup[:, t, c4].rearrange("p u d -> p (u d)") for t in range(NT)])
            for j in range(2):
                rows(("q", j), ("q", j))
            pe.wait_ge(S("kdup_ready"), 1)
            for c4 in range(4):
                transposes("kT", c4, [kdup[:, t, c4].rearrange("p u d -> p (u d)") for t in range(NT)])
            pe.wait_ge(S("blk_low"), 1)
            for i in range(4):
                a, b = (w.rearrange("p (k n) -> p k n", n=P) for w in weights(("cmp", i // 2, i % 2)))
                bank = group("cmp1", i)
                for k in range(16):
                    ins = split3(bank[:, 0:62], (a[:, k, :], b[:, k, :]), (blkh[:, i // 2, k, :], blkl[:, i // 2, k, :]), k == 0, k == 15)
                filled(ins)
            pe.wait_ge(S("gelu_done"), 4)
            w2 = cols(par, PAR, "w_cmp2").rearrange("p (c f d) -> p c f d", c=2, f=2)
            bank = group("cmpk", 0)
            for g in range(2):
                for f in range(2):
                    ins = pe.matmul(bank[0:31, g * HD:(g + 1) * HD], cw[:, f * 62 + g * 31:f * 62 + (g + 1) * 31], w2[:, 0, f, :],
                                    start=f == 0, stop=f == 1)
            filled(ins)
            bank = group("cmpv", 0)
            for r in range(4):
                for g in range(2):
                    for f in range(2):
                        ins = pe.matmul(bank[32 * r:32 * r + 31, g * 256 + r * HD:g * 256 + (r + 1) * HD],
                                        cw[:, (2 + f) * 62 + g * 31:(2 + f) * 62 + (g + 1) * 31], w2[:, 1, f, :],
                                        start=f == 0, stop=f == 1)
            filled(ins)
            kcd = cw[0:32, 1536:1792].rearrange("p (g u d) -> p g u d", g=2, u=2)
            kcT = cw[:, 1792:1856].rearrange("p (g i) -> p g i", g=2)
            VBD = PTs[:, 0, :].rearrange("p (g n) -> p g n", g=2)
            pe.wait_ge(S("kcd_ready"), 1)
            transposes("cmpkT", 0, [kcd[:, g].rearrange("p u d -> p (u d)") for g in range(2)], parts=32)
            pe.wait_ge(S("q_normed"), 1)
            for c4 in range(4):
                transposes("qT", c4, [Zq[:, t, c4 * P:(c4 + 1) * P] for t in range(NT)])
            wait_freed(pe, "qT", 3)
            for q in range(NT):
                for o in range(2):
                    bank = group("cS", 2 * q + o)
                    r = slice(64 * o, 64 * o + 64)
                    for j in range(4):
                        h = 2 * j + o
                        ins = pe.matmul(bank[:, j * 32:(j + 1) * 32], qT[r, j, q * P:(q + 1) * P], kcT[r, h // 4, :], start=True, stop=True)
                    filled(ins)
                pe.wait_ge(S("cmp_p"), q + 1)
                transposes("cP", q, [cw[:, 1024 + g * P:1024 + (g + 1) * P] for g in range(2)])
                wait_freed(pe, "cP", q)
                bank = group("cO", q)
                for g in range(2):
                    ins = pe.matmul(bank[:, g * 256:(g + 1) * 256], SP[:, 0, g * P:(g + 1) * P], VBD[:, g, :], start=True, stop=True)
                filled(ins)
            wait_freed(pe, "cO", NT - 1)

            def scores(u):
                ty, q, h = units[u]
                nk = (q + 1) * P
                r = slice(64 * (h % 2), 64 * (h % 2) + 64)
                if u >= 2:
                    pe.wait_ge(S("score_biased"), u - 1)
                pe.matmul(SA[u % 2][:, 0:nk], qT[r, h // 2, q * P:(q + 1) * P], kT[r, 2 * ty + h // 4, 0:nk], start=True, stop=True)\
                  .then_inc(S("scores_ready"), 1)

            def turned(u):
                ty, q, h = units[u]
                pe.wait_ge(S("probs_ready"), u + 1)
                if u >= 2:
                    pe.wait_ge(S("pt_copied"), u - 1)
                for k in range(q + 1):
                    ins = pe.transpose(PB[u % 2][:, k * P:(k + 1) * P], SP[:, u % 2, k * P:(k + 1) * P], ident)
                ins.then_inc(S("probs_transposed"), 1)

            def values(u):
                ty, q, h = units[u]
                v = u // 8
                pe.wait_ge(S("pt_copied"), u + 1)
                if u % 8 == 0 and v:
                    pe.wait_ge(S("out_freed"), v)
                for k in range(q + 1):
                    ins = pe.matmul(OB[:, h * HD:(h + 1) * HD], PTs[:, u % 2, k * P:(k + 1) * P],
                                    Zv[:, k, ty, (h // 4) * HD:(h // 4 + 1) * HD], start=k == 0, stop=k == q)
                ins.then_inc(S("values_summed"), 1)

            bank = None

            def conv_quarter(t):
                nonlocal bank
                g, part = divmod(t, 4)
                i, k6 = divmod(g, 6)
                name = ("hc", "cg", "bg")[k6 // 2]
                f = k6 % 2
                a, b = (w.rearrange("p (k n) -> p k n", n=PC) for w in weights((name, i)))
                if part == 0:
                    bank = group(name, 2 * i + f)
                for k in range(2 * part, 2 * part + 2):
                    ins = split3(bank[:, :], (a[:, k, f * P:(f + 1) * P], b[:, k, f * P:(f + 1) * P]), (Hhv[:, k, :], Hlv[:, k, :]),
                                 k == 0, k == KT - 1)
                if part == 3:
                    filled(ins)

            for t in range(len(units) + 3):
                if t < len(units):
                    scores(t)
                if t < 48:
                    conv_quarter(t)
                if 0 <= t - 1 < len(units):
                    turned(t - 1)
                if 0 <= t - 2 < len(units):
                    values(t - 2)
            bank = group("csq", 0)
            pe.wait_ge(S("conv_sq"), 4)
            for t in range(NT):
                for f in range(4):
                    ins = pe.matmul(bank[:, t:t + 1], SPsq(f)[:, t * P:(t + 1) * P], one, start=f == 0, stop=f == 3)
            filled(ins)
            pe.wait_ge(S("attn_normed"), NT)
            for f in range(4):
                transposes("aT", f, [kT[:, t, f * P:(f + 1) * P] for t in range(NT)])
            wait_freed(pe, "aT", 3)
            pe.wait_ge(S("conv_low"), 4)
            for n in range(4):
                a, b = (w.rearrange("p (k n) -> p k n", n=PC) for w in weights(("wo", n)))
                for tp in range(2):
                    for part in range(2):
                        bank = group("wo", 4 * n + 2 * tp + part)
                        for j in range(2):
                            t = 2 * tp + j
                            for k in range(4 * part, 4 * part + 4):
                                ins = split3(bank[:, j * PC:(j + 1) * PC], (Yhv[:, k, t * P:(t + 1) * P], Ylv[:, k, t * P:(t + 1) * P]),
                                             (a[:, k, :], b[:, k, :]), k % 4 == 0, k % 4 == 3)
                        filled(ins)
            pe.wait_ge(S("rows_normed"), 2 * NT)
            for f in range(KT):
                transposes("h1", f, [hraw[:, t, f * P:(f + 1) * P] for t in range(NT)])
            wait_freed(pe, "h1", KT - 1)

            def mod_piece(m):
                bank = group("mod", m)
                pe.wait_ge(S("mod_summed"), m + 1)
                for f in range(2):
                    ins = pe.matmul(bank[:, f:f + 1], macc[:, m % 2, f * P:(f + 1) * P], one, start=True, stop=True)
                filled(ins)

            m = 0
            for r in range(FQ):
                for j in range(4):
                    a, b = (w.rearrange("p (k n) -> p k n", n=PC) for w in weights(("up", r, j)))
                    for f in range(2):
                        bank = group("up", (r * 4 + j) * 2 + f)
                        for k in range(KT):
                            ins = split3(bank[:, :], (a[:, k, f * P:(f + 1) * P], b[:, k, f * P:(f + 1) * P]), (Hhv[:, k, :], Hlv[:, k, :]),
                                         k == 0, k == KT - 1)
                        filled(ins)
                    if m < MODN:
                        mod_piece(m)
                        m += 1
                for j in range(4):
                    if j == 0:
                        pe.wait_ge(S("ffn_sq"), 8 * (r + 1))
                    i = (r * 4 + j) * 2
                    rows("down", ("down", r, j), act=(Yhv, Ylv), names=[i, i + 1])
                    if m < MODN:
                        mod_piece(m)
                        m += 1

            pe.wait_ge(S("rows_normed"), 3 * NT)
            for f in range(KT):
                transposes("h2", f, [hraw2[:, t, f * P:(f + 1) * P] for t in range(NT)])
            wait_freed(pe, "h2", KT - 1)
            pe.wait_ge(S("sml_done"), 2)

            def small_rows(what, lo, n):
                bank = group(what, 0)
                a, b = (w[:, lo:lo + KT * n].rearrange("p (k n) -> p k n", k=KT) for w in (smh, sml))
                for t in range(NT):
                    for k in range(KT):
                        ins = split3(bank[:, t * n:(t + 1) * n], (Hhv[:, k, t * P:(t + 1) * P], Hlv[:, k, t * P:(t + 1) * P]),
                                     (a[:, k, :], b[:, k, :]), k == 0, k == KT - 1)
                filled(ins)

            def features(what, p, i0, ng=2, act=None, kts=range(KT), ncols=PC, k0=0):
                h, l = act or (Hhv, Hlv)
                n = len(kts)
                a, b = (w[:, 0:n * ncols].rearrange("p (k n) -> p k n", n=ncols) for w in weights(p))
                for f in range(ng):
                    bank = group(what, i0 + f)
                    for kk, k in enumerate(kts):
                        ins = split3(bank[:, :], (a[:, kk, f * P:(f + 1) * P], b[:, kk, f * P:(f + 1) * P]), (h[:, k, :], l[:, k, :]),
                                     kk == 0, kk == n - 1)
                    filled(ins)

            small_rows("if", SMW2["if"][0], 8)
            for j in range(4):
                features("qk", ("qk", j), 2 * j)
            for j in range(4):
                rows("om", ("om", j), names=[2 * j, 2 * j + 1])
            pe.wait_ge(S("lf_ready"), 1)
            tri = cols(con, CON, "tri")
            bank = group("cum", 0)
            for t in range(NT):
                for k in range(t + 1):
                    ins = pe.matmul(bank[:, 4 * t:4 * t + 4], tri if k == t else one.to_broadcast([P, P]), lf[:, k, :], start=k == 0, stop=k == t)
            filled(ins)
            pe.wait_ge(S("c_ready"), 1)
            for h in range(MH):
                bank = group("crow", h)
                for t in range(NT):
                    ins = pe.matmul(bank[:, t * P:(t + 1) * P], cc_[:, t, h:h + 1].to_broadcast([P, P]), ident, start=True, stop=True)
                filled(ins)
            for j in range(4):
                rows("vm", ("vm", j), names=[2 * j, 2 * j + 1])
            wait_freed(pe, "vm", 7)
            pe.wait_ge(S("qk_done"), 8)

            def mscores(u):
                h, q = munits[u]
                nk = (q + 1) * P
                pe.wait_ge(S("score_biased"), M0 + u - 1)
                pe.matmul(SA[u % 2][:, 0:nk], qkT[:, h, q * P:(q + 1) * P], qkT[:, MH + h, 0:nk], start=True, stop=True).then_inc(S("scores_ready"), 1)

            def mturned(u):
                h, q = munits[u]
                pe.wait_ge(S("score_biased"), M0 + u + 1)
                pe.wait_ge(S("pt_copied"), M0 + u - 1)
                for k in range(q + 1):
                    ins = pe.transpose(PB[u % 2][:, k * P:(k + 1) * P], SP2[:, u % 2, k * P:(k + 1) * P], ident)
                ins.then_inc(S("probs_transposed"), 1)

            def mvalues(u):
                h, q = munits[u]
                pe.wait_ge(S("pt_copied"), M0 + u + 1)
                if u == 0:
                    pe.wait_ge(S("out_freed"), 8)
                if u:
                    pe.wait_ge(S("m_out"), u)
                for k in range(q + 1):
                    ins = pe.matmul(OB[:, 0:MV], PT2[:, u % 2, k * P:(k + 1) * P], vm[:, k, h * MV:(h + 1) * MV],
                                    start=k == 0, stop=k == q)
                ins.then_inc(S("values_summed"), 1)

            def c3_third(t):
                nonlocal bank
                i, part = divmod(t, 3)
                j, tp = divmod(i, 2)
                a, b = (w.rearrange("p (k n) -> p k n", n=PC) for w in weights(("c3", j)))
                if part == 0:
                    bank = group("c3", i)
                steps = [(jj, k) for jj in range(2) for k in range(KT)]
                for jj, k in steps[(0, 6, 11)[part]:(6, 11, 16)[part]]:
                    tt = 2 * tp + jj
                    ins = split3(bank[:, jj * PC:(jj + 1) * PC], (Hhv[:, k, tt * P:(tt + 1) * P], Hlv[:, k, tt * P:(tt + 1) * P]),
                                 (a[:, k, :], b[:, k, :]), k == 0, k == KT - 1)
                if part == 2:
                    filled(ins)

            for t in range(len(munits) + 3):
                if t < len(munits):
                    mscores(t)
                if t < 18:
                    c3_third(t)
                if 0 <= t - 1 < len(munits):
                    mturned(t - 1)
                if 0 <= t - 2 < len(munits):
                    mvalues(t - 2)
            pe.wait_ge(S("m_out"), len(munits))
            for f in range(KT):
                transposes("yT", f, [To[:, t, f * P:(f + 1) * P] for t in range(NT)])
            wait_freed(pe, "yT", KT - 1)
            for j in range(4):
                features("gm", ("gm", j), 2 * j)
                features("bm", ("bm", j), 2 * j, act=(Yhv, Ylv))
            pe.wait_ge(S("kr_normed"), 1)
            for f in range(5):
                transposes("cT2", f, [c3[:, t, f * P:(f + 1) * P] for t in range(NT)])
            pe.wait_ge(S("kr_turned"), 1)
            transposes("krT", 0, [kr2[:, t].rearrange("p u n -> p (u n)") for t in range(NT)])
            wait_freed(pe, "cT2", 4)
            for j in range(2):
                features("qn", ("qn", j), 4 * j, ng=4, act=(Ch, Cl), kts=range(3), ncols=512)
            a, b = (w[:, 0:1536].rearrange("p (k n) -> p k n", n=512) for w in weights(("qr",)))
            for t in range(NT):
                bank = group("qr", t)
                for k in range(3):
                    ins = split3(bank[:, :], (Ch[:, k, t * P:(t + 1) * P], Cl[:, k, t * P:(t + 1) * P]), (a[:, k, :], b[:, k, :]), k == 0, k == 2)
                filled(ins)
            for t in range(NT):
                wait_freed(pe, "qr", t)
                transposes("qrT", t, [qrr[:, t, c * P:(c + 1) * P] for c in range(4)])
            features("kn", ("kn",), 0, ng=8, act=(Ch, Cl), kts=range(3, 5), ncols=1024)
            a, b = (w.rearrange("p (k n) -> p k n", n=1024) for w in weights(("va",)))
            for i in range(8):
                t, half = divmod(i, 2)
                bank = group("va", i)
                for k in range(2):
                    ins = split3(bank[:, :], (Ch[:, 3 + k, t * P:(t + 1) * P], Cl[:, 3 + k, t * P:(t + 1) * P]),
                                 (a[:, k, half * 512:(half + 1) * 512], b[:, k, half * 512:(half + 1) * 512]), k == 0, k == 1)
                filled(ins)
            wait_freed(pe, "va", 7)
            wait_freed(pe, "qrT", 3)
            wait_freed(pe, "krT", 0)

            def ascores(u):
                q, h = aunits[u]
                nk = (q + 1) * P
                r = slice(64 * (h % 2), 64 * (h % 2) + 64)
                pe.wait_ge(S("score_biased"), A0 + u - 1)
                pe.matmul(SA[u % 2][:, 0:nk], qn[:, h, q * P:(q + 1) * P], kn[:, h, 0:nk], start=True, stop=False)
                pe.matmul(SA[u % 2][:, 0:nk], qrT[r, h // 2, q * P:(q + 1) * P], krT[r, 0:nk], start=False, stop=True).then_inc(S("scores_ready"), 1)

            def aturned(u):
                q, h = aunits[u]
                pe.wait_ge(S("probs_ready"), M0 + u + 1)
                pe.wait_ge(S("pt_copied"), A0 + u - 1)
                for k in range(q + 1):
                    ins = pe.transpose(PB[u % 2][:, k * P:(k + 1) * P], SP3[:, u % 2, k * P:(k + 1) * P], ident)
                ins.then_inc(S("probs_transposed"), 1)

            def avalues(u):
                q, h = aunits[u]
                pe.wait_ge(S("pt_copied"), A0 + u + 1)
                if u:
                    pe.wait_ge(S("a_out"), u)
                for k in range(q + 1):
                    ins = pe.matmul(OB[:, 0:P], PT3[:, u % 2, k * P:(k + 1) * P], va[:, k, h * P:(h + 1) * P],
                                    start=k == 0, stop=k == q)
                ins.then_inc(S("values_summed"), 1)

            for t in range(len(aunits) + 4):
                if t < len(aunits):
                    ascores(t)
                if 0 <= t - 1 < len(aunits):
                    aturned(t - 1)
                if t >= 11 and (t - 11) % 8 == 0:
                    q = (t - 11) // 8
                    pe.wait_ge(S("a_out"), 8 * q + 8)
                    for i in range(2):
                        transposes("yaT", 2 * q + i, [ya[:, (4 * i + f) * P:(4 * i + f + 1) * P] for f in range(4)])
                if 0 <= t - 2 < len(aunits):
                    avalues(t - 2)
            wait_freed(pe, "yaT", 7)
            for j in range(4):
                features("ga", ("ga", j), 2 * j)
                features("ba", ("ba", j), 2 * j, act=(Yhv, Ylv))
            for i in range(2):
                bank = group("g1r", i)
                for k in range(4):
                    ins = pe.matmul(bank[:, k * P:(k + 1) * P], modv[:, 2, 4 * i + k:4 * i + k + 1].to_broadcast([P, P]), ident, start=True, stop=True)
                filled(ins)
            pe.wait_ge(S("merged_low"), KT)
            for j in range(4):
                rows("wout", ("wout", j), names=[2 * j, 2 * j + 1])

            for i in range(2):
                bank = group("g2r", i)
                for k in range(4):
                    ins = pe.matmul(bank[:, k * P:(k + 1) * P], modv[:, 5, 4 * i + k:4 * i + k + 1].to_broadcast([P, P]), ident, start=True, stop=True)
                filled(ins)
            pe.wait_ge(S("rows_normed"), 4 * NT)
            for f in range(KT):
                transposes("h3", f, [hraw3[:, t, f * P:(f + 1) * P] for t in range(NT)])
            wait_freed(pe, "h3", KT - 1)
            small_rows("gr", SMW2["gr"][0], 36)
            pe.wait_ge(S("assigned"), 1)
            bank = group("cnt", 0)
            for t in range(NT):
                ins = pe.matmul(bank[0:32, 0:1], Aa[:, t, :], one, start=t == 0, stop=t == NT - 1)
            filled(ins)
            bank = group("rank", 0)
            for t in range(NT):
                for k in range(t + 1):
                    ins = pe.matmul(bank[:, 32 * t:32 * t + 32], tri if k == t else one.to_broadcast([P, P]), Aa[:, k, :], start=k == 0, stop=k == t)
            filled(ins)
            pe.wait_ge(S("nb_ready"), 1)
            bank = group("pstart", 0)
            pe.matmul(bank[:, 0:32], nbc[0:32, :].to_broadcast([32, P]), triex[0:32, :], start=True, stop=True)
            pe.matmul(bank[0:32, 32:33], tri[0:32, 0:32], nbc[0:32, :], start=True, stop=True)
            ins = pe.matmul(bank[:, 33:34], one[0:32, :].to_broadcast([32, P]), nbc[0:32, :], start=True, stop=True)
            filled(ins)
            pe.wait_ge(S("ended_ready"), 1)
            bank = group("bexp", 0)
            filled(pe.matmul(bank[:, 0:NBLK], one[0:32, :].to_broadcast([32, P]), cmpe[0:32, :], start=True, stop=True))
            pe.wait_ge(S("slots_loaded"), 16)
            bank = group("slotT", 0)
            filled(pe.transpose(bank[0:BS, 0:NBLK], slotr[0:NBLK, :], ident[0:NBLK, 0:NBLK]))
            wait_freed(pe, "slotT", 0)
            for n in ("xt_ready", "up_ready", "y_ready", "tanh_free", "y_copied", "down_low_p", "down_low_v"):
                pe.sem_inc(S(n), 4)
            for u in range(2):
                pe.sem_inc(S(f"y_stored{u}"), 16)
            def rows_transposed(b, u, v, loaded):
                pe.wait_ge(S(f"xg_loaded{v}"), loaded)
                for k in range(KT):
                    args = XT[u][:, k * BS:(k + 1) * BS], xg[0:BS, v, k * P:(k + 1) * P], ident[0:BS, 0:BS]
                    ins = pe.transpose(*args) if k else pe.matmul(*args, start=True, stop=True)
                ins.then_inc(S("xt_ready"), 1)

            pe.wait_ge(S("bexp_ready"), 1)
            blocks = pe.value_load(nblk_i[0:1, :], min_val=0, max_val=NBLK)
            rows_transposed(0, 0, 0, 16)
            with pe.Fori(0, NBLK // WS) as i:
                for v in range(WS):
                    b, u = WS * i + v, v % 2
                    with pe.If(b < blocks):
                        wg = wgu[v].rearrange("p (j k n) -> p j k n", j=2, k=KT)
                        wd, wl_ = (w[:, u, :].rearrange("p (k n) -> p k n", k=2) for w in (wdh, wdl))
                        pe.wait_ge(S("xgT_ready"), b + 1)
                        pe.wait_ge(S(f"gu_loaded{v}"), 16 * i + 16)
                        for j, bank, ready in ((0, GB[u], "gate_ready"), (1, UB[u], "up_ready")):
                            for f in range(2):
                                for k in range(KT):
                                    ins = pe.matmul(bank[:, f * BS:(f + 1) * BS], wg[:, j, k, f * P:(f + 1) * P], xgT[:, u, k, :], start=k == 0, stop=k == KT - 1)
                            ins.then_inc(S(ready), 1)
                        rows_transposed(b + 1, 1 - u, (v + 1) % WS, 16 * i + 16 * ((v + 1) // WS) + 16)
                        pe.wait_ge(S("act_high"), b + 1)
                        pe.wait_ge(S("down_high"), b + 1)
                        pe.wait_ge(S("y_copied"), b + 4)
                        for lhs, rhs, last in ((ahh, wd, False), (ahh, wl_, False), (ahl, wd, True)):
                            if rhs is wl_:
                                pe.wait_ge(S("down_low_p"), b + 5)
                                pe.wait_ge(S("down_low_v"), b + 5)
                            if last:
                                pe.wait_ge(S("act_low"), b + 1)
                            for half in range(2):
                                for k in range(2):
                                    ins = pe.matmul(YB[half][0:BS, :], lhs[:, u, k * BS:(k + 1) * BS], rhs[:, k, half * 512:(half + 1) * 512],
                                                    start=k == 0 and lhs is ahh and rhs is wd, stop=k == 1 and last)
                        ins.then_inc(S("y_ready"), 1)


def _kxn(w):
    k, n = w.shape
    return w.reshape(k // P, P, n).transpose(1, 0, 2).reshape(P, -1)


def _col(v):
    return v.reshape(-1, P).T


def _rows(v):
    return np.broadcast_to(v.reshape(1, -1), (P, v.size))


def _padded(a):
    return np.concatenate([a, np.zeros((P, PIECE - a.shape[1]), a.dtype)], 1)


def _piece(inp, p):
    k, c = p[0], PC
    w, w2 = inp["w_in"][0], inp["w_in_2"][0]
    first = {"kcvc": 512, "ksvs": 768, "kwvw": 1024}
    conv = {"hc": 1304, "cg": 1816, "bg": 2328}
    second = {"qk": 0, "vm": 1024, "om": 2048, "gm": 3784, "ga": 4808}
    square = {"wo": "w_o", "mod": "mod_w_2", "bm": "w_branch_m_2", "ba": "w_branch_a_2", "wout": "w_out_2"}
    if k in first:
        return _kxn(w[:, first[k]:first[k] + c])
    if k == "q":
        return _kxn(w[:, p[1] * c:(p[1] + 1) * c])
    if k == "cmp":
        return _kxn(inp["w_cmp1"][0, p[1]][:, p[2] * P:(p[2] + 1) * P])
    if k in conv:
        o = conv[k] + p[1] * c
        return _kxn(w[:, o:o + c])
    if k == "up":
        o = (p[1] * 4 + p[2]) * c
        return _kxn(inp["w_up"][0][:, o:o + c])
    if k == "down":
        return _kxn(inp["w_down"][0][p[1] * D:(p[1] + 1) * D, p[2] * c:(p[2] + 1) * c])
    if k in square:
        return _kxn(inp[square[k]][0][:, p[1] * c:(p[1] + 1) * c])
    if k in second:
        o = second[k] + p[1] * c
        return _kxn(w2[:, o:o + c])
    if k == "c3":
        latent = np.concatenate([w2[:, 3080:3784], np.zeros((D, 64), w2.dtype)], 1)
        return _kxn(latent[:, p[1] * c:(p[1] + 1) * c])
    uq = inp["w_uq_2"][0].reshape(CQ, AH, 192)
    ukv = inp["w_ukv_2"][0].reshape(CKV, AH, 256)
    if k == "qn":
        return _padded(_kxn(uq[:, p[1] * 4:p[1] * 4 + 4, :P].reshape(CQ, 512)))
    if k == "qr":
        return _padded(_kxn(uq[:, :, P:].reshape(CQ, 512)))
    return _kxn((ukv[:, :, :P] if k == "kn" else ukv[:, :, P:]).reshape(CKV, 1024))


def _parameters(inp):
    twice = lambda v: np.concatenate([v, v])[:, None]
    pe_cmp = inp["pe_cmp"][0].reshape(2, 16, 2, HD)
    par = [_col(inp[n][0]) for n in ("g_mix_norm", "g_ffn_norm", "g_out")]
    par += [twice(inp["g_q"][0])] + [twice(inp["g_k"][0, i]) for i in range(3)]
    par += [_col(inp["b_cmp1"][0].reshape(-1)), pe_cmp.transpose(2, 3, 0, 1).reshape(P, 32),
            inp["conv_w"][0].reshape(3, 4, P).transpose(2, 1, 0).reshape(P, 12),
            inp["w_cmp2"][0].reshape(2, 2, P, HD).transpose(2, 0, 1, 3).reshape(P, 256),
            _rows(inp["b_cmp2"][0]), _col(inp["c_2"][0]), _col(inp["mod_b_2"][0])]
    par2 = [_col(inp["norm1_g_2"][0]), _col(inp["norm2_g_2"][0]),
            inp["conv_w_2"][0].reshape(4, 8, P).transpose(2, 1, 0).reshape(P, 32), _col(inp["conv_b_2"][0]),
            _col(inp["q_norm_g_2"][0]), _col(inp["kv_norm_g_2"][0]),
            _rows(inp["igate_b_2"][0]), _rows(inp["fgate_b_2"][0]), _rows(inp["b_group_2"][0]), _rows(inp["b_router_2"][0])]
    return np.concatenate(par, 1), np.concatenate(par2, 1)


def _constants():
    p, j = np.arange(P)[:, None], np.arange(T)[None]
    con = [np.eye(P), np.triu(np.ones((P, P))), np.ones((P, 1)), np.full((P, 1), -0.5)]
    slope = np.power(np.float32(2.0), np.float32(-8.0) * np.arange(1, NH + 1, dtype=np.float32) / NH).astype(np.float32)
    dist = (p + (T - P) - j).astype(np.float32)
    alibi = np.where(dist[:, None] >= 0, -slope[None, :, None] * dist[:, None], NEG)
    tok = np.arange(T).reshape(NT, P).T
    dist = (tok[:, :, None] - (np.arange(32) * CS + 31)).astype(np.float32)
    seen = (dist >= 0) & (np.arange(32) < CMP_I)
    cmpb = np.where(seen[:, :, None], -slope[None, None, :, None] * dist[:, :, None], NEG)
    inv = (1.0 / (np.float32(10000.0) ** (np.arange(0, 64, 2, dtype=np.float32) / np.float32(64)))).astype(np.float32)
    ang = np.arange(T, dtype=np.float32)[:, None] * inv[None]
    tab2 = [f(ang).reshape(NT, P, 32).transpose(1, 0, 2).reshape(P, -1) for f in (np.cos, np.sin)]
    j = j - (T - P)
    tab2 += [np.where(j <= p, 0, NEG), np.where(j // 64 <= p // 64, 0, NEG)]
    bias = [a.reshape(P, -1) for a in (alibi, cmpb, seen)]
    return [np.concatenate(a, 1).astype(np.float32) for a in (con, bias, tab2)]


_OUTS = [((1, T, D), "float32")]


def kernel(**inputs):
    from concourse import bacc
    from concourse.bass_utils import run_bass_kernel_spmd

    par, par2 = _parameters(inputs)
    con, bias, tab2 = _constants()
    dense, w_in_2 = _kxn(inputs["w_in"][0][:, 1280:1304]), inputs["w_in_2"][0]
    route = np.concatenate([inputs["w_group_2"][0], inputs["w_router_2"][0]], 1)
    tab3 = np.concatenate([_rows(np.arange(32, 0, -1)), _rows(np.arange(NBLK)), _rows(BS * np.arange(8) + 1),
                           np.arange(T).reshape(NT, P).T, _rows(inputs["final_norm_g_2"])], 1, dtype=np.float32)
    experts = [inputs[n][0].reshape(NE, -1, P, inputs[n].shape[-1]).transpose(0, 2, 1, 3).reshape(NE, P, PIECE)
               for n in ("w_expert_gate_2", "w_expert_up_2", "w_expert_down_2")]
    laid = {
        "x": inputs["x"][0],
        "pieces": np.stack([_piece(inputs, p) for p in all_pieces()]),
        "par": par, "con": con, "smw": dense, "bias": bias, "par2": par2,
        "smw2": np.concatenate([_kxn(w_in_2[:, 3072:3080]), _kxn(route)], 1),
        "tab2": tab2, "tab3": tab3, "wexp": np.concatenate(experts, 2),
    }
    nc = bacc.Bacc("TRN2", target_bir_lowering=False, num_devices=1)
    arrays, args = {}, []
    for name, a in laid.items():
        a = np.ascontiguousarray(a)
        arrays[f"in_{name}_dram"] = a
        args.append(nc.dram_tensor(f"in_{name}_dram", a.shape, mybir.dt.from_np(a.dtype), kind="ExternalInput").ap())
    out = nc.dram_tensor("out_0_dram", (T, D), F32, kind="ExternalOutput").ap()
    build(nc, *args, out)
    r = run_bass_kernel_spmd(nc, [arrays], core_ids=[0])
    return r.results[0]["out_0_dram"].reshape(_OUTS[0][0])
```

```python
from contextlib import ExitStack

import concourse.bass as bass
import numpy as np
from concourse import mybir

F32 = mybir.dt.float32
F32R = mybir.dt.float32r
I32 = mybir.dt.int32
ALU = mybir.AluOpType
ACT = mybir.ActivationFunctionType
AX = mybir.AxisListType

P = 128
T = 512
D = 1024
NT = T // P
KT = D // P
PC = 256
PIECE = KT * PC
EPS = 1e-6
NEG = -1e30

HD = 64
NH = 8
CMP_I = 31
CS = 16
FQ = 4



def first_pieces():
    return ([("kcvc",), ("ksvs",), ("kwvw",), ("q", 0), ("q", 1)]
            + [("cmp", c, f) for c in range(2) for f in range(2)]
            + [(n, i) for i in range(2) for n in ("hc", "cg", "bg")]
            + [("wo", n) for n in range(4)])


def ffn_pieces():
    return [(n, r, j) for r in range(FQ) for n in ("up", "down") for j in range(4)]


MOD_PIECES = 24

MH = 4
MV = 256
AH = 8
NE = 32
NEG_ = 4
EG = NE // NEG_
BS = 64
NBLK = 48
MIN_BLK = 2 * T // BS
WE = 3 * PIECE
WS = 4
CQ, CKV = 384, 256


def mixer_pieces():
    return ([("qk", j) for j in range(4)] + [("om", j) for j in range(4)] + [("vm", j) for j in range(4)]
            + [("c3", j) for j in range(3)]
            + [(n, j) for j in range(4) for n in ("gm", "bm")]
            + [("qn", 0), ("qn", 1), ("qr",), ("va",), ("kn",)]
            + [(n, j) for j in range(4) for n in ("ga", "ba")]
            + [("wout", j) for j in range(4)])


def split_pieces():
    return first_pieces() + ffn_pieces() + mixer_pieces()


def all_pieces():
    out = list(first_pieces())
    for i, p in enumerate(ffn_pieces()):
        out.append(p)
        if i < MOD_PIECES:
            out.append(("mod", i))
    return out + mixer_pieces()


def columns(fields):
    at, out = 0, {}
    for name, n in fields:
        out[name] = (at, at + n)
        at += n
    out["_"] = (0, at)
    return out


PAR = columns([("g_mix", 8), ("g_ffn", 8), ("g_out", 8), ("g_q", 1), ("g_k", 3), ("b_cmp1", 4), ("pe", 32),
               ("conv_w", 12), ("w_cmp2", 256), ("b_cmp2", 128), ("c", 8), ("mod_b", 48)])
PAR2 = columns([("g_1", 8), ("g_2", 8), ("conv_w2", 32), ("conv_b2", 8), ("g_cq", 3), ("g_ckv", 2), ("b_if", 8), ("b_gr", 36)])
TAB3 = columns([("dec", 32), ("iota", NBLK), ("thr", 8), ("tok", 2 * NT), ("iota_r", BS), ("iota_b", NBLK + 2), ("final_g", D)])
SMW = columns([("gl", KT * 24)])
SMW2 = columns([("if", KT * 8), ("gr", KT * 36)])
TAB2 = columns([("cos", NT * 32), ("sin", NT * 32), ("causal", T), ("chunk", T)])
CON = columns([("ident", P), ("tri", P), ("one", 1), ("mhalf", 1)])
BIAS = columns([("alibi", NH * T), ("cmpb", NT * NH * 32), ("cmpm", NT * 32)])



def plan_groups():
    g = [("h0", f, "v") for f in range(KT)]
    g += [("gl", 0, "a")]
    for n in ("kcvc", "ksvs", "kwvw"):
        g += [(n, t, "a") for t in range(2)]
        g += [("glT", 0, "a")] if n == "kcvc" else []
    g += [("cT", c, "v") for c in range(4)]
    g += [(("q", j), t, "a") for j in range(2) for t in range(2)]
    g += [("kT", c, "v") for c in range(4)]
    g += [("cmp1", c, "v") for c in range(4)] + [("cmpT", c, "v") for c in range(2)]
    g += [("cmpk", 0, "v"), ("cmpv", 0, "v"), ("cmpkT", 0, "v")]
    g += [("qT", c, "v") for c in range(4)]
    g += [("cS", o, "v") for o in range(2)] + [("cP", i, "v") for i in range(2)] + [("cO", q, "v") for q in range(NT)]
    for i in range(2):
        g += [("hc", 2 * i + f, "a") for f in range(2)]
        g += [("cg", 2 * i + f, "v") for f in range(2)]
        g += [("bg", 2 * i + f, "v") for f in range(2)]
    g += [("csq", 0, "v")]
    g += [("aT", f, "v") for f in range(4)]
    g += [("wo", i, "v") for i in range(16)]
    g += [("h1", f, "v") for f in range(KT)]
    m = 0
    for r in range(FQ):
        for j in range(4):
            g += [("up", (r * 4 + j) * 2 + f, "a") for f in range(2)]
            if m < MOD_PIECES:
                g += [("mod", m, "v")]
                m += 1
        for j in range(4):
            g += [("down", (r * 4 + j) * 2 + t, "v") for t in range(2)]
            if m < MOD_PIECES:
                g += [("mod", m, "v")]
                m += 1
    g += [("h2", f, "v") for f in range(KT)]
    g += [("if", 0, "v")]
    g += [("qk", f, "a") for f in range(2)]
    g += [("ifT", 0, "v")]
    g += [("qk", f, "a") for f in range(2, 8)]
    g += [("om", t, "a") for t in range(8)]
    g += [("cum", 0, "v")]
    g += [("crow", h, "v") for h in range(MH)]
    g += [("vm", t, "a") for t in range(8)]
    g += [("c3", t, "a") for t in range(6)]
    g += [("yT", f, "v") for f in range(KT)]
    for j in range(4):
        g += [("gm", 2 * j + f, "a") for f in range(2)]
        g += [("bm", 2 * j + f, "v") for f in range(2)]
    g += [("cT2", f, "v") for f in range(5)]
    g += [("qn", h, "a") for h in range(AH)]
    g += [("krT", 0, "v")]
    for t in range(NT):
        g += [("qr", t, "v")]
    g += [("va", i, "a") for i in range(8)]
    g += [("qrT", t, "v") for t in range(NT)]
    g += [("kn", h, "a") for h in range(AH)]
    g += [("yaT", i, "v") for i in range(8)]
    for j in range(4):
        g += [("ga", 2 * j + f, "a") for f in range(2)]
        g += [("ba", 2 * j + f, "v") for f in range(2)]
    g += [("g1r", i, "a") for i in range(2)]
    g += [("wout", i, "v") for i in range(8)]
    g += [("g2r", i, "a") for i in range(2)]
    g += [("h3", f, "v") for f in range(KT)]
    g += [("gr", 0, "v"), ("grT", 0, "v"), ("cnt", 0, "v"), ("rank", 0, "v"), ("pstart", 0, "v"), ("bexp", 0, "v"), ("slots", 0, "v")]
    return g


GROUPS = plan_groups()
GIDX = {(w, i): n for n, (w, i, _) in enumerate(GROUPS)}
GRING = 3


def last_groups():
    out = {}
    for p in first_pieces() + ffn_pieces() + [("mod", m) for m in range(MOD_PIECES)] + mixer_pieces():
        k = p[0]
        if k in ("kcvc", "ksvs", "kwvw"):
            out[p] = GIDX[k, 1]
        elif k == "q":
            out[p] = GIDX[p, 1]
        elif k == "cmp":
            out[p] = GIDX["cmp1", 2 * p[1] + p[2]]
        elif k in ("hc", "cg", "bg"):
            out[p] = GIDX[k, 2 * p[1] + 1]
        elif k == "wo":
            out[p] = GIDX[k, 4 * p[1] + 3]
        elif k == "mod":
            out[p] = GIDX[p]
        elif k in ("om", "vm", "c3", "gm", "bm", "ga", "ba", "wout"):
            out[p] = GIDX[k, 2 * p[1] + 1]
        elif k == "qk":
            out[p] = GIDX[k, 2 * p[1] + 1]
        elif k == "qn":
            out[p] = GIDX[k, 4 * p[1] + 3]
        elif k in ("qr", "kn", "va"):
            out[p] = GIDX[k, 3 if k == "qr" else 7]
        else:
            out[p] = GIDX[k, 2 * (4 * p[1] + p[2]) + 1]
    return out


LAST = last_groups()


def freed_count(n):
    e = GROUPS[n][2]
    return e, sum(1 for x in GROUPS[:n + 1] if x[2] == e)


def build(nc, x, wp, par_d, con_d, smw_d, bias_d, par2_d, smw2_d, tab2_d, tab3_d, wexp, out):
    with ExitStack() as ctx:
        def sb(name, n, dt=F32):
            return ctx.enter_context(nc.sbuf_tensor(name, [P, n], dt))

        sems = {}

        def S(name):
            if name not in sems:
                sems[name] = ctx.enter_context(nc.semaphore(name))
            return sems[name]

        X = sb("X", NT * D)
        raw = sb("raw", 2 * PIECE)
        par = sb("par", PAR["_"][1])
        con = sb("con", CON["_"][1])
        smh, sml = sb("smh", SMW2["_"][1], F32R), sb("sml", SMW2["_"][1], F32R)
        st = sb("st", 384)
        arena = sb("arena", 18560)
        with ExitStack() as dense:
            def part(name, n, dt=F32R):
                return dense.enter_context(nc.sbuf_tensor(name, [P, n], dt))

            wh, wl = part("wh", 2 * PIECE), part("wl", 2 * PIECE)
            Hh, Hl = part("Hh", KT * T), part("Hl", KT * T)
            Yh, Yl = part("Yh", KT * T), part("Yl", KT * T)
        wgu2, wgu3, wdn2, wdn3 = sb("wgu2", 2 * PIECE), sb("wgu3", 2 * PIECE), sb("wdn2", PIECE), sb("wdn3", PIECE)
        wdh_, wdl_ = sb("wdh", 2 * PIECE, F32R), sb("wdl", 2 * PIECE, F32R)
        ahh_, ahl_ = sb("ahh", 256, F32R), sb("ahl", 256, F32R)
        yb_ = sb("yb", 2 * D)

        smw = arena[:, 0:SMW["_"][1]]
        smw2 = arena[:, 0:SMW2["_"][1]]
        x_spill = nc.dram_tensor("x_spill", (P, NT * D), F32).ap()
        Xv = X[:, :].rearrange("p (t n) -> p t n", t=NT)

        def AR(a, n):
            return arena[:, a:a + n]

        def cols(t, table, name):
            a, b = table[name]
            return t[:, a:b]

        ident = cols(con, CON, "ident")
        one = cols(con, CON, "one")
        mhalf = cols(con, CON, "mhalf")

        alibi = AR(0, 4096).rearrange("p (h n) -> p h n", h=NH)
        cmpb = AR(4096, 1024).rearrange("p (q h i) -> p q h i", q=NT, h=NH)
        cmpm = AR(5120, 128).rearrange("p (q i) -> p q i", q=NT)
        Zq = AR(5248, 2048).rearrange("p (t n) -> p t n", t=NT)
        Oat = Zq
        Zk = AR(7296, 2048).rearrange("p (t n) -> p t n", t=NT)
        gl_rows = AR(10368, 512)[0:24, :]
        if_rows = AR(17536, 512)[0:8, :]
        gr_rows = AR(12288, 512)[0:36, :]
        Zv = AR(9344, 1024).rearrange("p (t s n) -> p t s n", t=NT, s=2)
        cpre = AR(16512, 512)[0:62, :]
        csv = AR(7296, 1024)
        cpv = AR(8320, 1024)
        conv = AR(7296, 2048).rearrange("p (f n) -> p f n", f=4)
        kdup = AR(10368, 2048).rearrange("p (t c u d) -> p t c u d", t=NT, c=4, u=2)
        cw = AR(10368, 2048)
        ctmp_h = AR(10368, 1024).rearrange("p (f n) -> p f n", f=2)
        ctmp_u = AR(11392, 512)
        otmp = AR(11904, 512)
        fsq = AR(10368, 1024).rearrange("p (r n) -> p r n", r=2)
        kT = AR(12416, 2048).rearrange("p (c n) -> p c n", c=4)
        qT = AR(14464, 2048).rearrange("p (c n) -> p c n", c=4)
        blkt = AR(14464, 1984).rearrange("p (c b a i) -> p c b a i", c=4, b=2, a=8)
        cdup = AR(16512, 2048).rearrange("p (t c u d) -> p t c u d", t=NT, c=4, u=2)
        SP = AR(16512, 1024).rearrange("p (r n) -> p r n", r=2)
        PTs = AR(17536, 1024).rearrange("p (r n) -> p r n", r=2)
        frelu = SP
        hraw = AR(12416, 4096).rearrange("p (t n) -> p t n", t=NT)
        blkh = Yh[:, 0:1984].rearrange("p (c k n) -> p c k n", c=2, k=16)
        blkl = Yl[:, 0:1984].rearrange("p (c k n) -> p c k n", c=2, k=16)
        Hhv, Hlv = (t[:, :].rearrange("p (k n) -> p k n", k=KT) for t in (Hh, Hl))
        Yhv, Ylv = (t[:, :].rearrange("p (k n) -> p k n", k=KT) for t in (Yh, Yl))

        modc = st[:, 0:48]
        condc = st[:, 48:56]
        mraw = AR(4096, 2 * PIECE)
        macc = AR(17536, 512).rearrange("p (r n) -> p r n", r=2)
        nst = [48 + 16]

        def small(n):
            nst[0] += n
            assert nst[0] <= 384
            return st[:, nst[0] - n:nst[0]]

        ss = small(NT)
        ms = small(NT)
        rstd = small(NT)
        ssqk = small(48)
        msqk = small(48)
        rqk = small(48)
        gates = small(96).rearrange("p (t n) -> p t n", t=NT)
        csum = cw[:, 768:800]
        cmaxn = cw[:, 800:832]
        ccoef = cw[:, 832:864]
        ssk = small(2)
        msk = small(2)
        rsk = small(2)
        ncoef = small(8)
        rsum = small(16)
        nmax = small(2)
        cond_t = small(8)

        modv = modc.rearrange("p (m k) -> p m k", m=6)
        nst[0] = 64
        ss2, ms2, rstd2 = small(NT), small(NT), small(NT)
        aff1, aff2 = small(KT), small(KT)
        ifr = small(32).rearrange("p (t n) -> p t n", t=NT)
        fabs = small(16).rearrange("p (t n) -> p t n", t=NT)
        flog = small(16).rearrange("p (t n) -> p t n", t=NT)
        lf = small(16).rearrange("p (t n) -> p t n", t=NT)
        Bc = small(16).rearrange("p (t n) -> p t n", t=NT)
        cc_ = small(16).rearrange("p (t n) -> p t n", t=NT)
        nm, emn, den, rr = small(16), small(16), small(16), small(16)
        ssc, msc, rsc = small(8), small(8), small(8)
        xpad_done = small(1)
        ssc_done = small(1)
        rsum2, nmax2, rinv = small(16), small(2), small(16)
        hraw2 = AR(8192, 4096).rearrange("p (t n) -> p t n", t=NT)
        qkT = AR(0, 4096).rearrange("p (f n) -> p f n", f=8)
        To = AR(4096, 4096).rearrange("p (t n) -> p t n", t=NT)
        c3 = AR(8192, 3072).rearrange("p (t n) -> p t n", t=NT)
        crow = AR(11264, 2048).rearrange("p (h n) -> p h n", h=MH)
        Eb = AR(13312, 1024).rearrange("p (r n) -> p r n", r=2)
        SP2 = AR(14336, 1024).rearrange("p (r n) -> p r n", r=2)
        PT2 = AR(15360, 1024).rearrange("p (r n) -> p r n", r=2)
        cacc, cth = Eb, SP2
        xpad = AR(16384, 1032).rearrange("p (r n) -> p r n", r=2)
        causal = AR(17924, 512)
        vm = Xv
        merged = AR(0, 4096).rearrange("p (f n) -> p f n", f=8)
        tg = Eb
        qn = AR(4096, 4096).rearrange("p (h n) -> p h n", h=AH)
        qrT = AR(8192, 2048).rearrange("p (c n) -> p c n", c=4)
        krT = AR(10240, 512)
        chunk = AR(10752, 512)
        cosT = AR(12288, 128).rearrange("p (t n) -> p t n", t=NT)
        sinT = AR(12416, 128).rearrange("p (t n) -> p t n", t=NT)
        kr2 = AR(12544, 512).rearrange("p (t u n) -> p t u n", t=NT, u=2)
        ropet = AR(13056, 256)
        kn = AR(11264, 4096).rearrange("p (h n) -> p h n", h=AH)
        SP3 = AR(15360, 1024).rearrange("p (r n) -> p r n", r=2)
        PT3 = AR(16384, 1024).rearrange("p (r n) -> p r n", r=2)
        qrr = AR(15360, 2048).rearrange("p (t n) -> p t n", t=NT)
        ya = AR(17408, 1024)
        va = Xv
        Ch, Cl = Yhv, Ylv
        tga = AR(16384, 1024).rearrange("p (r n) -> p r n", r=2)
        tba = AR(15360, 1024).rearrange("p (r n) -> p r n", r=2)
        g1row = AR(4096, 1024)
        wtmp = AR(5120, 1024).rearrange("p (r n) -> p r n", r=2)

        xn_rows = nc.dram_tensor("xn_rows", (T, D), F32).ap()
        y_rows = nc.dram_tensor("y_rows", (NBLK * BS, D), F32).ap()
        hraw3 = AR(0, 4096).rearrange("p (t n) -> p t n", t=NT)
        wgu = [AR(0, 2 * PIECE), AR(2 * PIECE, 2 * PIECE), wgu2[:, :], wgu3[:, :]]
        wdn = [AR(4 * PIECE, PIECE), AR(5 * PIECE, PIECE), wdn2[:, :], wdn3[:, :]]
        xgT = AR(12288, 1024).rearrange("p (u k n) -> p u k n", u=2, k=KT)
        g2row = AR(13312, 1024)
        tab3 = AR(14336, TAB3["_"][1])
        at = [14336 + TAB3["_"][1]]

        def AT(n):
            at[0] += n
            assert at[0] <= 18560
            return AR(at[0] - n, n)

        def v3(n):
            return AT(NT * n).rearrange("p (t n) -> p t n", t=NT)

        Lg, gsh, gex, okey = v3(36), v3(4), v3(4), v3(4)
        oh_g, insh, key8, oh1, oh2, d2 = v3(4), v3(8), v3(8), v3(8), v3(8), v3(8)
        gmx, gsum, pg, km, m1, m2, e2, w1c, w2c = (AT(NT) for _ in range(9))
        slots = AT(8)
        ing4 = AT(NT * 32)
        A1, A2, Aa, Sl, Tmp = v3(32), v3(32), v3(32), v3(32), v3(32)
        cntc, nbc, pend = AT(1), AT(1), AT(1)
        nb8 = AT(8)
        triex = AT(32)
        ps64 = AT(32)
        cmpe = AT(NBLK)
        bexpf = AT(NBLK)
        dst_r, dst_b = AT(8), AT(8)
        dst_ri = AT(8).bitcast(I32)
        place = AR(12288, 8 * BS).rearrange("p (c n) -> p c n", c=8)
        block_tok = AR(12288 + 8 * BS, 8 * (NBLK + 2)).rearrange("p (c n) -> p c n", c=8)
        bexp_i = AT(NBLK).bitcast(I32)
        slot_i = AT(NBLK + 2).bitcast(I32)
        dst_i = AT(8).bitcast(I32)
        idxc = AT(WS).bitcast(I32)
        nblkf = AT(1)
        nblk_i = AT(1).bitcast(I32)
        tanhg = AT(2 * 128).rearrange("p (u n) -> p u n", u=2)
        acth = AT(2 * 128).rearrange("p (u n) -> p u n", u=2)
        ahh, ahl, wdh, wdl, yb = (t[:, :].rearrange("p (u n) -> p u n", u=2) for t in (ahh_, ahl_, wdh_, wdl_, yb_))
        xg = raw[:, :].rearrange("p (u n) -> p u n", u=WS)
        r12 = AR(0, 8192).rearrange("p (t k n) -> p t k n", t=NT, k=2)
        ssf, msf, rsf = AT(NT), AT(NT), AT(NT)

        G = [ctx.enter_context(nc.psum_tensor(f"G{i}", [P, 512], F32)) for i in range(GRING)]
        SA = [ctx.enter_context(nc.psum_tensor(f"SA{i}", [P, 512], F32)) for i in range(2)]
        PB = [ctx.enter_context(nc.psum_tensor(f"PB{i}", [P, 512], F32)) for i in range(2)]
        OB = ctx.enter_context(nc.psum_tensor("OB", [P, 512], F32))

        SPL = {p: n for n, p in enumerate(split_pieces())}
        ORDER = all_pieces()

        def wait_group(eng, what, i):
            eng.wait_ge(S("group_filled"), GIDX[what, i] + 1)
            return G[GIDX[what, i] % GRING]

        def free_group(ins, what, i):
            ins.then_inc(S("bank_freed_" + GROUPS[GIDX[what, i]][2]), 1)

        def wait_freed(eng, what, i):
            e, n = freed_count(GIDX[what, i])
            eng.wait_ge(S("bank_freed_" + e), n)

        def wait_used(eng, p):
            eng.wait_ge(S("group_filled"), LAST[p] + 1)

        def split_slot(s):
            a = (s % 2) * PIECE
            return slice(a, a + PIECE)

        def raw_slot(p):
            if p[0] == "mod":
                n, slot = p[1], mraw[:, (p[1] % 2) * PIECE:(p[1] % 2 + 1) * PIECE]
                return slot, S(f"mod_loaded{n % 2}"), n // 2 + 1
            n = SPL[p]
            return raw[:, (n % 2) * PIECE:(n % 2 + 1) * PIECE], S(f"raw_loaded{n % 2}"), n // 2 + 1

        def wait_raw(eng, p):
            slot, loaded, count = raw_slot(p)
            eng.wait_ge(loaded, 16 * count)
            return slot

        units = [(ty, q, h) for ty in range(2) for q in range(NT) for h in range(NH)]
        munits = [(h, q) for h in range(MH) for q in range(NT)]
        aunits = [(q, h) for q in range(NT) for h in range(AH)]
        M0, A0 = len(units), len(units) + len(munits)
        MSCALE = 0.25 * 128 ** -0.5
        ASCALE = 192 ** -0.5

        def bc4(a):
            return a.unsqueeze(3).to_broadcast([P, NT, NEG_, EG])

        XT = [G[0], G[1]]
        GB, UB = [G[2], SA[0]], [SA[1], PB[0]]
        YB = [PB[1], OB]

        def SPsq(f):
            return AR(10368 + 512 * f, 512) if f < 3 else PTs[:, 0, :]

        block = ctx.enter_context(nc.Block())

        @block.sync
        def _(sp):
            for t in range(NT):
                sp.dma_start(Xv[:, t:t + 1, :], x.rearrange("(t p) n -> p t n", p=P)[:, t:t + 1, :]).then_inc(S(f"x_loaded{t}"), 16)
            sp.dma_start(con[:, :], con_d).then_inc(S("con_loaded"), 16)
            sp.dma_start(par[:, :], par_d).then_inc(S("par_loaded"), 16)
            sp.dma_start(smw, smw_d).then_inc(S("smw_loaded"), 16)
            for n, p in enumerate(ORDER):
                if p == ("bg", 0):
                    sp.wait_ge(S("bias_loaded"), 16)
                    for k in range(MIN_BLK * BS, NBLK * BS, T):
                        sp.dma_start(y_rows[k:k + T, :].rearrange("(t p) n -> p t n", p=P), AR(0, 4096).rearrange("p (t n) -> p t n", t=NT)).then_inc(S("rows_filled"), 16)
                if p[0] == "mod":
                    if p[1] == 0:
                        wait_group(sp, "wo", 0)
                    if p[1] >= 2:
                        sp.wait_ge(S("mod_summed"), p[1] - 1)
                elif SPL[p] >= 2:
                    sp.wait_ge(S("low_split"), SPL[p] - 1)
                slot, loaded, _ = raw_slot(p)
                sp.dma_start(slot, wp[n]).then_inc(loaded, 16)
                if p == ("qk", 0):
                    wait_freed(sp, "mod", MOD_PIECES - 1)
                    wait_group(sp, "down", 0)
                    sp.wait_ge(S("rows_filled"), 16 * (NBLK - MIN_BLK) * BS // T)
                    sp.dma_start(par[:, 0:PAR2["_"][1]], par2_d).then_inc(S("par2_loaded"), 16)
                    sp.dma_start(smw2, smw2_d).then_inc(S("smw2_loaded"), 16)
                if p == ("om", 0):
                    sp.wait_ge(S("rows_normed"), 3 * NT)
                    sp.dma_start(x_spill, X[:, :]).then_inc(S("x_spilled"), 16)
                if p == ("vm", 0):
                    wait_freed(sp, "h2", KT - 1)
                    sp.wait_ge(S("qk_done"), 8)
                    sp.dma_start(causal, tab2_d[:, 256:768]).then_inc(S("causal_loaded"), 16)
                if p == ("qr",):
                    wait_freed(sp, "bm", 7)
                    sp.wait_ge(S("kr_normed"), 1)
                    sp.dma_start(AR(12288, 256), tab2_d[:, 0:256]).then_inc(S("cos_loaded"), 16)
                if p == ("va",):
                    wait_group(sp, "krT", 0)
                    wait_group(sp, "cT2", 4)
                    sp.dma_start(chunk, tab2_d[:, 768:1280]).then_inc(S("chunk_loaded"), 16)
                if p == ("wout", 0):
                    sp.wait_ge(S("values_summed"), A0 + len(aunits))
                    sp.dma_start(X[:, :], x_spill).then_inc(S("x_back"), 16)
                if n == 1:
                    sp.wait_ge(S("sml_done"), 1)
                    sp.dma_start(AR(0, BIAS["_"][1]), bias_d).then_inc(S("bias_loaded"), 16)
            wait_freed(sp, "ba", 7)
            sp.dma_start(tab3, tab3_d).then_inc(S("tab3_loaded"), 16)
            sp.wait_ge(S("rows_normed"), 4 * NT)
            sp.dma_start(xn_rows.rearrange("(t p) n -> p t n", p=P), hraw3).then_inc(S("xn_stored"), 16)
            sp.wait_ge(S("xn_stored"), 16)
            sp.wait_ge(S("bexp_ready"), 1)
            blocks = sp.value_load(nblk_i[0:1, :], min_val=0, max_val=NBLK)
            with sp.Fori(0, NBLK // WS) as i:
                for v in range(WS):
                    with sp.If(WS * i + v < blocks):
                        e = sp.value_load(bexp_i[0:1, bass.ds(WS * i + v, 1)], min_val=0, max_val=NE - 1)
                        sp.wait_ge(S("up_ready"), WS * i + v + 1)
                        sp.dma_start(wgu[v].rearrange("p (o n) -> p o n", o=1),
                                     wexp[bass.ds(e, 1), :, 0:2 * PIECE].rearrange("o p n -> p o n")).then_inc(S(f"gu_loaded{v}"), 16)
                        sp.wait_ge(S("down_low_p"), WS * i + v + 1)
                        sp.wait_ge(S("down_low_v"), WS * i + v + 1)
                        sp.dma_start(wdn[v].rearrange("p (o n) -> p o n", o=1),
                                     wexp[bass.ds(e, 1), :, 2 * PIECE:WE].rearrange("o p n -> p o n")).then_inc(S(f"down_loaded{v}"), 16)
            for t in range(NT):
                sp.wait_ge(S("out_ready"), t + 1)
                sp.dma_start(out[t * P:(t + 1) * P, :], Xv[:, t, :]).then_inc(S("stored"), 16)
            sp.wait_ge(S("stored"), 16 * NT)

        @block.gpsimd
        def _(pool):
            c = [0]

            def own(ins):
                c[0] += 1
                ins.then_inc(S("pool_step"), 1)
                pool.wait_ge(S("pool_step"), c[0])

            def low(p):
                s = SPL[p]
                pool.wait_ge(S("high_split"), s + 1)
                pool.tensor_tensor(wl[:, split_slot(s)], wait_raw(pool, p), wh[:, split_slot(s)].bitcast(F32),
                                   ALU.subtract).then_inc(S("low_split"), 1)

            def rstd_of(dst, tmp, src, n, width):
                own(pool.tensor_scalar(tmp, src, 1.0 / width, EPS, ALU.mult, ALU.add))
                return pool.tensor_tensor(dst, tmp, mhalf.to_broadcast([P, n]), ALU.pow)

            sp_list = split_pieces()
            pool.wait_ge(S("con_loaded"), 16)
            pool.wait_ge(S("ss_x"), 1)
            pool.wait_ge(S("ss_last"), 1)
            rstd_of(rstd, ms, ss, NT, D).then_inc(S("rstd_x"), 1)
            pool.wait_ge(S("smh_done"), 1)
            pool.tensor_tensor(sml[:, 0:SMW["_"][1]], smw, smh[:, 0:SMW["_"][1]].bitcast(F32), ALU.subtract).then_inc(S("sml_done"), 1)
            for p in sp_list[:5]:
                low(p)
            pool.wait_ge(S("ss_k"), 1)
            rstd_of(rqk[:, 0:16], msqk[:, 0:16], ssqk[:, 0:16], 16, HD).then_inc(S("rstd_k"), 1)
            low(sp_list[5])
            for j in range(2):
                pool.wait_ge(S("ss_q"), j + 1)
                rq, mq, sq = (t[:, 16:48].rearrange("p (t c) -> p t c", t=NT)[:, :, 4 * j:4 * j + 4] for t in (rqk, msqk, ssqk))
                own(pool.tensor_scalar(mq, sq, 1.0 / HD, EPS, ALU.mult, ALU.add))
                pool.tensor_tensor(rq, mq, mhalf.unsqueeze(2).to_broadcast([P, NT, 4]), ALU.pow).then_inc(S("rstd_q"), 1)
                low(sp_list[6 + j])
            low(sp_list[8])
            pool.wait_ge(S("ss_kc"), 1)
            own(pool.tensor_scalar(msk[0:32, :], ssk[0:32, :], 1.0 / HD, EPS, ALU.mult, ALU.add))
            pool.tensor_tensor(rsk[0:32, :], msk[0:32, :], mhalf[0:32, :].to_broadcast([32, 2]), ALU.pow).then_inc(S("rstd_kc"), 1)
            for p in sp_list[9:16]:
                low(p)
            pool.wait_ge(S("ss_attn"), 1)
            rstd_of(rqk[:, 0:4], msqk[:, 0:4], ssqk[:, 0:4], NT, 512).then_inc(S("rstd_attn"), 1)
            wait_freed(pool, "csq", 0)
            rstd_of(rqk[:, 4:8], msqk[:, 4:8], ssqk[:, 4:8], NT, 512).then_inc(S("rstd_conv"), 1)
            for p in sp_list[16:20]:
                low(p)
            pool.wait_ge(S("ss_x"), 2)
            pool.wait_ge(S("ss_last"), 2)
            rstd_of(rstd, ms, ss, NT, D).then_inc(S("rstd_x"), 1)
            NB1 = len(first_pieces()) + len(ffn_pieces())
            for p in sp_list[20:NB1]:
                low(p)
            pool.wait_ge(S("ss_x"), 3)
            pool.wait_ge(S("ss_last"), 3)
            rstd_of(rstd2, ms2, ss2, NT, D).then_inc(S("rstd_x"), 1)
            pool.wait_ge(S("smh_done"), 2)
            pool.tensor_tensor(sml[:, :], smw2, smh[:, :].bitcast(F32), ALU.subtract).then_inc(S("sml_done"), 1)
            NC3 = NB1 + 15
            for p in sp_list[NB1:NC3]:
                low(p)
            low(sp_list[NC3])
            pool.wait_ge(S("ss_c"), 1)
            own(pool.tensor_scalar(msc[:, 0:4], ssc[:, 0:4], 1.0 / CQ, EPS, ALU.mult, ALU.add))
            own(pool.tensor_scalar(msc[:, 4:8], ssc[:, 4:8], 1.0 / CKV, EPS, ALU.mult, ALU.add))
            pool.tensor_tensor(rsc, msc, mhalf.to_broadcast([P, 8]), ALU.pow).then_inc(S("rstd_c"), 1)
            for p in sp_list[NC3 + 1:]:
                low(p)
            pool.wait_ge(S("ss_x"), 4)
            pool.wait_ge(S("ss_last"), 4)
            rstd_of(rstd2, ms2, ss2, NT, D).then_inc(S("rstd_x"), 1)
            pool.wait_ge(S("slot_idx_ready"), 1)
            pool.wait_ge(S("bexp_ready"), 1)
            pool.wait_ge(S("xn_stored"), 16)
            blocks = pool.value_load(nblk_i[0:1, :], min_val=0, max_val=NBLK)

            def gather(b, u, turn):
                if turn is not None:
                    pool.wait_ge(S("xt_ready"), turn)
                pool.tensor_copy(idxc[0:BS, u:u + 1], slot_i[0:BS, bass.ds(b, 1)]).then_inc(S("idx_ready"), 1)
                pool.wait_ge(S("idx_ready"), b + 1)
                pool.sem_inc(S("gather_turn"), 1)
                pool.indirect_dma_start(xg[0:BS, u, :], None, xn_rows, bass.IndirectOffsetOnAxis(ap=idxc[0:BS, u:u + 1], axis=0))                    .then_inc(S(f"xg_loaded{u}"), 16)

            gather(0, 0, None)
            gather(1, 1, None)
            with pool.Fori(0, NBLK // WS) as i:
                for v in range(WS):
                    with pool.If(WS * i + v < blocks):
                        b, u = WS * i + v, v % 2
                        gather(b + 2, (v + 2) % WS, b + 3)
                        pool.wait_ge(S("down_high"), b + 1)
                        pool.tensor_tensor(wdl[:, u, 0:1024], wdn[v][:, 0:1024], wdh[:, u, 0:1024].bitcast(F32), ALU.subtract).then_inc(S("down_low_p"), 1)
            for u in range(2):
                pool.wait_ge(S(f"y_stored{u}"), 16 * (NBLK // 2) + 16)
            for t in range(NT):
                for k in range(2):
                    pool.indirect_dma_start(r12[:, t, k, :], None, y_rows, bass.IndirectOffsetOnAxis(ap=dst_i[:, 4 * k + t:4 * k + t + 1], axis=0))\
                        .then_inc(S(f"picked{t}"), 16)
            for t in range(NT):
                pool.wait_ge(S("ss_f"), t + 1)
                own(pool.tensor_scalar(msf[:, t:t + 1], ssf[:, t:t + 1], 1.0 / D, EPS, ALU.mult, ALU.add))
                pool.tensor_tensor(rsf[:, t:t + 1], msf[:, t:t + 1], mhalf, ALU.pow).then_inc(S("rstd_f"), 1)

        @block.scalar
        def _(act):
            c = [0]

            def own(ins):
                c[0] += 1
                ins.then_inc(S("act_step"), 1)
                act.wait_ge(S("act_step"), c[0])

            sp_list = split_pieces()

            def high(s):
                if s >= len(sp_list):
                    return
                if s >= 2:
                    wait_used(act, sp_list[s - 2])
                act.activation(wh[:, split_slot(s)], wait_raw(act, sp_list[s]), ACT.Copy).then_inc(S("high_split"), 1)

            def squares(n, junk, sums, updates):
                for t in range(NT - 1):
                    if n == 0:
                        act.wait_ge(S(f"x_loaded{t}"), 16)
                    elif t % 2 == 0:
                        wait_freed(act, *updates[t // 2])
                    ins = act.activation(junk[:, t, :], Xv[:, t, :], ACT.Square, accum_out=sums[:, t:t + 1])
                ins.then_inc(S("ss_x"), 1)

            def norm_rows(n, dst, factor):
                act.wait_ge(S("rstd_x"), n + 1)
                for t in (1, 2):
                    act.activation(dst[:, t, :], Xv[:, t, :], ACT.Copy, scale=factor[:, t:t + 1]).then_inc(S("rows_normed"), 1)

            def transposed_high(what, n, dst, scale):
                for f in range(n):
                    b = wait_group(act, what, f)
                    act.activation(dst[:, f, :], b[:, :], ACT.Copy, scale=scale[:, f:f + 1]).then_inc(S(what + "_high"), 1)

            squares(0, hraw, ss, None)
            act.wait_ge(S("par_loaded"), 16)
            act.activation(cond_t, cols(par, PAR, "c"), ACT.Tanh, scale=0.5).then_inc(S("cond_tanh"), 1)
            norm_rows(0, hraw, rstd)
            act.wait_ge(S("smw_loaded"), 16)
            act.activation(smh[:, 0:SMW["_"][1]], smw, ACT.Copy).then_inc(S("smh_done"), 1)
            high(0)
            act.wait_ge(S("par_loaded"), 16)
            transposed_high("h0", KT, Hhv, cols(par, PAR, "g_mix"))
            high(1)
            b = wait_group(act, "gl", 0)
            free_group(act.activation(gl_rows, b[0:24, :], ACT.Copy), "gl", 0)
            for s, what in enumerate(("kcvc", "ksvs", "kwvw")):
                if s:
                    high(s + 1)
                for t in range(2):
                    b = wait_group(act, what, t)
                    bv = b[:, :].rearrange("p (t n) -> p t n", t=2)
                    if s == 0:
                        ins = act.activation(Zk[:, 2 * t:2 * t + 2, 0:256], bv, ACT.Copy)
                    else:
                        act.activation(Zk[:, 2 * t:2 * t + 2, 128 + s * 128:256 + s * 128], bv[:, :, 0:128], ACT.Copy)
                        ins = act.activation(Zv[:, 2 * t:2 * t + 2, s - 1, :], bv[:, :, 128:256], ACT.Copy)
                    free_group(ins, what, t)
                if s == 0:
                    b = wait_group(act, "glT", 0)
                    own(act.activation(gates, b[:, 0:96].rearrange("p (t n) -> p t n", t=NT), ACT.Tanh, scale=0.5))
                    free_group(act.activation(gates, gates, ACT.Copy, scale=0.5, bias=0.5), "glT", 0)
            for j in range(2):
                high(4 + j)
                if j == 0:
                    wait_freed(act, "cT", 3)
                    for cc in range(2):
                        ins = act.activation(Yh[:, 0:1984].rearrange("p (c k g i) -> p c k g i", c=2, k=16, g=2)[:, cc],
                                             AR(14464, 1984).rearrange("p (c g k i) -> p c k g i", c=2, g=2, k=16)[:, cc], ACT.Copy)
                    ins.then_inc(S("blk_high"), 1)
                for t in range(2):
                    b = wait_group(act, ("q", j), t)
                    free_group(act.activation(Zq[:, 2 * t:2 * t + 2, j * 256:(j + 1) * 256], b[:, :].rearrange("p (t n) -> p t n", t=2), ACT.Copy), ("q", j), t)
            for s in range(6, 10):
                high(s)
            act.wait_ge(S("gelu_in"), 1)
            act.activation(cw[:, 512:760], cw[:, 256:504], ACT.Tanh, scale=0.7978845608028654).then_inc(S("gelu_tanh"), 1)
            act.wait_ge(S("cmp_shifted"), 1)
            act.activation(cpv, csv, ACT.Exp).then_inc(S("cmp_exp"), 1)

            def unit(u):
                act.wait_ge(S("score_biased"), u + 1)
                ty, q, h = units[u]
                nk = (q + 1) * P
                act.activation(SP[:, u % 2, 0:nk], SP[:, u % 2, 0:nk], ACT.Exp, scale=-1.0, bias=nmax[:, u % 2:u % 2 + 1],
                               accum_out=rsum[:, ((u // 8) % 2) * 8 + h:((u // 8) % 2) * 8 + h + 1]).then_inc(S("probs_ready"), 1)

            for t in range(len(units) + 3):
                if t % 8 == 0 and t < 48:
                    high(10 + t // 8)
                if t < len(units):
                    unit(t)
                if t % 4 == 3 and t < 48 and (t // 4) % 6 < 2:
                    g = t // 4
                    f = 2 * (g // 6) + g % 6
                    b = wait_group(act, "hc", f)
                    if f >= 2:
                        wait_freed(act, "cg", f - 2)
                    free_group(act.activation(ctmp_h[:, f % 2, :], b[:, :], ACT.Copy), "hc", f)
                if t in (52, 54, 56, 58):
                    f = (t - 52) // 2
                    wait_freed(act, "bg", 3)
                    if f < 3:
                        act.activation(SPsq(f), conv[:, f, :], ACT.Square).then_inc(S("conv_sq"), 1)
                    act.activation(Yhv[:, 4 + f, :], conv[:, f, :], ACT.Copy, scale=cols(par, PAR, "g_out")[:, 4 + f:5 + f]).then_inc(S("conv_high"), 1)
            act.wait_ge(S("values_summed"), len(units))
            act.activation(SPsq(3), conv[:, 3, :], ACT.Square).then_inc(S("conv_sq"), 1)
            act.wait_ge(S("attn_sum"), NT * 2)
            for t in range(NT):
                ins = act.activation(kT[:, t, :], Oat[:, t, :], ACT.Square, accum_out=ssqk[:, t:t + 1])
            ins.then_inc(S("ss_attn"), 1)
            high(16)
            transposed_high("aT", 4, Yhv, cols(par, PAR, "g_out"))
            high(17)
            high(18)
            high(19)
            squares(1, hraw, ss, [("wo", 13), ("wo", 15)])
            norm_rows(1, hraw, rstd)
            transposed_high("h1", KT, Hhv, cols(par, PAR, "g_ffn"))
            s = 20
            for r in range(FQ):
                for j in range(4):
                    high(s)
                    s += 1
                    for f in range(2):
                        i = (r * 4 + j) * 2 + f
                        b = wait_group(act, "up", i)
                        if i >= 2:
                            act.wait_ge(S("ffn_sq"), i - 1)
                        ins = act.activation(frelu[:, i % 2, :], b[:, :], ACT.Relu)
                        free_group(ins, "up", i)
                        e, n = freed_count(GIDX["up", i])
                        act.wait_ge(S("bank_freed_a"), n)
                        act.activation(Yhv[:, 2 * j + f, :], frelu[:, i % 2, :], ACT.Square).then_inc(S("ffn_high"), 1)
                for j in range(4):
                    high(s)
                    s += 1

            NB1 = len(first_pieces()) + len(ffn_pieces())
            assert s == NB1 + 1
            squares(2, hraw2, ss2, [("down", 30), ("down", 31)])
            norm_rows(2, hraw2, rstd2)
            act.wait_ge(S("smw2_loaded"), 16)
            act.activation(smh[:, :], smw2, ACT.Copy).then_inc(S("smh_done"), 1)
            act.wait_ge(S("aff_ready"), 1)
            for f in range(KT):
                b = wait_group(act, "h2", f)
                act.activation(Hhv[:, f, :], b[:, :], ACT.Identity, scale=aff1[:, f:f + 1], bias=modv[:, 0, f:f + 1]).then_inc(S("h2_high"), 1)
            for i in range(8):
                if i % 2 == 0:
                    high(s)
                    s += 1
                b = wait_group(act, "qk", i)
                if i == 0:
                    act.wait_ge(S("xpad_zeroed"), 1)
                if i >= 2:
                    act.wait_ge(S("conv2_done"), i - 1)
                free_group(act.activation(xpad[:, i % 2, 3:515], b[:, :], ACT.Copy), "qk", i)
                if i >= 1:
                    act.wait_ge(S("conv2_done"), i)
                    act.activation(cth[:, (i - 1) % 2, :], cacc[:, (i - 1) % 2, :], ACT.Tanh, scale=0.5).then_inc(S("conv2_tanh"), 1)
            high(s)
            s += 1
            act.wait_ge(S("conv2_done"), 8)
            act.activation(cth[:, 1, :], cacc[:, 1, :], ACT.Tanh, scale=0.5).then_inc(S("conv2_tanh"), 1)
            act.wait_ge(S("fabs_ready"), 1)
            own(act.activation(flog, fabs, ACT.Exp, scale=-1.0))
            act.activation(flog, flog, ACT.Ln, bias=1.0).then_inc(S("flog_ready"), 1)
            for j in range(4):
                if j:
                    high(s)
                    s += 1
                for tp in range(2):
                    b = wait_group(act, "om", 2 * j + tp)
                    free_group(act.activation(To[:, 2 * tp:2 * tp + 2, j * PC:(j + 1) * PC], b[:, :].rearrange("p (t n) -> p t n", t=2), ACT.Tanh, scale=0.5), "om", 2 * j + tp)
            act.wait_ge(S("x_spilled"), 16)
            for j in range(4):
                high(s)
                s += 1
                for tp in range(2):
                    b = wait_group(act, "vm", 2 * j + tp)
                    free_group(act.activation(vm[:, 2 * tp:2 * tp + 2, j * PC:(j + 1) * PC], b[:, :].rearrange("p (t n) -> p t n", t=2), ACT.Copy), "vm", 2 * j + tp)

            def munit(u):
                h, q = munits[u]
                nk = (q + 1) * P
                act.wait_ge(S("decay_biased"), u + 1)
                act.activation(Eb[:, u % 2, 0:nk], Eb[:, u % 2, 0:nk], ACT.Exp, scale=-1.0, bias=nm[:, u:u + 1]).then_inc(S("decay_ready"), 1)
                act.activation(emn[:, u:u + 1], Bc[:, q, h:h + 1], ACT.Exp, scale=-1.0, bias=nm[:, u:u + 1]).then_inc(S("floor_ready"), 1)

            for t in range(len(munits) + 3):
                if t % 6 == 0 and t < 18:
                    high(s)
                    s += 1
                if t < len(munits):
                    munit(t)
                if t % 3 == 2 and t < 18:
                    i = t // 3
                    j, tp = divmod(i, 2)
                    b = wait_group(act, "c3", i)
                    free_group(act.activation(c3[:, 2 * tp:2 * tp + 2, j * PC:(j + 1) * PC], b[:, :].rearrange("p (t n) -> p t n", t=2), ACT.Copy), "c3", i)
            wait_freed(act, "c3", 5)
            for t in range(NT):
                own(act.activation(Eb[:, 0, 0:CQ], c3[:, t, 0:CQ], ACT.Square, accum_out=ssc[:, t:t + 1]))
                own(act.activation(Eb[:, 0, 0:CKV], c3[:, t, CQ:CQ + CKV], ACT.Square, accum_out=ssc[:, 4 + t:5 + t]))
            act.activation(ssc_done, mhalf, ACT.Copy).then_inc(S("ss_c"), 1)
            for f in range(KT):
                b = wait_group(act, "yT", f)
                act.activation(Yhv[:, f, :], b[:, :], ACT.Copy, scale=0.5).then_inc(S("yT_high"), 1)
            for j in range(4):
                high(s)
                s += 1
                for f in range(2):
                    i = 2 * j + f
                    b = wait_group(act, "gm", i)
                    if i >= 2:
                        wait_freed(act, "bm", i - 2)
                    free_group(act.activation(tg[:, f, :], b[:, :], ACT.Tanh, scale=0.5), "gm", i)
                high(s)
                s += 1
            for f in range(5):
                b = wait_group(act, "cT2", f)
                act.activation(Ch[:, f, :], b[:, :], ACT.Copy, scale=cols(par, PAR2, "g_cq")[:, f:f + 1] if f < 3 else cols(par, PAR2, "g_ckv")[:, f - 3:f - 2]).then_inc(S("cT2_high"), 1)
            for j in range(2):
                high(s)
                s += 1
                for h in range(4 * j, 4 * j + 4):
                    b = wait_group(act, "qn", h)
                    free_group(act.activation(qn[:, h, :], b[:, :], ACT.Copy), "qn", h)
            high(s)
            s += 1
            high(s)
            s += 1
            for i in range(8):
                b = wait_group(act, "va", i)
                free_group(act.activation(va[:, i // 2, (i % 2) * 512:(i % 2 + 1) * 512], b[:, :], ACT.Copy), "va", i)
            high(s)
            s += 1
            for h in range(AH):
                b = wait_group(act, "kn", h)
                free_group(act.activation(kn[:, h, :], b[:, :], ACT.Copy), "kn", h)

            def aunit(u):
                q, h = aunits[u]
                nk = (q + 1) * P
                act.wait_ge(S("score_biased"), A0 + u + 1)
                act.activation(SP3[:, u % 2, 0:nk], SP3[:, u % 2, 0:nk], ACT.Exp, scale=-1.0, bias=nmax2[:, u % 2:u % 2 + 1],
                               accum_out=rsum2[:, (q % 2) * 8 + h:(q % 2) * 8 + h + 1]).then_inc(S("probs_ready"), 1)

            for t in range(len(aunits) + 4):
                if t < len(aunits):
                    aunit(t)
                if t >= 11 and (t - 11) % 8 == 0:
                    q = (t - 11) // 8
                    for i in range(2):
                        b = wait_group(act, "yaT", 2 * q + i)
                        act.activation(Yhv[:, 4 * i:4 * i + 4, q * P:(q + 1) * P], b[:, :].rearrange("p (f n) -> p f n", f=4), ACT.Copy).then_inc(S("yaT_high"), 1)
            for j in range(4):
                high(s)
                s += 1
                for f in range(2):
                    i = 2 * j + f
                    b = wait_group(act, "ga", i)
                    if i >= 2:
                        wait_freed(act, "ba", i - 2)
                    free_group(act.activation(tga[:, f, :], b[:, :], ACT.Tanh, scale=0.5), "ga", i)
                high(s)
                s += 1
            for f in range(KT):
                act.wait_ge(S("merged_done"), f + 1)
                act.activation(Hhv[:, f, :], merged[:, f, :], ACT.Copy).then_inc(S("merged_high"), 1)
            for i in range(2):
                b = wait_group(act, "g1r", i)
                free_group(act.activation(g1row[:, i * 512:(i + 1) * 512], b[:, :], ACT.Copy, scale=0.5), "g1r", i)
            while s < len(sp_list):
                high(s)
                s += 1
            squares(3, hraw3, ss2, [("wout", 6), ("wout", 7)])
            for i in range(2):
                b = wait_group(act, "g2r", i)
                free_group(act.activation(g2row[:, i * 512:(i + 1) * 512], b[:, :], ACT.Copy, scale=0.5), "g2r", i)
            norm_rows(3, hraw3, rstd2)
            for f in range(KT):
                b = wait_group(act, "h3", f)
                act.activation(Hhv[:, f, :], b[:, :], ACT.Identity, scale=aff2[:, f:f + 1], bias=modv[:, 3, f:f + 1]).then_inc(S("h3_high"), 1)
            act.wait_ge(S("group_shifted"), 1)
            act.activation(gex, gsh, ACT.Exp).then_inc(S("group_exp"), 1)
            act.wait_ge(S("second_ready"), 1)
            act.activation(e2, m2, ACT.Exp).then_inc(S("second_exp"), 1)
            act.wait_ge(S("bexp_ready"), 1)
            blocks = act.value_load(nblk_i[0:1, :], min_val=0, max_val=NBLK)
            with act.Fori(0, NBLK // WS) as i:
                for v in range(WS):
                    b, u = WS * i + v, v % 2
                    with act.If(b < blocks):
                        act.wait_ge(S(f"down_loaded{v}"), 16 * i + 16)
                        act.wait_ge(S("y_ready"), b + 3)
                        act.activation(wdh[:, u, :], wdn[v], ACT.Copy).then_inc(S("down_high"), 1)
                        act.wait_ge(S("gate_ready"), b + 1)
                        act.wait_ge(S("tanh_free"), b + 3)
                        act.activation(tanhg[:, u, :], GB[u][:, 0:128], ACT.Tanh, scale=0.5).then_inc(S("tanh_ready"), 1)
                        act.wait_ge(S("y_copied"), b + 5)
                        act.dma_start(y_rows[bass.ds(b * BS, BS), :], yb[0:BS, u, :]).then_inc(S(f"y_stored{u}"), 16)
                    with act.Else():
                        act.sem_inc(S(f"y_stored{u}"), 16)
            for t in range(NT):
                act.wait_ge(S("x_final"), t + 1)
                act.activation(r12[:, t, 0, :], Xv[:, t, :], ACT.Square, accum_out=ssf[:, t:t + 1]).then_inc(S("ss_f"), 1)

        @block.vector
        def _(dve):
            c = [0]

            def own(ins):
                c[0] += 1
                ins.then_inc(S("dve_step"), 1)
                dve.wait_ge(S("dve_step"), c[0])

            def square_last(dst, sums, *update):
                if update:
                    wait_freed(dve, *update)
                else:
                    for t in (0, NT - 1):
                        dve.wait_ge(S(f"x_loaded{t}"), 16)
                dve.tensor_tensor_reduce(dst[:, NT - 1, :], Xv[:, NT - 1, :], Xv[:, NT - 1, :], 1.0, 0.0, ALU.mult, ALU.add,
                                         sums[:, NT - 1:NT]).then_inc(S("ss_last"), 1)

            def norm_rows(n, dst, factor):
                dve.wait_ge(S("rstd_x"), n + 1)
                for t in (0, 3):
                    dve.tensor_scalar(dst[:, t, :], Xv[:, t, :], factor[:, t:t + 1], None, ALU.mult).then_inc(S("rows_normed"), 1)

            def transposed_low(what, n, dst, high, scale):
                for f in range(n):
                    b = wait_group(dve, what, f)
                    dve.wait_ge(S(what + "_high"), f + 1)
                    free_group(dve.scalar_tensor_tensor(dst[:, f, :], b[:, :], scale[:, f:f + 1], high[:, f, :].bitcast(F32),
                                                        ALU.mult, ALU.subtract), what, f)

            dve.wait_ge(S("con_loaded"), 16)
            dve.wait_ge(S("par_loaded"), 16)
            square_last(hraw, ss)
            norm_rows(0, hraw, rstd)
            transposed_low("h0", KT, Hlv, Hhv, cols(par, PAR, "g_mix"))
            wait_freed(dve, "kcvc", 1)
            for u in range(2):
                ins = dve.tensor_copy(cdup[:, :, :, u, :], Zk[:, :, 0:256].rearrange("p t (c d) -> p t c d", c=4))
            ins.then_inc(S("cdup_ready"), 1)
            wait_freed(dve, "kwvw", 1)
            kview = Zk[:, :, 256:512]
            ksq = AR(14464, 1024).rearrange("p (t n) -> p t n", t=NT)
            own(dve.tensor_tensor(ksq, kview, kview, ALU.mult))
            dve.tensor_reduce(ssqk[:, 0:16].rearrange("p (c o) -> p c o", o=1), AR(14464, 1024).rearrange("p (c d) -> p c d", d=HD), AX.X, ALU.add).then_inc(S("ss_k"), 1)
            dve.wait_ge(S("ss_k"), 1)
            pe = cols(par, PAR, "pe").rearrange("p (c b a) -> p c b a", c=2, b=2)
            for c4 in range(4):
                b = wait_group(dve, "cT", c4)
                for half in range(2):
                    r = slice(64 * half, 64 * half + 64)
                    for a in range(2):
                        src = b[r, 16 * a:16 * a + 496].rearrange("p (i s) -> p s i", s=16)[:, half:16:2, :]
                        ins = dve.tensor_tensor(blkt[r, c4, a, :, :], src,
                                                pe[r, c4 // 2, a, :].unsqueeze(2).to_broadcast([64, 8, CMP_I]), ALU.add)
                free_group(ins, "cT", c4)
            dve.wait_ge(S("rstd_k"), 1)
            for u in range(2):
                ins = dve.tensor_tensor(kdup[:, :, :, u, :], kview.rearrange("p t (c d) -> p t c d", d=HD),
                                        rqk[:, 0:16].rearrange("p (t c) -> p t c", t=NT).unsqueeze(3).to_broadcast([P, NT, 4, HD]), ALU.mult)
            ins.then_inc(S("kdup_ready"), 1)
            dve.wait_ge(S("blk_high"), 1)
            for cc in range(2):
                ins = dve.tensor_tensor(Yl[:, 0:1984].rearrange("p (c k g i) -> p c k g i", c=2, k=16, g=2)[:, cc],
                                        AR(14464, 1984).rearrange("p (c g k i) -> p c k g i", c=2, g=2, k=16)[:, cc],
                                        Yh[:, 0:1984].bitcast(F32).rearrange("p (c k g i) -> p c k g i", c=2, k=16, g=2)[:, cc], ALU.subtract)
            ins.then_inc(S("blk_low"), 1)
            dve.wait_ge(S("blk_low"), 1)
            qsq = AR(14464, 2048).rearrange("p (t c d) -> p t c d", t=NT, c=8)
            qview = AR(5248, 2048).rearrange("p (t c d) -> p t c d", t=NT, c=8)
            for j in range(2):
                wait_freed(dve, ("q", j), 1)
                own(dve.tensor_tensor(qsq[:, :, 4 * j:4 * j + 4], qview[:, :, 4 * j:4 * j + 4], qview[:, :, 4 * j:4 * j + 4], ALU.mult))
                dve.tensor_reduce(ssqk[:, 16:48].rearrange("p (t c o) -> p t c o", t=NT, o=1)[:, :, 4 * j:4 * j + 4], qsq[:, :, 4 * j:4 * j + 4],
                                  AX.X, ALU.add).then_inc(S("ss_q"), 1)
            gk = cols(par, PAR, "g_k")
            for c4 in range(4):
                b = wait_group(dve, "kT", c4)
                free_group(dve.tensor_scalar(kT[:, c4, :], b[:, :], gk[:, 1 + c4 // 2:2 + c4 // 2], None, ALU.mult), "kT", c4)
            own(dve.memset(PTs[:, 0, :], 0.0))
            own(dve.memset(cw[:, 1280:1856], 0.0))
            for i in range(4):
                b = wait_group(dve, "cmp1", i)
                half = cpre[:, (i // 2) * 256:(i // 2 + 1) * 256]
                if i % 2 == 0:
                    free_group(dve.tensor_copy(half, b[0:62, 0:256]), "cmp1", i)
                else:
                    free_group(dve.tensor_tensor(half, half, b[0:62, 0:256], ALU.add), "cmp1", i)
                wait_freed(dve, "cmp1", i)
            dve.wait_ge(S("rstd_q"), 2)
            dve.tensor_tensor(AR(5248, 2048).rearrange("p (c d) -> p c d", d=HD), AR(5248, 2048).rearrange("p (c d) -> p c d", d=HD),
                              rqk[:, 16:48].unsqueeze(2).to_broadcast([P, 32, HD]), ALU.mult).then_inc(S("q_normed"), 1)
            hid, gin, gth = cw[:, 0:248], cw[:, 256:504], cw[:, 512:760]
            for i in range(4):
                b = wait_group(dve, "cmpT", i // 2)
                ins = dve.tensor_scalar(hid[:, i * 62:(i + 1) * 62], b[:, (i % 2) * 62:(i % 2 + 1) * 62], cols(par, PAR, "b_cmp1")[:, i:i + 1], None, ALU.add)
                if i % 2:
                    free_group(ins, "cmpT", i // 2)
            wait_freed(dve, "cmpT", 1)
            own(dve.tensor_tensor(gin, hid, hid, ALU.mult))
            own(dve.tensor_scalar(gin, gin, 0.044715, 1.0, ALU.mult, ALU.add))
            dve.tensor_tensor(gin, gin, hid, ALU.mult).then_inc(S("gelu_in"), 1)
            dve.wait_ge(S("gelu_tanh"), 1)
            own(dve.scalar_tensor_tensor(hid, gth, 1.0, hid, ALU.add, ALU.mult))
            dve.tensor_scalar(hid, hid, 0.5, None, ALU.mult).then_inc(S("gelu_done"), 1)
            b2k = cols(par, PAR, "b_cmp2").rearrange("p (c d) -> p c d", c=2)
            kcr = cw[0:32, 1280:1408].rearrange("p (g d) -> p g d", g=2)
            ksqr = cw[0:32, 1408:1536]
            kcd = cw[0:32, 1536:1792].rearrange("p (g u d) -> p g u d", g=2, u=2)
            kcT = cw[:, 1792:1856].rearrange("p (g i) -> p g i", g=2)
            VBD = PTs[:, 0, :].rearrange("p (g n) -> p g n", g=2)
            b = wait_group(dve, "cmpk", 0)
            ins = dve.tensor_tensor(kcr[0:31], b[0:31, 0:128].rearrange("p (g d) -> p g d", g=2),
                                    b2k[0:31, 0:1, :].to_broadcast([31, 2, HD]), ALU.add)
            free_group(ins, "cmpk", 0)
            wait_freed(dve, "cmpk", 0)
            own(dve.tensor_tensor(ksqr.rearrange("p (g d) -> p g d", g=2), kcr, kcr, ALU.mult))
            dve.tensor_reduce(ssk[0:32, :].unsqueeze(2), ksqr.rearrange("p (g d) -> p g d", g=2), AX.X, ALU.add).then_inc(S("ss_kc"), 1)
            b = wait_group(dve, "cmpv", 0)
            for r in range(4):
                ins = dve.tensor_tensor(VBD[32 * r:32 * r + 31, :, r * HD:(r + 1) * HD],
                                        b[32 * r:32 * r + 31, :].rearrange("p (g n) -> p g n", g=2)[:, :, r * HD:(r + 1) * HD],
                                        b2k[32 * r:32 * r + 31, 1:2, :].to_broadcast([31, 2, HD]), ALU.add)
            free_group(ins, "cmpv", 0)
            dve.wait_ge(S("rstd_kc"), 1)
            for u in range(2):
                ins = dve.tensor_tensor(kcd[:, :, u, :], kcr, rsk[0:32, :].unsqueeze(2).to_broadcast([32, 2, HD]), ALU.mult)
            ins.then_inc(S("kcd_ready"), 1)
            b = wait_group(dve, "cmpkT", 0)
            free_group(dve.tensor_scalar(kcT[:, :, :], b[:, 0:64].rearrange("p (g i) -> p g i", g=2), gk[:, 0:1], None, ALU.mult), "cmpkT", 0)
            for c4 in range(4):
                b = wait_group(dve, "qT", c4)
                free_group(dve.tensor_scalar(qT[:, c4, :], b[:, :], cols(par, PAR, "g_q"), 0.125, ALU.mult, ALU.mult), "qT", c4)
            dve.wait_ge(S("bias_loaded"), 16)
            sv, pv = (t.rearrange("p (q h i) -> p q h i", q=NT, h=8) for t in (csv, cpv))
            svr, pvr = (t.rearrange("p (c i) -> p c i", i=32) for t in (csv, cpv))
            for o in range(2):
                b = wait_group(dve, "cS", o)
                ins = dve.tensor_tensor(sv[:, :, o:8:2, :], b[:, :].rearrange("p (q h i) -> p q h i", q=NT, h=4), cmpb[:, :, o:8:2, :], ALU.add)
                free_group(ins, "cS", o)
            wait_freed(dve, "cS", 1)
            own(dve.tensor_reduce(cmaxn.unsqueeze(2), svr, AX.X, ALU.max))
            dve.tensor_tensor(svr, svr, cmaxn.unsqueeze(2).to_broadcast([P, 32, 32]), ALU.subtract).then_inc(S("cmp_shifted"), 1)
            dve.wait_ge(S("cmp_exp"), 1)
            dve.tensor_tensor(pv, pv, cmpm.unsqueeze(2).to_broadcast([P, NT, 8, 32]), ALU.mult).then_inc(S("cmp_p"), 1)
            dve.wait_ge(S("cmp_p"), 1)
            own(dve.tensor_reduce(csum.unsqueeze(2), pvr, AX.X, ALU.add))
            own(dve.tensor_scalar(csum, csum, 1e-30, None, ALU.max))
            own(dve.reciprocal(csum, csum))
            own(dve.tensor_tensor(ccoef.rearrange("p (q h) -> p q h", q=NT), csum.rearrange("p (q h) -> p q h", q=NT), gates[:, :, 0:24:3], ALU.mult))
            for i in range(2):
                b = wait_group(dve, "cP", i)
                free_group(dve.tensor_copy(SP[:, i, :], b[:, :]), "cP", i)
            for q in range(NT):
                b = wait_group(dve, "cO", q)
                ins = dve.tensor_tensor(Oat[:, q, :].rearrange("p (h d) -> p h d", h=8), b[:, :].rearrange("p (h d) -> p h d", h=8),
                                        ccoef[:, 8 * q:8 * q + 8].unsqueeze(2).to_broadcast([P, 8, HD]), ALU.mult)
                free_group(ins, "cO", q)
            wait_freed(dve, "cO", NT - 1)

            def biased(u):
                ty, q, h = units[u]
                nk = (q + 1) * P
                dve.wait_ge(S("scores_ready"), u + 1)
                if u >= 2:
                    dve.wait_ge(S("probs_transposed"), u - 1)
                dve.tensor_tensor_reduce(SP[:, u % 2, 0:nk], SA[u % 2][:, 0:nk], alibi[:, h, T - nk:T], -1.0, 3e38,
                                         ALU.add, ALU.min, nmax[:, u % 2:u % 2 + 1]).then_inc(S("score_biased"), 1)

            def copied(u):
                ty, q, h = units[u]
                nk = (q + 1) * P
                dve.wait_ge(S("probs_transposed"), u + 1)
                if u >= 2:
                    dve.wait_ge(S("values_summed"), u - 1)
                dve.tensor_copy(PTs[:, u % 2, 0:nk], PB[u % 2][:, 0:nk]).then_inc(S("pt_copied"), 1)

            def weighted(v):
                ty, q = divmod(v, NT)
                own(dve.reciprocal(ncoef, rsum[:, (v % 2) * 8:(v % 2) * 8 + 8]))
                own(dve.tensor_tensor(ncoef, ncoef, gates[:, q, 1 + ty:24:3], ALU.mult))
                dve.wait_ge(S("values_summed"), 8 * v + 8)
                ins = dve.tensor_tensor(otmp.rearrange("p (h d) -> p h d", h=8), OB[:, :].rearrange("p (h d) -> p h d", h=8),
                                        ncoef.unsqueeze(2).to_broadcast([P, 8, HD]), ALU.mult)
                ins.then_inc(S("out_freed"), 1)

            def summed(v):
                q = v % NT
                dve.wait_ge(S("out_freed"), v + 1)
                dve.tensor_tensor(Oat[:, q, :], Oat[:, q, :], otmp, ALU.add).then_inc(S("attn_sum"), 1)

            def conv_group(g):
                i, k = divmod(g, 6)
                f = 2 * i + k % 2
                cwt = cols(par, PAR, "conv_w").rearrange("p (f k) -> p f k", k=3)
                if k < 2:
                    return
                if k < 4:
                    b = wait_group(dve, "cg", f)
                    wait_freed(dve, "hc", f)
                    free_group(dve.tensor_tensor(ctmp_u, b[:, :], ctmp_h[:, f % 2, :], ALU.mult), "cg", f)
                    wait_freed(dve, "cg", f)
                    own(dve.tensor_scalar(conv[:, f, :], ctmp_u, cwt[:, f, 2:3], None, ALU.mult))
                    own(dve.scalar_tensor_tensor(conv[:, f, 1:T], ctmp_u[:, 0:T - 1], cwt[:, f, 1:2], conv[:, f, 1:T], ALU.mult, ALU.add))
                    own(dve.scalar_tensor_tensor(conv[:, f, 2:T], ctmp_u[:, 0:T - 2], cwt[:, f, 0:1], conv[:, f, 2:T], ALU.mult, ALU.add))
                else:
                    b = wait_group(dve, "bg", f)
                    ins = dve.tensor_tensor(conv[:, f, :], conv[:, f, :], b[:, :], ALU.mult)
                    free_group(ins, "bg", f)

            for t in range(len(units) + 3):
                v = (t - 2) // 8 - 1 if t >= 10 and (t - 2) % 8 == 0 else None
                if v is not None:
                    weighted(v)
                if t < len(units):
                    biased(t)
                if 0 <= t - 1 < len(units):
                    copied(t - 1)
                if t % 4 == 3 and t < 48:
                    conv_group(t // 4)
                if v is not None:
                    summed(v)

            go = cols(par, PAR, "g_out")
            for f in range(4):
                dve.wait_ge(S("conv_high"), f + 1)
                dve.scalar_tensor_tensor(Ylv[:, 4 + f, :], conv[:, f, :], go[:, 4 + f:5 + f], Yhv[:, 4 + f, :].bitcast(F32),
                                         ALU.mult, ALU.subtract).then_inc(S("conv_low"), 1)
            b = wait_group(dve, "csq", 0)
            free_group(dve.tensor_copy(ssqk[:, 4:8], b[:, 0:4]), "csq", 0)
            dve.wait_ge(S("rstd_attn"), 1)
            for t in range(NT):
                dve.tensor_scalar(kT[:, t, :], Oat[:, t, :], rqk[:, t:t + 1], None, ALU.mult).then_inc(S("attn_normed"), 1)
            transposed_low("aT", 4, Ylv, Yhv, go)
            dve.wait_ge(S("rstd_conv"), 1)
            for n in range(4):
                for tp in range(2):
                    i = 4 * n + 2 * tp
                    xs = Xv[:, 2 * tp:2 * tp + 2, n * PC:(n + 1) * PC]
                    b = wait_group(dve, "wo", i)
                    ins = dve.tensor_tensor(xs, xs, b[:, :].rearrange("p (t n) -> p t n", t=2), ALU.add)
                    free_group(ins, "wo", i)
                    wait_freed(dve, "wo", i)
                    b = wait_group(dve, "wo", i + 1)
                    for j in range(2):
                        xt = Xv[:, 2 * tp + j, n * PC:(n + 1) * PC]
                        ins = dve.scalar_tensor_tensor(xt, b[:, j * PC:(j + 1) * PC], rqk[:, 4 + 2 * tp + j:5 + 2 * tp + j], xt, ALU.mult, ALU.add)
                    free_group(ins, "wo", i + 1)
            square_last(hraw, ss, "wo", 15)
            norm_rows(1, hraw, rstd)
            transposed_low("h1", KT, Hlv, Hhv, cols(par, PAR, "g_ffn"))
            m = 0

            def mod_cols(m):
                b = wait_group(dve, "mod", m)
                ins = dve.tensor_tensor(modc[:, 2 * m:2 * m + 2], b[:, 0:2],
                                        cols(par, PAR, "mod_b")[:, 2 * m:2 * m + 2], ALU.add)
                free_group(ins, "mod", m)

            dve.wait_ge(S("cond_tanh"), 1)
            own(dve.scalar_tensor_tensor(cond_t, cond_t, 1.0, cols(par, PAR, "c"), ALU.add, ALU.mult))
            own(dve.tensor_scalar(condc, cond_t, 0.5, None, ALU.mult))

            def mod_part(m):
                w = wait_raw(dve, ("mod", m)).rearrange("p (k n) -> p k n", n=PC)
                if m >= 2:
                    wait_freed(dve, "mod", m - 2)
                a = macc[:, m % 2, :]
                own(dve.tensor_scalar(a, w[:, 0, :], condc[:, 0:1], None, ALU.mult))
                for k in range(1, KT - 1):
                    own(dve.scalar_tensor_tensor(a, w[:, k, :], condc[:, k:k + 1], a, ALU.mult, ALU.add))
                dve.scalar_tensor_tensor(a, w[:, KT - 1, :], condc[:, KT - 1:KT], a, ALU.mult, ALU.add).then_inc(S("mod_summed"), 1)

            for r in range(FQ):
                for j in range(4):
                    if m < MOD_PIECES:
                        mod_part(m)
                    for f in range(2):
                        i = (r * 4 + j) * 2 + f
                        wait_freed(dve, "up", i)
                        own(dve.tensor_tensor(fsq[:, i % 2, :], frelu[:, i % 2, :], frelu[:, i % 2, :], ALU.mult))
                        dve.wait_ge(S("ffn_high"), i + 1)
                        dve.tensor_tensor(Ylv[:, 2 * j + f, :], fsq[:, i % 2, :], Yhv[:, 2 * j + f, :].bitcast(F32), ALU.subtract).then_inc(S("ffn_sq"), 1)
                    if m < MOD_PIECES:
                        mod_cols(m)
                        m += 1
                for j in range(4):
                    if m < MOD_PIECES:
                        mod_part(m)
                    for tp in range(2):
                        i = (r * 4 + j) * 2 + tp
                        xs = Xv[:, 2 * tp:2 * tp + 2, j * PC:(j + 1) * PC]
                        b = wait_group(dve, "down", i)
                        ins = dve.tensor_tensor(xs, xs, b[:, :].rearrange("p (t n) -> p t n", t=2), ALU.add)
                        free_group(ins, "down", i)
                    if m < MOD_PIECES:
                        mod_cols(m)
                        m += 1

            square_last(hraw2, ss2, "down", 31)
            dve.wait_ge(S("ffn_high"), 32)
            own(dve.memset(xpad, 0.0))
            dve.wait_ge(S("par2_loaded"), 16)
            wait_freed(dve, "mod", MOD_PIECES - 1)
            own(dve.scalar_tensor_tensor(aff1, modv[:, 1, :], 1.0, cols(par, PAR2, "g_1"), ALU.add, ALU.mult))
            dve.scalar_tensor_tensor(aff2, modv[:, 4, :], 1.0, cols(par, PAR2, "g_2"), ALU.add, ALU.mult).then_inc(S("aff_ready"), 1)
            dve.wait_ge(S("aff_ready"), 1)
            norm_rows(2, hraw2, rstd2)
            ftmp = AR(17536, 1024).rearrange("p (r n) -> p r n", r=2)
            for f in range(KT):
                b = wait_group(dve, "h2", f)
                dve.wait_ge(S("h2_high"), f + 1)
                own(dve.tensor_scalar(ftmp[:, f % 2, :], b[:, :], aff1[:, f:f + 1], modv[:, 0, f:f + 1], ALU.mult, ALU.add))
                free_group(dve.tensor_tensor(Hlv[:, f, :], ftmp[:, f % 2, :], Hhv[:, f, :].bitcast(F32), ALU.subtract), "h2", f)
            wait_freed(dve, "h2", KT - 1)
            b = wait_group(dve, "if", 0)
            free_group(dve.tensor_copy(if_rows, b[0:8, :]), "if", 0)
            b = wait_group(dve, "ifT", 0)
            free_group(dve.tensor_tensor(ifr, b[:, 0:32].rearrange("p (t n) -> p t n", t=NT),
                                         cols(par, PAR2, "b_if").unsqueeze(1).to_broadcast([P, NT, 8]), ALU.add), "ifT", 0)
            wait_freed(dve, "ifT", 0)
            dve.scalar_tensor_tensor(fabs, ifr[:, :, 4:8], -1.0, ifr[:, :, 4:8], ALU.mult, ALU.max).then_inc(S("fabs_ready"), 1)
            own(dve.tensor_scalar(lf, ifr[:, :, 4:8], 0.0, None, ALU.min))
            dve.memset(xpad_done, 0.0).then_inc(S("xpad_zeroed"), 1)
            w4 = cols(par, PAR2, "conv_w2").rearrange("p (f k) -> p f k", k=4)
            b4 = cols(par, PAR2, "conv_b2")

            def silu_of(i):
                dve.wait_ge(S("conv2_tanh"), i + 1)
                dve.scalar_tensor_tensor(qkT[:, i, :], cth[:, i % 2, :], 1.0, cacc[:, i % 2, :], ALU.add, ALU.mult).then_inc(S("qk_done"), 1)

            for i in range(8):
                wait_freed(dve, "qk", i)
                xp, ac = xpad[:, i % 2, :], cacc[:, i % 2, :]
                if i >= 2:
                    dve.wait_ge(S("qk_done"), i - 1)
                own(dve.tensor_scalar(ac, xp[:, 3:515], w4[:, i, 3:4], b4[:, i:i + 1], ALU.mult, ALU.add))
                own(dve.scalar_tensor_tensor(ac, xp[:, 2:514], w4[:, i, 2:3], ac, ALU.mult, ALU.add))
                own(dve.scalar_tensor_tensor(ac, xp[:, 1:513], w4[:, i, 1:2], ac, ALU.mult, ALU.add))
                dve.scalar_tensor_tensor(ac, xp[:, 0:512], w4[:, i, 0:1], ac, ALU.mult, ALU.add).then_inc(S("conv2_done"), 1)
                if i:
                    silu_of(i - 1)
            silu_of(7)
            dve.wait_ge(S("flog_ready"), 1)
            dve.tensor_tensor(lf, lf, flog, ALU.subtract).then_inc(S("lf_ready"), 1)
            for j in range(4):
                wait_freed(dve, "om", 2 * j + 1)
                dve.tensor_scalar(To[:, :, j * PC:(j + 1) * PC], To[:, :, j * PC:(j + 1) * PC], 1.0, None, ALU.add).then_inc(S("ogate_done"), 1)
            b = wait_group(dve, "cum", 0)
            free_group(dve.tensor_copy(Bc, b[:, 0:16].rearrange("p (t n) -> p t n", t=NT)), "cum", 0)
            wait_freed(dve, "cum", 0)
            dve.tensor_tensor(cc_, ifr[:, :, 0:4], Bc, ALU.subtract).then_inc(S("c_ready"), 1)
            for h in range(MH):
                b = wait_group(dve, "crow", h)
                free_group(dve.tensor_copy(crow[:, h, :], b[:, :]), "crow", h)
            wait_freed(dve, "crow", MH - 1)
            dve.wait_ge(S("causal_loaded"), 16)
            dve.wait_ge(S("ogate_done"), 4)
            dve.wait_ge(S("qk_done"), 8)

            def mdecay(u):
                h, q = munits[u]
                nk = (q + 1) * P
                own(dve.tensor_tensor_reduce(Eb[:, u % 2, 0:nk], crow[:, h, 0:nk], causal[:, T - nk:T], -1.0, 3e38,
                                             ALU.add, ALU.min, nm[:, u:u + 1]))
                dve.tensor_scalar(nm[:, u:u + 1], nm[:, u:u + 1], 0.0, None, ALU.min).then_inc(S("decay_biased"), 1)

            def mscore(u):
                h, q = munits[u]
                nk = (q + 1) * P
                dve.wait_ge(S("scores_ready"), M0 + u + 1)
                dve.wait_ge(S("decay_ready"), u + 1)
                if u >= 2:
                    dve.wait_ge(S("probs_transposed"), M0 + u - 1)
                dve.tensor_tensor_reduce(SP2[:, u % 2, 0:nk], SA[u % 2][:, 0:nk], Eb[:, u % 2, 0:nk], MSCALE, 0.0,
                                         ALU.mult, ALU.add, den[:, u:u + 1]).then_inc(S("score_biased"), 1)
                dve.wait_ge(S("score_biased"), M0 + u + 1)
                own(dve.scalar_tensor_tensor(rr[:, u:u + 1], den[:, u:u + 1], -1.0, den[:, u:u + 1], ALU.mult, ALU.max))
                dve.wait_ge(S("floor_ready"), u + 1)
                own(dve.tensor_tensor(rr[:, u:u + 1], rr[:, u:u + 1], emn[:, u:u + 1], ALU.max))
                own(dve.reciprocal(rr[:, u:u + 1], rr[:, u:u + 1]))

            def mcopied(u):
                h, q = munits[u]
                nk = (q + 1) * P
                dve.wait_ge(S("probs_transposed"), M0 + u + 1)
                if u >= 2:
                    dve.wait_ge(S("values_summed"), M0 + u - 1)
                dve.tensor_copy(PT2[:, u % 2, 0:nk], PB[u % 2][:, 0:nk]).then_inc(S("pt_copied"), 1)

            def mout(u):
                h, q = munits[u]
                dve.wait_ge(S("values_summed"), M0 + u + 1)
                yt = To[:, q, h * MV:(h + 1) * MV]
                dve.scalar_tensor_tensor(yt, OB[:, 0:MV], rr[:, u:u + 1], yt, ALU.mult, ALU.mult).then_inc(S("m_out"), 1)

            mdecay(0)
            for t in range(len(munits) + 3):
                if 0 <= t - 3 < len(munits):
                    mout(t - 3)
                if t + 1 < len(munits):
                    mdecay(t + 1)
                if t < len(munits):
                    mscore(t)
                if 0 <= t - 1 < len(munits):
                    mcopied(t - 1)
            for f in range(KT):
                b = wait_group(dve, "yT", f)
                dve.wait_ge(S("yT_high"), f + 1)
                free_group(dve.scalar_tensor_tensor(Ylv[:, f, :], b[:, :], 0.5, Yhv[:, f, :].bitcast(F32), ALU.mult, ALU.subtract), "yT", f)
            dve.wait_ge(S("rstd_c"), 1)
            for t in range(NT):
                dve.tensor_scalar(c3[:, t, 0:CQ], c3[:, t, 0:CQ], rsc[:, t:t + 1], None, ALU.mult)
                ins = dve.tensor_scalar(c3[:, t, CQ:CQ + CKV], c3[:, t, CQ:CQ + CKV], rsc[:, 4 + t:5 + t], None, ALU.mult)
            ins.then_inc(S("kr_normed"), 1)
            for i in range(8):
                b = wait_group(dve, "bm", i)
                wait_freed(dve, "gm", i)
                free_group(dve.scalar_tensor_tensor(merged[:, i, :], tg[:, i % 2, :], 1.0, b[:, :], ALU.add, ALU.mult), "bm", i)
            for f in range(5):
                b = wait_group(dve, "cT2", f)
                dve.wait_ge(S("cT2_high"), f + 1)
                sc = cols(par, PAR2, "g_cq")[:, f:f + 1] if f < 3 else cols(par, PAR2, "g_ckv")[:, f - 3:f - 2]
                free_group(dve.scalar_tensor_tensor(Cl[:, f, :], b[:, :], sc, Ch[:, f, :].bitcast(F32), ALU.mult, ALU.subtract), "cT2", f)
            dve.wait_ge(S("cos_loaded"), 16)

            def rope(dst1, dst2, x1, x2, cs, sn, t1, t2):
                own(dve.tensor_tensor(t1, x1, cs, ALU.mult))
                own(dve.tensor_tensor(t2, x2, sn, ALU.mult))
                own(dve.tensor_tensor(dst1, t1, t2, ALU.subtract))
                own(dve.tensor_tensor(t1, x1, sn, ALU.mult))
                own(dve.tensor_tensor(t2, x2, cs, ALU.mult))
                return dve.tensor_tensor(dst2, t1, t2, ALU.add)

            tk = ropet.rearrange("p (r t n) -> p r t n", r=2, t=NT)
            kx = c3[:, :, CQ + CKV:CQ + CKV + 64]
            own(rope(kr2[:, :, 0, 0:32], kr2[:, :, 0, 32:64], kx[:, :, 0:32], kx[:, :, 32:64], cosT, sinT, tk[:, 0], tk[:, 1]))
            dve.tensor_copy(kr2[:, :, 1, :], kr2[:, :, 0, :]).then_inc(S("kr_turned"), 1)
            b = wait_group(dve, "krT", 0)
            free_group(dve.tensor_copy(krT, b[:, :]), "krT", 0)
            rt = ya.rearrange("p (r h n) -> p r h n", r=4, h=8)
            for t in range(NT):
                b = wait_group(dve, "qr", t)
                bx = b[:, :].rearrange("p (h n) -> p h n", h=8)
                dst = qrr[:, t, :].rearrange("p (h n) -> p h n", h=8)
                cs = cosT[:, t:t + 1, :].to_broadcast([P, 8, 32])
                sn = sinT[:, t:t + 1, :].to_broadcast([P, 8, 32])
                if t:
                    wait_freed(dve, "qr", t - 1)
                ins = rope(dst[:, :, 0:32], dst[:, :, 32:64], bx[:, :, 0:32], bx[:, :, 32:64], cs, sn, rt[:, 0], rt[:, 1])
                free_group(ins, "qr", t)
            for t in range(NT):
                b = wait_group(dve, "qrT", t)
                free_group(dve.tensor_copy(qrT[:, :, t * P:(t + 1) * P], b[:, :].rearrange("p (c n) -> p c n", c=4)), "qrT", t)
            dve.wait_ge(S("chunk_loaded"), 16)

            def abiased(u):
                q, h = aunits[u]
                nk = (q + 1) * P
                dve.wait_ge(S("scores_ready"), A0 + u + 1)
                if u >= 2:
                    dve.wait_ge(S("probs_transposed"), A0 + u - 1)
                dve.tensor_tensor_reduce(SP3[:, u % 2, 0:nk], SA[u % 2][:, 0:nk], chunk[:, T - nk:T], -ASCALE, 3e38,
                                         ALU.add, ALU.min, nmax2[:, u % 2:u % 2 + 1]).then_inc(S("score_biased"), 1)

            def acopied(u):
                q, h = aunits[u]
                nk = (q + 1) * P
                dve.wait_ge(S("probs_transposed"), A0 + u + 1)
                if u >= 2:
                    dve.wait_ge(S("values_summed"), A0 + u - 1)
                dve.tensor_copy(PT3[:, u % 2, 0:nk], PB[u % 2][:, 0:nk]).then_inc(S("pt_copied"), 1)

            def aout(u):
                q, h = aunits[u]
                j = (q % 2) * 8 + h
                dve.wait_ge(S("values_summed"), A0 + u + 1)
                own(dve.reciprocal(rinv[:, j:j + 1], rsum2[:, j:j + 1]))
                if h == 0 and q:
                    wait_group(dve, "yaT", 2 * q - 1)
                dve.tensor_scalar(ya[:, h * P:(h + 1) * P], OB[:, 0:P], rinv[:, j:j + 1], None, ALU.mult).then_inc(S("a_out"), 1)

            for t in range(len(aunits) + 4):
                if 0 <= t - 3 < len(aunits):
                    aout(t - 3)
                if t < len(aunits):
                    abiased(t)
                if 0 <= t - 1 < len(aunits):
                    acopied(t - 1)
                if t >= 11 and (t - 11) % 8 == 0:
                    q = (t - 11) // 8
                    for i in range(2):
                        b = wait_group(dve, "yaT", 2 * q + i)
                        dve.wait_ge(S("yaT_high"), 2 * q + i + 1)
                        free_group(dve.tensor_tensor(Ylv[:, 4 * i:4 * i + 4, q * P:(q + 1) * P], b[:, :].rearrange("p (f n) -> p f n", f=4),
                                                     Yhv[:, 4 * i:4 * i + 4, q * P:(q + 1) * P].bitcast(F32), ALU.subtract), "yaT", 2 * q + i)
            def merged_low(f):
                dve.wait_ge(S("merged_high"), f + 1)
                dve.tensor_tensor(Hlv[:, f, :], merged[:, f, :], Hhv[:, f, :].bitcast(F32), ALU.subtract).then_inc(S("merged_low"), 1)

            for i in range(8):
                if i == 6:
                    wait_group(dve, "ga", 7)
                    for f in range(6):
                        merged_low(f)
                b = wait_group(dve, "ba", i)
                wait_freed(dve, "ga", i)
                free_group(dve.scalar_tensor_tensor(tba[:, i % 2, :], tga[:, i % 2, :], 1.0, b[:, :], ALU.add, ALU.mult), "ba", i)
                wait_freed(dve, "ba", i)
                dve.tensor_tensor(merged[:, i, :], merged[:, i, :], tba[:, i % 2, :], ALU.add).then_inc(S("merged_done"), 1)
            for f in (6, 7):
                merged_low(f)
            wait_freed(dve, "g1r", 1)
            dve.wait_ge(S("x_back"), 16)
            for j in range(4):
                for tp in range(2):
                    i = 2 * j + tp
                    b = wait_group(dve, "wout", i)
                    w = wtmp[:, i % 2, :].rearrange("p (t n) -> p t n", t=2)
                    own(dve.tensor_tensor(w, b[:, :].rearrange("p (t n) -> p t n", t=2),
                                          g1row[:, j * PC:(j + 1) * PC].unsqueeze(1).to_broadcast([P, 2, PC]), ALU.mult))
                    xs = Xv[:, 2 * tp:2 * tp + 2, j * PC:(j + 1) * PC]
                    free_group(dve.tensor_tensor(xs, xs, w, ALU.add), "wout", i)

            square_last(hraw3, ss2, "wout", 7)
            norm_rows(3, hraw3, rstd2)
            dve.wait_ge(S("tab3_loaded"), 16)
            ftmp3 = xgT.rearrange("p u k n -> p u (k n)")
            for f in range(KT):
                b = wait_group(dve, "h3", f)
                dve.wait_ge(S("h3_high"), f + 1)
                own(dve.tensor_scalar(ftmp3[:, f % 2, :], b[:, :], aff2[:, f:f + 1], modv[:, 3, f:f + 1], ALU.mult, ALU.add))
                free_group(dve.tensor_tensor(Hlv[:, f, :], ftmp3[:, f % 2, :], Hhv[:, f, :].bitcast(F32), ALU.subtract), "h3", f)

            def bc(a, n):
                return a.unsqueeze(2).to_broadcast([P, NT, n])

            dec = cols(tab3, TAB3, "dec")

            def first_of(dst, key, x, n):
                own(dve.tensor_scalar(key, x, 0.0, None, ALU.is_ge))
                own(dve.tensor_tensor(key, key, dec[:, 32 - n:32].unsqueeze(1).to_broadcast([P, NT, n]), ALU.mult))
                own(dve.tensor_reduce(km.unsqueeze(2), key, AX.X, ALU.max))
                own(dve.tensor_tensor(dst, key, bc(km, n), ALU.is_equal))

            wait_freed(dve, "h3", KT - 1)
            b = wait_group(dve, "gr", 0)
            free_group(dve.tensor_copy(gr_rows, b[0:36, :]), "gr", 0)
            b = wait_group(dve, "grT", 0)
            free_group(dve.tensor_tensor(Lg, b[:, 0:144].rearrange("p (t n) -> p t n", t=NT),
                                         cols(par, PAR2, "b_gr").unsqueeze(1).to_broadcast([P, NT, 36]), ALU.add), "grT", 0)
            wait_freed(dve, "grT", 0)
            own(dve.tensor_reduce(gmx.unsqueeze(2), Lg[:, :, 0:4], AX.X, ALU.max))
            dve.tensor_tensor(gsh, Lg[:, :, 0:4], bc(gmx, 4), ALU.subtract).then_inc(S("group_shifted"), 1)
            dve.wait_ge(S("group_shifted"), 1)
            first_of(oh_g, okey, gsh, 4)
            own(dve.tensor_tensor(ing4.rearrange("p (t e g) -> p t e g", t=NT, e=EG), Lg[:, :, 4:36].rearrange("p t (g e) -> p t e g", g=NEG_),
                                  oh_g.unsqueeze(2).to_broadcast([P, NT, EG, NEG_]), ALU.mult))
            own(dve.tensor_reduce(insh.rearrange("p t e -> p (t e)").unsqueeze(2), ing4.rearrange("p (a g) -> p a g", g=NEG_), AX.X, ALU.add))
            own(dve.tensor_reduce(m1.unsqueeze(2), insh, AX.X, ALU.max))
            own(dve.tensor_tensor(insh, insh, bc(m1, EG), ALU.subtract))
            first_of(oh1, key8, insh, EG)
            own(dve.scalar_tensor_tensor(d2, oh1, NEG, insh, ALU.mult, ALU.add))
            dve.tensor_reduce(m2.unsqueeze(2), d2, AX.X, ALU.max).then_inc(S("second_ready"), 1)
            dve.wait_ge(S("second_ready"), 1)
            own(dve.tensor_tensor(d2, d2, bc(m2, EG), ALU.subtract))
            first_of(oh2, key8, d2, EG)
            for A, oh in ((A1, oh1), (A2, oh2)):
                own(dve.tensor_tensor(A.rearrange("p t (g e) -> p t g e", g=NEG_), bc4(oh_g), oh.unsqueeze(2).to_broadcast([P, NT, NEG_, EG]), ALU.mult))
            own(dve.tensor_tensor(triex[0:32, :], cols(con, CON, "tri")[0:32, 0:32], ident[0:32, 0:32], ALU.subtract))
            dve.tensor_tensor(Aa, A1, A2, ALU.add).then_inc(S("assigned"), 1)
            dve.wait_ge(S("assigned"), 1)
            dve.wait_ge(S("group_exp"), 1)
            own(dve.tensor_reduce(gsum.unsqueeze(2), gex, AX.X, ALU.add))
            own(dve.reciprocal(pg, gsum))
            dve.wait_ge(S("second_exp"), 1)
            own(dve.tensor_scalar(gsum, e2, 1.0, None, ALU.add))
            own(dve.reciprocal(gsum, gsum))
            own(dve.tensor_tensor(w1c, pg, gsum, ALU.mult))
            own(dve.tensor_tensor(w2c, w1c, e2, ALU.mult))
            b = wait_group(dve, "cnt", 0)
            free_group(dve.tensor_copy(cntc[0:32, :], b[0:32, 0:1]), "cnt", 0)
            wait_freed(dve, "cnt", 0)
            own(dve.tensor_scalar(nb8[0:32, :], cols(tab3, TAB3, "thr")[0:32, :], cntc[0:32, :], None, ALU.is_le))
            dve.tensor_reduce(nbc[0:32, :], nb8[0:32, :], AX.X, ALU.add).then_inc(S("nb_ready"), 1)
            b = wait_group(dve, "rank", 0)
            free_group(dve.tensor_tensor(Sl, b[:, 0:128].rearrange("p (t n) -> p t n", t=NT), Aa, ALU.subtract), "rank", 0)
            b = wait_group(dve, "pstart", 0)
            own(dve.tensor_scalar(ps64, b[:, 0:32], float(BS), None, ALU.mult))
            own(dve.tensor_copy(nblkf, b[:, 33:34]))
            free_group(dve.tensor_copy(pend[0:32, :], b[0:32, 32:33]), "pstart", 0)
            wait_freed(dve, "pstart", 0)
            dve.tensor_scalar(cmpe[0:32, :], cols(tab3, TAB3, "iota")[0:32, :], pend[0:32, :], None, ALU.is_ge).then_inc(S("ended_ready"), 1)
            b = wait_group(dve, "bexp", 0)
            free_group(dve.tensor_scalar(bexpf, b[:, 0:NBLK], float(NE - 1), None, ALU.min), "bexp", 0)
            wait_freed(dve, "bexp", 0)
            own(dve.tensor_copy(nblk_i, nblkf))
            dve.tensor_copy(bexp_i[:, :], bexpf).then_inc(S("bexp_ready"), 1)
            own(dve.tensor_tensor(Sl, Sl, ps64.unsqueeze(1).to_broadcast([P, NT, 32]), ALU.add))
            for A, k in ((A1, 0), (A2, 1)):
                own(dve.tensor_tensor(Tmp, A, Sl, ALU.mult))
                own(dve.tensor_reduce(slots[:, 4 * k:4 * k + 4].unsqueeze(2), Tmp, AX.X, ALU.add))
            own(dve.tensor_copy(dst_i[:, :], slots))
            own(dve.tensor_scalar(dst_ri[:, :], dst_i[:, :], BS - 1, None, ALU.bitwise_and))
            own(dve.tensor_copy(dst_r, dst_ri[:, :]))
            own(dve.tensor_tensor(dst_b, slots, dst_r, ALU.subtract))
            iota_b = cols(tab3, TAB3, "iota_b").unsqueeze(1).to_broadcast([P, 8, NBLK + 2])
            own(dve.tensor_tensor(block_tok, iota_b, dst_b.unsqueeze(2).to_broadcast([P, 8, NBLK + 2]), ALU.is_equal))
            own(dve.tensor_tensor(block_tok, block_tok, cols(tab3, TAB3, "tok").unsqueeze(2).to_broadcast([P, 8, NBLK + 2]), ALU.mult))
            dve.tensor_tensor(place, cols(tab3, TAB3, "iota_r").unsqueeze(1).to_broadcast([P, 8, BS]),
                              dst_r.unsqueeze(2).to_broadcast([P, 8, BS]), ALU.is_equal).then_inc(S("places_ready"), 1)
            b = wait_group(dve, "slots", 0)
            dve.tensor_copy(slot_i[0:BS, :], b[0:BS, 0:NBLK + 2]).then_inc(S("slot_idx_ready"), 1)

            a2b = aff2.unsqueeze(2).to_broadcast([P, KT, BS])
            s2b = modv[:, 3, :].unsqueeze(2).to_broadcast([P, KT, BS])

            def scale_shift(b, u):
                dve.wait_ge(S("xt_ready"), b + 5)
                dve.tensor_tensor(xgT[:, u, :, :], XT[u][:, :].rearrange("p (k n) -> p k n", k=KT), a2b, ALU.mult).then_inc(S("xt_scaled"), 1)
                dve.wait_ge(S("xt_scaled"), b + 1)
                dve.tensor_tensor(xgT[:, u, :, :], xgT[:, u, :, :], s2b, ALU.add).then_inc(S("xgT_ready"), 1)

            blocks = dve.value_load(nblk_i[0:1, :], min_val=0, max_val=NBLK)
            scale_shift(0, 0)
            with dve.Fori(0, NBLK // WS) as i:
                for v in range(WS):
                    b, u = WS * i + v, v % 2
                    with dve.If(b < blocks):
                        dve.wait_ge(S("down_high"), b + 1)
                        dve.tensor_tensor(wdl[:, u, 1024:2048], wdn[v][:, 1024:2048], wdh[:, u, 1024:2048].bitcast(F32), ALU.subtract).then_inc(S("down_low_v"), 1)
                        dve.wait_ge(S("tanh_ready"), b + 1)
                        dve.wait_ge(S("y_ready"), b + 3)
                        dve.scalar_tensor_tensor(acth[:, u, :], tanhg[:, u, :], 1.0, GB[u][:, 0:128], ALU.add, ALU.mult).then_inc(S("tanh_free"), 1)
                        dve.wait_ge(S("tanh_free"), b + 5)
                        dve.wait_ge(S("up_ready"), b + 5)
                        dve.tensor_tensor(ahh[:, u, :], acth[:, u, :], UB[u][:, 0:128], ALU.mult).then_inc(S("act_high"), 1)
                        dve.tensor_tensor(acth[:, u, :], acth[:, u, :], UB[u][:, 0:128], ALU.mult).then_inc(S("act_whole"), 1)
                        dve.wait_ge(S("act_whole"), b + 1)
                        dve.wait_ge(S("act_high"), b + 1)
                        dve.tensor_tensor(ahl[:, u, :], acth[:, u, :], ahh[:, u, :].bitcast(F32), ALU.subtract).then_inc(S("act_low"), 1)
                        scale_shift(b + 1, 1 - u)
                        dve.wait_ge(S("y_ready"), b + 5)
                        dve.wait_ge(S(f"y_stored{u}"), 32 * i + 16 * (v // 2) + 16)
                        dve.tensor_tensor(yb[0:BS, u, 0:512], YB[0][0:BS, :], g2row[0:BS, 0:512], ALU.mult)
                        dve.tensor_tensor(yb[0:BS, u, 512:1024], YB[1][0:BS, :], g2row[0:BS, 512:1024], ALU.mult).then_inc(S("y_copied"), 1)
            def final(t):
                dve.wait_ge(S("rstd_f"), t + 1)
                dve.scalar_tensor_tensor(Xv[:, t, :], Xv[:, t, :], rsf[:, t:t + 1], cols(tab3, TAB3, "final_g"), ALU.mult, ALU.mult).then_inc(S("out_ready"), 1)

            for t in range(NT):
                dve.wait_ge(S(f"picked{t}"), 32)
                own(dve.scalar_tensor_tensor(Xv[:, t, :], r12[:, t, 0, :], w1c[:, t:t + 1], Xv[:, t, :], ALU.mult, ALU.add))
                dve.scalar_tensor_tensor(Xv[:, t, :], r12[:, t, 1, :], w2c[:, t:t + 1], Xv[:, t, :], ALU.mult, ALU.add).then_inc(S("x_final"), 1)
                if t:
                    final(t - 1)
            final(NT - 1)

        @block.tensor
        def _(pe):
            done = [0]

            def group(what, i):
                n = GIDX[what, i]
                assert n == done[0], (what, i, n, done[0])
                done[0] += 1
                if n >= GRING:
                    e, k = freed_count(n - GRING)
                    pe.wait_ge(S("bank_freed_" + e), k)
                return G[n % GRING]

            def filled(ins):
                ins.then_inc(S("group_filled"), 1)

            def weights(p):
                s = SPL[p]
                pe.wait_ge(S("low_split"), s + 1)
                return wh[:, split_slot(s)], wl[:, split_slot(s)]

            def split3(out, lhs, rhs, first, last):
                (ah, al), (bh, bl) = lhs, rhs
                pe.matmul(out, ah, bh, start=first, stop=False)
                pe.matmul(out, ah, bl, start=False, stop=False)
                return pe.matmul(out, al, bh, start=False, stop=last)

            def rows(what, p, act=None, kts=range(KT), names=None, ready=None):
                h, l = act or (Hhv, Hlv)
                a, b = (w.rearrange("p (k n) -> p k n", n=PC) for w in weights(p))
                for tp in range(2):
                    bank = group(what, names[tp] if names else tp)
                    for j in range(2):
                        t = 2 * tp + j
                        for k in kts:
                            if ready is not None and tp == j == 0:
                                pe.wait_ge(S("ffn_sq"), ready + k + 1)
                            ins = split3(bank[:, j * PC:(j + 1) * PC], (h[:, k, t * P:(t + 1) * P], l[:, k, t * P:(t + 1) * P]),
                                         (a[:, k, :], b[:, k, :]), k == kts[0], k == kts[-1])
                    filled(ins)

            def transposes(what, i, srcs, width=P, parts=P):
                bank = group(what, i)
                for j, s in enumerate(srcs):
                    ins = pe.transpose(bank[:, j * width:(j + 1) * width] if parts == P else bank[:, j * parts:(j + 1) * parts], s, ident[0:parts, 0:parts])
                filled(ins)

            pe.wait_ge(S("con_loaded"), 16)
            pe.wait_ge(S("rows_normed"), NT)
            for f in range(KT):
                transposes("h0", f, [hraw[:, t, f * P:(f + 1) * P] for t in range(NT)])
            pe.wait_ge(S("sml_done"), 1)

            def narrow(what, lo, n, source):
                bank = group(what, 0)
                a, b = (w[:, lo:lo + KT * n].rearrange("p (k n) -> p k n", k=KT) for w in (smh, sml))
                for k in range(KT):
                    wait_freed(pe, source, k)
                    ins = split3(bank[0:n, :], (a[:, k, :], b[:, k, :]), (Hhv[:, k, :], Hlv[:, k, :]), k == 0, k == KT - 1)
                filled(ins)

            def narrow_turned(what, src, n):
                wait_freed(pe, what, 0)
                bank = group(what + "T", 0)
                for t in range(NT):
                    ins = pe.transpose(bank[:, t * n:(t + 1) * n], src[:, t * P:(t + 1) * P], ident[0:n, 0:n])
                filled(ins)

            narrow("gl", 0, 24, "h0")
            for n in ("kcvc", "ksvs", "kwvw"):
                rows(n, (n,))
                if n == "kcvc":
                    narrow_turned("gl", gl_rows, 24)
            pe.wait_ge(S("cdup_ready"), 1)
            for c4 in range(4):
                transposes("cT", c4, [cdup[:, t, c4].rearrange("p u d -> p (u d)") for t in range(NT)])
            for j in range(2):
                rows(("q", j), ("q", j))
            pe.wait_ge(S("kdup_ready"), 1)
            for c4 in range(4):
                transposes("kT", c4, [kdup[:, t, c4].rearrange("p u d -> p (u d)") for t in range(NT)])
            pe.wait_ge(S("blk_low"), 1)
            for i in range(4):
                a, b = (w.rearrange("p (k n) -> p k n", n=PC) for w in weights(("cmp", i // 2, i % 2)))
                bank = group("cmp1", i)
                for k in range(KT):
                    kk = KT * (i % 2) + k
                    ins = split3(bank[0:62, 0:PC], (blkh[:, i // 2, kk, :], blkl[:, i // 2, kk, :]), (a[:, k, :], b[:, k, :]), k == 0, k == KT - 1)
                filled(ins)
            for c in range(2):
                wait_freed(pe, "cmp1", 2 * c + 1)
                bank = group("cmpT", c)
                for f in range(2):
                    ins = pe.transpose(bank[:, f * 62:(f + 1) * 62], cpre[:, c * 256 + f * P:c * 256 + (f + 1) * P], ident[0:62, 0:62])
                filled(ins)
            pe.wait_ge(S("gelu_done"), 1)
            w2 = cols(par, PAR, "w_cmp2").rearrange("p (c f d) -> p c f d", c=2, f=2)
            bank = group("cmpk", 0)
            for g in range(2):
                for f in range(2):
                    ins = pe.matmul(bank[0:31, g * HD:(g + 1) * HD], cw[:, f * 62 + g * 31:f * 62 + (g + 1) * 31], w2[:, 0, f, :],
                                    start=f == 0, stop=f == 1)
            filled(ins)
            bank = group("cmpv", 0)
            for r in range(4):
                for g in range(2):
                    for f in range(2):
                        ins = pe.matmul(bank[32 * r:32 * r + 31, g * 256 + r * HD:g * 256 + (r + 1) * HD],
                                        cw[:, (2 + f) * 62 + g * 31:(2 + f) * 62 + (g + 1) * 31], w2[:, 1, f, :],
                                        start=f == 0, stop=f == 1)
            filled(ins)
            kcd = cw[0:32, 1536:1792].rearrange("p (g u d) -> p g u d", g=2, u=2)
            kcT = cw[:, 1792:1856].rearrange("p (g i) -> p g i", g=2)
            VBD = PTs[:, 0, :].rearrange("p (g n) -> p g n", g=2)
            pe.wait_ge(S("kcd_ready"), 1)
            transposes("cmpkT", 0, [kcd[:, g].rearrange("p u d -> p (u d)") for g in range(2)], parts=32)
            pe.wait_ge(S("q_normed"), 1)
            for c4 in range(4):
                transposes("qT", c4, [Zq[:, t, c4 * P:(c4 + 1) * P] for t in range(NT)])
            wait_freed(pe, "qT", 3)
            for o in range(2):
                bank = group("cS", o)
                r = slice(64 * o, 64 * o + 64)
                for q in range(NT):
                    for j in range(4):
                        ins = pe.matmul(bank[:, (4 * q + j) * 32:(4 * q + j + 1) * 32], qT[r, j, q * P:(q + 1) * P], kcT[r, (2 * j + o) // 4, :], start=True, stop=True)
                filled(ins)
            pe.wait_ge(S("cmp_p"), 1)
            for i in range(2):
                transposes("cP", i, [cpv[:, (4 * i + g) * P:(4 * i + g + 1) * P] for g in range(4)])
            for q in range(NT):
                wait_freed(pe, "cP", q // 2)
                bank = group("cO", q)
                for g in range(2):
                    ins = pe.matmul(bank[:, g * 256:(g + 1) * 256], SP[:, q // 2, (q % 2) * 256 + g * P:(q % 2) * 256 + (g + 1) * P], VBD[:, g, :], start=True, stop=True)
                filled(ins)
            wait_freed(pe, "cO", NT - 1)

            def scores(u):
                ty, q, h = units[u]
                nk = (q + 1) * P
                r = slice(64 * (h % 2), 64 * (h % 2) + 64)
                if u >= 2:
                    pe.wait_ge(S("score_biased"), u - 1)
                pe.matmul(SA[u % 2][:, 0:nk], qT[r, h // 2, q * P:(q + 1) * P], kT[r, 2 * ty + h // 4, 0:nk], start=True, stop=True)\
                  .then_inc(S("scores_ready"), 1)

            def turned(u):
                ty, q, h = units[u]
                pe.wait_ge(S("probs_ready"), u + 1)
                if u >= 2:
                    pe.wait_ge(S("pt_copied"), u - 1)
                for k in range(q + 1):
                    ins = pe.transpose(PB[u % 2][:, k * P:(k + 1) * P], SP[:, u % 2, k * P:(k + 1) * P], ident)
                ins.then_inc(S("probs_transposed"), 1)

            def values(u):
                ty, q, h = units[u]
                v = u // 8
                pe.wait_ge(S("pt_copied"), u + 1)
                if u % 8 == 0 and v:
                    pe.wait_ge(S("out_freed"), v)
                for k in range(q + 1):
                    ins = pe.matmul(OB[:, h * HD:(h + 1) * HD], PTs[:, u % 2, k * P:(k + 1) * P],
                                    Zv[:, k, ty, (h // 4) * HD:(h // 4 + 1) * HD], start=k == 0, stop=k == q)
                ins.then_inc(S("values_summed"), 1)

            bank = None

            def conv_quarter(t):
                nonlocal bank
                g, part = divmod(t, 4)
                i, k6 = divmod(g, 6)
                name = ("hc", "cg", "bg")[k6 // 2]
                f = k6 % 2
                a, b = (w.rearrange("p (k n) -> p k n", n=PC) for w in weights((name, i)))
                if part == 0:
                    bank = group(name, 2 * i + f)
                for k in range(2 * part, 2 * part + 2):
                    ins = split3(bank[:, :], (a[:, k, f * P:(f + 1) * P], b[:, k, f * P:(f + 1) * P]), (Hhv[:, k, :], Hlv[:, k, :]),
                                 k == 0, k == KT - 1)
                if part == 3:
                    filled(ins)

            for t in range(len(units) + 3):
                if t < len(units):
                    scores(t)
                if t < 48:
                    conv_quarter(t)
                if 0 <= t - 1 < len(units):
                    turned(t - 1)
                if 0 <= t - 2 < len(units):
                    values(t - 2)
            bank = group("csq", 0)
            pe.wait_ge(S("conv_sq"), 4)
            for t in range(NT):
                for f in range(4):
                    ins = pe.matmul(bank[:, t:t + 1], SPsq(f)[:, t * P:(t + 1) * P], one, start=f == 0, stop=f == 3)
            filled(ins)
            pe.wait_ge(S("attn_normed"), NT)
            for f in range(4):
                transposes("aT", f, [kT[:, t, f * P:(f + 1) * P] for t in range(NT)])
            wait_freed(pe, "aT", 3)
            pe.wait_ge(S("conv_low"), 4)
            for n in range(4):
                a, b = (w.rearrange("p (k n) -> p k n", n=PC) for w in weights(("wo", n)))
                for tp in range(2):
                    for part in range(2):
                        bank = group("wo", 4 * n + 2 * tp + part)
                        for j in range(2):
                            t = 2 * tp + j
                            for k in range(4 * part, 4 * part + 4):
                                ins = split3(bank[:, j * PC:(j + 1) * PC], (Yhv[:, k, t * P:(t + 1) * P], Ylv[:, k, t * P:(t + 1) * P]),
                                             (a[:, k, :], b[:, k, :]), k % 4 == 0, k % 4 == 3)
                        filled(ins)
            pe.wait_ge(S("rows_normed"), 2 * NT)
            for f in range(KT):
                transposes("h1", f, [hraw[:, t, f * P:(f + 1) * P] for t in range(NT)])

            def mod_piece(m):
                bank = group("mod", m)
                pe.wait_ge(S("mod_summed"), m + 1)
                for f in range(2):
                    ins = pe.matmul(bank[:, f:f + 1], macc[:, m % 2, f * P:(f + 1) * P], one, start=True, stop=True)
                filled(ins)

            m = 0
            for r in range(FQ):
                for j in range(4):
                    a, b = (w.rearrange("p (k n) -> p k n", n=PC) for w in weights(("up", r, j)))
                    for f in range(2):
                        bank = group("up", (r * 4 + j) * 2 + f)
                        for k in range(KT):
                            if r == j == f == 0:
                                wait_freed(pe, "h1", k)
                            ins = split3(bank[:, :], (a[:, k, f * P:(f + 1) * P], b[:, k, f * P:(f + 1) * P]), (Hhv[:, k, :], Hlv[:, k, :]),
                                         k == 0, k == KT - 1)
                        filled(ins)
                    if m < MOD_PIECES:
                        mod_piece(m)
                        m += 1
                for j in range(4):
                    i = (r * 4 + j) * 2
                    rows("down", ("down", r, j), act=(Yhv, Ylv), names=[i, i + 1], ready=8 * r if j == 0 else None)
                    if m < MOD_PIECES:
                        mod_piece(m)
                        m += 1

            pe.wait_ge(S("rows_normed"), 3 * NT)
            for f in range(KT):
                transposes("h2", f, [hraw2[:, t, f * P:(f + 1) * P] for t in range(NT)])
            pe.wait_ge(S("sml_done"), 2)

            def features(what, p, i0, ng=2, act=None, kts=range(KT), ncols=PC):
                h, l = act or (Hhv, Hlv)
                n = len(kts)
                a, b = (w[:, 0:n * ncols].rearrange("p (k n) -> p k n", n=ncols) for w in weights(p))
                for f in range(ng):
                    bank = group(what, i0 + f)
                    for kk, k in enumerate(kts):
                        ins = split3(bank[:, :], (a[:, kk, f * P:(f + 1) * P], b[:, kk, f * P:(f + 1) * P]), (h[:, k, :], l[:, k, :]),
                                     kk == 0, kk == n - 1)
                    filled(ins)

            narrow("if", SMW2["if"][0], 8, "h2")
            for j in range(4):
                features("qk", ("qk", j), 2 * j)
                if j == 0:
                    narrow_turned("if", if_rows, 8)
            for j in range(4):
                rows("om", ("om", j), names=[2 * j, 2 * j + 1])
            pe.wait_ge(S("lf_ready"), 1)
            tri = cols(con, CON, "tri")
            bank = group("cum", 0)
            for t in range(NT):
                for k in range(t + 1):
                    ins = pe.matmul(bank[:, 4 * t:4 * t + 4], tri if k == t else one.to_broadcast([P, P]), lf[:, k, :], start=k == 0, stop=k == t)
            filled(ins)
            pe.wait_ge(S("c_ready"), 1)
            for h in range(MH):
                bank = group("crow", h)
                for t in range(NT):
                    ins = pe.matmul(bank[:, t * P:(t + 1) * P], cc_[:, t, h:h + 1].to_broadcast([P, P]), ident, start=True, stop=True)
                filled(ins)
            for j in range(4):
                rows("vm", ("vm", j), names=[2 * j, 2 * j + 1])
            wait_freed(pe, "vm", 7)
            pe.wait_ge(S("qk_done"), 8)

            def mscores(u):
                h, q = munits[u]
                nk = (q + 1) * P
                pe.wait_ge(S("score_biased"), M0 + u - 1)
                pe.matmul(SA[u % 2][:, 0:nk], qkT[:, h, q * P:(q + 1) * P], qkT[:, MH + h, 0:nk], start=True, stop=True).then_inc(S("scores_ready"), 1)

            def mturned(u):
                h, q = munits[u]
                pe.wait_ge(S("score_biased"), M0 + u + 1)
                pe.wait_ge(S("pt_copied"), M0 + u - 1)
                for k in range(q + 1):
                    ins = pe.transpose(PB[u % 2][:, k * P:(k + 1) * P], SP2[:, u % 2, k * P:(k + 1) * P], ident)
                ins.then_inc(S("probs_transposed"), 1)

            def mvalues(u):
                h, q = munits[u]
                pe.wait_ge(S("pt_copied"), M0 + u + 1)
                if u == 0:
                    pe.wait_ge(S("out_freed"), 8)
                if u:
                    pe.wait_ge(S("m_out"), u)
                for k in range(q + 1):
                    ins = pe.matmul(OB[:, 0:MV], PT2[:, u % 2, k * P:(k + 1) * P], vm[:, k, h * MV:(h + 1) * MV],
                                    start=k == 0, stop=k == q)
                ins.then_inc(S("values_summed"), 1)

            def c3_third(t):
                nonlocal bank
                i, part = divmod(t, 3)
                j, tp = divmod(i, 2)
                a, b = (w.rearrange("p (k n) -> p k n", n=PC) for w in weights(("c3", j)))
                if part == 0:
                    bank = group("c3", i)
                steps = [(jj, k) for jj in range(2) for k in range(KT)]
                for jj, k in steps[(0, 6, 11)[part]:(6, 11, 16)[part]]:
                    tt = 2 * tp + jj
                    ins = split3(bank[:, jj * PC:(jj + 1) * PC], (Hhv[:, k, tt * P:(tt + 1) * P], Hlv[:, k, tt * P:(tt + 1) * P]),
                                 (a[:, k, :], b[:, k, :]), k == 0, k == KT - 1)
                if part == 2:
                    filled(ins)

            for t in range(len(munits) + 3):
                if t < len(munits):
                    mscores(t)
                if t < 18:
                    c3_third(t)
                if 0 <= t - 1 < len(munits):
                    mturned(t - 1)
                if 0 <= t - 2 < len(munits):
                    mvalues(t - 2)
            pe.wait_ge(S("m_out"), len(munits))
            for f in range(KT):
                transposes("yT", f, [To[:, t, f * P:(f + 1) * P] for t in range(NT)])
            wait_freed(pe, "yT", KT - 1)
            for j in range(4):
                features("gm", ("gm", j), 2 * j)
                features("bm", ("bm", j), 2 * j, act=(Yhv, Ylv))
            pe.wait_ge(S("kr_normed"), 1)
            for f in range(5):
                transposes("cT2", f, [c3[:, t, f * P:(f + 1) * P] for t in range(NT)])
            wait_freed(pe, "cT2", 4)
            for j in range(2):
                features("qn", ("qn", j), 4 * j, ng=4, act=(Ch, Cl), kts=range(3), ncols=512)
            pe.wait_ge(S("kr_turned"), 1)
            transposes("krT", 0, [kr2[:, t].rearrange("p u n -> p (u n)") for t in range(NT)])
            a, b = (w[:, 0:1536].rearrange("p (k n) -> p k n", n=512) for w in weights(("qr",)))
            for t in range(NT):
                bank = group("qr", t)
                for k in range(3):
                    ins = split3(bank[:, :], (Ch[:, k, t * P:(t + 1) * P], Cl[:, k, t * P:(t + 1) * P]), (a[:, k, :], b[:, k, :]), k == 0, k == 2)
                filled(ins)
            a, b = (w.rearrange("p (k n) -> p k n", n=1024) for w in weights(("va",)))
            for i in range(8):
                t, half = divmod(i, 2)
                bank = group("va", i)
                for k in range(2):
                    ins = split3(bank[:, :], (Ch[:, 3 + k, t * P:(t + 1) * P], Cl[:, 3 + k, t * P:(t + 1) * P]),
                                 (a[:, k, half * 512:(half + 1) * 512], b[:, k, half * 512:(half + 1) * 512]), k == 0, k == 1)
                filled(ins)
            for t in range(NT):
                wait_freed(pe, "qr", t)
                transposes("qrT", t, [qrr[:, t, c * P:(c + 1) * P] for c in range(4)])
            features("kn", ("kn",), 0, ng=8, act=(Ch, Cl), kts=range(3, 5), ncols=1024)
            wait_freed(pe, "kn", 7)
            wait_freed(pe, "qrT", 3)
            wait_freed(pe, "krT", 0)

            def ascores(u):
                q, h = aunits[u]
                nk = (q + 1) * P
                r = slice(64 * (h % 2), 64 * (h % 2) + 64)
                pe.wait_ge(S("score_biased"), A0 + u - 1)
                pe.matmul(SA[u % 2][:, 0:nk], qn[:, h, q * P:(q + 1) * P], kn[:, h, 0:nk], start=True, stop=False)
                pe.matmul(SA[u % 2][:, 0:nk], qrT[r, h // 2, q * P:(q + 1) * P], krT[r, 0:nk], start=False, stop=True).then_inc(S("scores_ready"), 1)

            def aturned(u):
                q, h = aunits[u]
                pe.wait_ge(S("probs_ready"), M0 + u + 1)
                pe.wait_ge(S("pt_copied"), A0 + u - 1)
                for k in range(q + 1):
                    ins = pe.transpose(PB[u % 2][:, k * P:(k + 1) * P], SP3[:, u % 2, k * P:(k + 1) * P], ident)
                ins.then_inc(S("probs_transposed"), 1)

            def avalues(u):
                q, h = aunits[u]
                pe.wait_ge(S("pt_copied"), A0 + u + 1)
                if u:
                    pe.wait_ge(S("a_out"), u)
                for k in range(q + 1):
                    ins = pe.matmul(OB[:, 0:P], PT3[:, u % 2, k * P:(k + 1) * P], va[:, k, h * P:(h + 1) * P],
                                    start=k == 0, stop=k == q)
                ins.then_inc(S("values_summed"), 1)

            for t in range(len(aunits) + 4):
                if t < len(aunits):
                    ascores(t)
                if 0 <= t - 1 < len(aunits):
                    aturned(t - 1)
                if t >= 11 and (t - 11) % 8 == 0:
                    q = (t - 11) // 8
                    pe.wait_ge(S("a_out"), 8 * q + 8)
                    for i in range(2):
                        transposes("yaT", 2 * q + i, [ya[:, (4 * i + f) * P:(4 * i + f + 1) * P] for f in range(4)])
                if 0 <= t - 2 < len(aunits):
                    avalues(t - 2)
            wait_freed(pe, "yaT", 7)
            for j in range(4):
                features("ga", ("ga", j), 2 * j)
                features("ba", ("ba", j), 2 * j, act=(Yhv, Ylv))
            for i in range(2):
                bank = group("g1r", i)
                for k in range(4):
                    ins = pe.matmul(bank[:, k * P:(k + 1) * P], modv[:, 2, 4 * i + k:4 * i + k + 1].to_broadcast([P, P]), ident, start=True, stop=True)
                filled(ins)
            pe.wait_ge(S("merged_low"), KT)
            for j in range(4):
                rows("wout", ("wout", j), names=[2 * j, 2 * j + 1])

            for i in range(2):
                bank = group("g2r", i)
                for k in range(4):
                    ins = pe.matmul(bank[:, k * P:(k + 1) * P], modv[:, 5, 4 * i + k:4 * i + k + 1].to_broadcast([P, P]), ident, start=True, stop=True)
                filled(ins)
            pe.wait_ge(S("rows_normed"), 4 * NT)
            for f in range(KT):
                transposes("h3", f, [hraw3[:, t, f * P:(f + 1) * P] for t in range(NT)])
            narrow("gr", SMW2["gr"][0], 36, "h3")
            narrow_turned("gr", gr_rows, 36)
            pe.wait_ge(S("assigned"), 1)
            bank = group("cnt", 0)
            for t in range(NT):
                ins = pe.matmul(bank[0:32, 0:1], Aa[:, t, :], one, start=t == 0, stop=t == NT - 1)
            filled(ins)
            bank = group("rank", 0)
            for t in range(NT):
                for k in range(t + 1):
                    ins = pe.matmul(bank[:, 32 * t:32 * t + 32], tri if k == t else one.to_broadcast([P, P]), Aa[:, k, :], start=k == 0, stop=k == t)
            filled(ins)
            pe.wait_ge(S("nb_ready"), 1)
            bank = group("pstart", 0)
            pe.matmul(bank[:, 0:32], nbc[0:32, :].to_broadcast([32, P]), triex[0:32, :], start=True, stop=True)
            pe.matmul(bank[0:32, 32:33], tri[0:32, 0:32], nbc[0:32, :], start=True, stop=True)
            ins = pe.matmul(bank[:, 33:34], one[0:32, :].to_broadcast([32, P]), nbc[0:32, :], start=True, stop=True)
            filled(ins)
            pe.sem_inc(S("up_ready"), 1)
            pe.wait_ge(S("ended_ready"), 1)
            bank = group("bexp", 0)
            filled(pe.matmul(bank[:, 0:NBLK], one[0:32, :].to_broadcast([32, P]), cmpe[0:32, :], start=True, stop=True))
            pe.wait_ge(S("places_ready"), 1)
            bank = group("slots", 0)
            for c in range(8):
                ins = pe.matmul(bank[0:BS, 0:NBLK + 2], place[:, c, :], block_tok[:, c, :], start=c == 0, stop=c == 7)
            filled(ins)
            pe.wait_ge(S("slot_idx_ready"), 1)
            for n in ("xt_ready", "y_ready", "tanh_free", "y_copied", "down_low_p", "down_low_v"):
                pe.sem_inc(S(n), 4)
            for u in range(2):
                pe.sem_inc(S(f"y_stored{u}"), 16)
            def rows_transposed(b, u, v, loaded):
                pe.wait_ge(S(f"xg_loaded{v}"), loaded)
                for k in range(KT):
                    args = XT[u][:, k * BS:(k + 1) * BS], xg[0:BS, v, k * P:(k + 1) * P], ident[0:BS, 0:BS]
                    ins = pe.transpose(*args) if k else pe.matmul(*args, start=True, stop=True)
                ins.then_inc(S("xt_ready"), 1)

            pe.wait_ge(S("bexp_ready"), 1)
            blocks = pe.value_load(nblk_i[0:1, :], min_val=0, max_val=NBLK)
            rows_transposed(0, 0, 0, 16)
            pe.sem_inc(S("up_ready"), 3)
            with pe.Fori(0, NBLK // WS) as i:
                for v in range(WS):
                    b, u = WS * i + v, v % 2
                    with pe.If(b < blocks):
                        wg = wgu[v].rearrange("p (j k n) -> p j k n", j=2, k=KT)
                        wd, wl_ = (w[:, u, :].rearrange("p (k n) -> p k n", k=2) for w in (wdh, wdl))
                        pe.wait_ge(S("xgT_ready"), b + 1)
                        pe.wait_ge(S(f"gu_loaded{v}"), 16 * i + 16)
                        for j, bank, ready in ((0, GB[u], "gate_ready"), (1, UB[u], "up_ready")):
                            for f in range(2):
                                for k in range(KT):
                                    ins = pe.matmul(bank[:, f * BS:(f + 1) * BS], wg[:, j, k, f * P:(f + 1) * P], xgT[:, u, k, :], start=k == 0, stop=k == KT - 1)
                            ins.then_inc(S(ready), 1)
                        rows_transposed(b + 1, 1 - u, (v + 1) % WS, 16 * i + 16 * ((v + 1) // WS) + 16)
                        pe.wait_ge(S("act_high"), b + 1)
                        pe.wait_ge(S("down_high"), b + 1)
                        pe.wait_ge(S("y_copied"), b + 4)
                        for lhs, rhs, last in ((ahh, wd, False), (ahh, wl_, False), (ahl, wd, True)):
                            if rhs is wl_:
                                pe.wait_ge(S("down_low_p"), b + 5)
                                pe.wait_ge(S("down_low_v"), b + 5)
                            if last:
                                pe.wait_ge(S("act_low"), b + 1)
                            for half in range(2):
                                for k in range(2):
                                    ins = pe.matmul(YB[half][0:BS, :], lhs[:, u, k * BS:(k + 1) * BS], rhs[:, k, half * 512:(half + 1) * 512],
                                                    start=k == 0 and lhs is ahh and rhs is wd, stop=k == 1 and last)
                        ins.then_inc(S("y_ready"), 1)


def _kxn(w):
    k, n = w.shape
    return w.reshape(k // P, P, n).transpose(1, 0, 2).reshape(P, -1)


def _col(v):
    return v.reshape(-1, P).T


def _rows(v):
    return np.broadcast_to(v.reshape(1, -1), (P, v.size))


def _padded(a):
    return np.concatenate([a, np.zeros((P, PIECE - a.shape[1]), a.dtype)], 1)


def _piece(inp, p):
    k, c = p[0], PC
    w, w2 = inp["w_in"][0], inp["w_in_2"][0]
    first = {"kcvc": 512, "ksvs": 768, "kwvw": 1024}
    conv = {"hc": 1304, "cg": 1816, "bg": 2328}
    second = {"qk": 0, "vm": 1024, "om": 2048, "gm": 3784, "ga": 4808}
    square = {"wo": "w_o", "mod": "mod_w_2", "bm": "w_branch_m_2", "ba": "w_branch_a_2", "wout": "w_out_2"}
    if k in first:
        return _kxn(w[:, first[k]:first[k] + c])
    if k == "q":
        return _kxn(w[:, p[1] * c:(p[1] + 1) * c])
    if k == "cmp":
        return _kxn(inp["w_cmp1"][0, p[1]][p[2] * D:(p[2] + 1) * D])
    if k in conv:
        o = conv[k] + p[1] * c
        return _kxn(w[:, o:o + c])
    if k == "up":
        o = (p[1] * 4 + p[2]) * c
        return _kxn(inp["w_up"][0][:, o:o + c])
    if k == "down":
        return _kxn(inp["w_down"][0][p[1] * D:(p[1] + 1) * D, p[2] * c:(p[2] + 1) * c])
    if k in square:
        return _kxn(inp[square[k]][0][:, p[1] * c:(p[1] + 1) * c])
    if k in second:
        o = second[k] + p[1] * c
        return _kxn(w2[:, o:o + c])
    if k == "c3":
        latent = np.concatenate([w2[:, 3080:3784], np.zeros((D, 64), w2.dtype)], 1)
        return _kxn(latent[:, p[1] * c:(p[1] + 1) * c])
    uq = inp["w_uq_2"][0].reshape(CQ, AH, 192)
    ukv = inp["w_ukv_2"][0].reshape(CKV, AH, 256)
    if k == "qn":
        return _padded(_kxn(uq[:, p[1] * 4:p[1] * 4 + 4, :P].reshape(CQ, 512)))
    if k == "qr":
        return _padded(_kxn(uq[:, :, P:].reshape(CQ, 512)))
    return _kxn((ukv[:, :, :P] if k == "kn" else ukv[:, :, P:]).reshape(CKV, 1024))


def _parameters(inp):
    twice = lambda v: np.concatenate([v, v])[:, None]
    pe_cmp = inp["pe_cmp"][0].reshape(2, 16, 2, HD)
    par = [_col(inp[n][0]) for n in ("g_mix_norm", "g_ffn_norm", "g_out")]
    par += [twice(inp["g_q"][0])] + [twice(inp["g_k"][0, i]) for i in range(3)]
    par += [_col(inp["b_cmp1"][0].reshape(-1)), pe_cmp.transpose(2, 3, 0, 1).reshape(P, 32),
            inp["conv_w"][0].reshape(3, 4, P).transpose(2, 1, 0).reshape(P, 12),
            inp["w_cmp2"][0].reshape(2, 2, P, HD).transpose(2, 0, 1, 3).reshape(P, 256),
            _rows(inp["b_cmp2"][0]), _col(inp["c_2"][0]), _col(inp["mod_b_2"][0])]
    par2 = [_col(inp["norm1_g_2"][0]), _col(inp["norm2_g_2"][0]),
            inp["conv_w_2"][0].reshape(4, 8, P).transpose(2, 1, 0).reshape(P, 32), _col(inp["conv_b_2"][0]),
            _col(inp["q_norm_g_2"][0]), _col(inp["kv_norm_g_2"][0]),
            _rows(inp["igate_b_2"][0]), _rows(inp["fgate_b_2"][0]), _rows(inp["b_group_2"][0]), _rows(inp["b_router_2"][0])]
    return np.concatenate(par, 1), np.concatenate(par2, 1)


def _constants():
    p, j = np.arange(P)[:, None], np.arange(T)[None]
    con = [np.eye(P), np.triu(np.ones((P, P))), np.ones((P, 1)), np.full((P, 1), -0.5)]
    slope = np.power(np.float32(2.0), np.float32(-8.0) * np.arange(1, NH + 1, dtype=np.float32) / NH).astype(np.float32)
    dist = (p + (T - P) - j).astype(np.float32)
    alibi = np.where(dist[:, None] >= 0, -slope[None, :, None] * dist[:, None], NEG)
    tok = np.arange(T).reshape(NT, P).T
    dist = (tok[:, :, None] - (np.arange(32) * CS + 31)).astype(np.float32)
    seen = (dist >= 0) & (np.arange(32) < CMP_I)
    cmpb = np.where(seen[:, :, None], -slope[None, None, :, None] * dist[:, :, None], NEG)
    inv = (1.0 / (np.float32(10000.0) ** (np.arange(0, 64, 2, dtype=np.float32) / np.float32(64)))).astype(np.float32)
    ang = np.arange(T, dtype=np.float32)[:, None] * inv[None]
    tab2 = [f(ang).reshape(NT, P, 32).transpose(1, 0, 2).reshape(P, -1) for f in (np.cos, np.sin)]
    j = j - (T - P)
    tab2 += [np.where(j <= p, 0, NEG), np.where(j // 64 <= p // 64, 0, NEG)]
    bias = [a.reshape(P, -1) for a in (alibi, cmpb, seen)]
    return [np.concatenate(a, 1).astype(np.float32) for a in (con, bias, tab2)]


_OUTS = [((1, T, D), "float32")]


def kernel(**inputs):
    from concourse import bacc
    from concourse.bass_utils import run_bass_kernel_spmd

    par, par2 = _parameters(inputs)
    con, bias, tab2 = _constants()
    dense, w_in_2 = _kxn(inputs["w_in"][0][:, 1280:1304]), inputs["w_in_2"][0]
    route = np.concatenate([inputs["w_group_2"][0], inputs["w_router_2"][0]], 1)
    tab3 = np.concatenate([_rows(np.arange(32, 0, -1)), _rows(np.arange(NBLK)), _rows(BS * np.arange(8) + 1),
                           np.arange(T).reshape(NT, P).T, np.arange(T).reshape(NT, P).T, _rows(np.arange(BS)),
                           _rows(BS * np.arange(NBLK + 2)), _rows(inputs["final_norm_g_2"])], 1, dtype=np.float32)
    experts = [inputs[n][0].reshape(NE, -1, P, inputs[n].shape[-1]).transpose(0, 2, 1, 3).reshape(NE, P, PIECE)
               for n in ("w_expert_gate_2", "w_expert_up_2", "w_expert_down_2")]
    laid = {
        "x": inputs["x"][0],
        "pieces": np.stack([_piece(inputs, p) for p in all_pieces()]),
        "par": par, "con": con, "smw": dense, "bias": bias, "par2": par2,
        "smw2": np.concatenate([_kxn(w_in_2[:, 3072:3080]), _kxn(route)], 1),
        "tab2": tab2, "tab3": tab3, "wexp": np.concatenate(experts, 2),
    }
    nc = bacc.Bacc("TRN2", target_bir_lowering=False, num_devices=1)
    arrays, args = {}, []
    for name, a in laid.items():
        a = np.ascontiguousarray(a)
        arrays[f"in_{name}_dram"] = a
        args.append(nc.dram_tensor(f"in_{name}_dram", a.shape, mybir.dt.from_np(a.dtype), kind="ExternalInput").ap())
    out = nc.dram_tensor("out_0_dram", (T, D), F32, kind="ExternalOutput").ap()
    build(nc, *args, out)
    r = run_bass_kernel_spmd(nc, [arrays], core_ids=[0])
    return r.results[0]["out_0_dram"].reshape(_OUTS[0][0])
```
